# Optimizing a Trainium2 kernel written in Bass

```python
import jax, jax.numpy as jnp
from jax import lax
import numpy as np

D_MODEL = 1024
BATCH = 1
SEQ = 1024
DEPTH = 1
DEC_BATCH = 8
DEC_SEQ = 8
PAST_LEN = 8192
PAGE_SIZE = 128

CONV_DIM = D_MODEL // 2
CONV_W = 3
GLA_HEADS = 4
GLA_DK = D_MODEL // 2
GLA_DV = D_MODEL
GLA_HEAD_K = GLA_DK // GLA_HEADS
GLA_HEAD_V = GLA_DV // GLA_HEADS
GLA_GATE_RANK = 16
GLA_GATE_TAU = 16.0
GLA_CHUNK = 16
PEER_HEADS = 8
PEER_NKEYS = 128
PEER_EXPERTS = PEER_NKEYS * PEER_NKEYS
PEER_QDIM = 256
PEER_HALF = PEER_QDIM // 2
PEER_TOPK = 16
PEER_BLOCK = 128
N_MOD = 6
EPS = 1e-6
IN_SIZES = (CONV_DIM, CONV_DIM, CONV_DIM, GLA_DK, GLA_DK, GLA_DV, GLA_DV, D_MODEL, D_MODEL, GLA_GATE_RANK)
W_IN_COLS = sum(IN_SIZES)

kernel_name = "hybrid_conv_gla_peer_decoder_step"

def rms_norm(x, w):
    x32 = x.astype(jnp.float32)
    y = x32 * lax.rsqrt(jnp.mean(x32 * x32, axis=-1, keepdims=True) + EPS)
    return (y * w.astype(jnp.float32)).astype(x.dtype)

def short_conv(u, buf, w, bias):
    t = u.shape[1]
    full = jnp.concatenate([buf.astype(u.dtype), u], axis=1)
    y = bias + w[CONV_W - 1] * full[:, CONV_W - 1:CONV_W - 1 + t]
    for i in range(CONV_W - 1):
        y = y + w[i] * full[:, i:i + t]
    return y, full[:, t:].astype(buf.dtype)

def gla_chunked(q, k, v, log_a, s0):
    b, t, h, _ = q.shape
    dv = v.shape[-1]
    n_chunks = -(-t // GLA_CHUNK)
    pad = n_chunks * GLA_CHUNK - t

    def prep(a):
        a = jnp.pad(a.astype(jnp.float32), ((0, 0), (0, pad), (0, 0), (0, 0)))
        return a.reshape(b, n_chunks, GLA_CHUNK, h, a.shape[-1]).transpose(1, 0, 3, 2, 4)

    qc, kc, vc, gc = prep(q), prep(k), prep(v), prep(log_a)
    causal = jnp.tril(jnp.ones((GLA_CHUNK, GLA_CHUNK), dtype=bool))[None, None, :, :, None]

    def step(s, inp):
        qi, ki, vi, gi = inp
        cum = jnp.cumsum(gi, axis=2)
        o_inter = jnp.einsum('bhcd,bhde->bhce', qi * jnp.exp(cum), s)
        rel = cum[:, :, :, None, :] - cum[:, :, None, :, :]
        decay = jnp.exp(jnp.where(causal, rel, -jnp.inf))
        scores = jnp.einsum('bhid,bhjd,bhijd->bhij', qi, ki, decay)
        o = o_inter + jnp.einsum('bhij,bhje->bhie', scores, vi)
        last = cum[:, :, -1:, :]
        s_new = jnp.exp(last[:, :, 0, :])[..., None] * s + jnp.einsum('bhjd,bhje->bhde', ki * jnp.exp(last - cum), vi)
        return s_new, o

    s_fin, o = lax.scan(step, s0.astype(jnp.float32), (qc, kc, vc, gc))
    o = o.transpose(1, 0, 3, 2, 4).reshape(b, n_chunks * GLA_CHUNK, h, dv)[:, :t]
    return o, s_fin

def mixer(h, conv_buf, gla_state, w_in, conv_w, conv_b, w_alpha, b_alpha, gla_norm_w, w_proj_a, w_proj_b, w_out):
    bsz, t, _ = h.shape
    points = [int(p) for p in np.cumsum(IN_SIZES)[:-1]]
    bg, cg, hin, q, k, v, r, ga, gb, alow = jnp.split(h @ w_in, points, axis=-1)
    y_conv, new_buf = short_conv(cg * hin, conv_buf, conv_w, conv_b)
    branch_a = (bg * y_conv) @ w_proj_a
    log_a = jax.nn.log_sigmoid((alow @ w_alpha + b_alpha).astype(jnp.float32)) / GLA_GATE_TAU
    qh = q.reshape(bsz, t, GLA_HEADS, GLA_HEAD_K) * (GLA_HEAD_K ** -0.5)
    kh = k.reshape(bsz, t, GLA_HEADS, GLA_HEAD_K)
    vh = v.reshape(bsz, t, GLA_HEADS, GLA_HEAD_V)
    ah = log_a.reshape(bsz, t, GLA_HEADS, GLA_HEAD_K)
    o, s_new = gla_chunked(qh, kh, vh, ah, gla_state)
    o = rms_norm(o.astype(h.dtype), gla_norm_w.reshape(GLA_HEADS, GLA_HEAD_V))
    o = o.reshape(bsz, t, GLA_DV) * jax.nn.silu(r)
    branch_b = o @ w_proj_b
    merged = jax.nn.sigmoid(ga) * branch_a + jax.nn.sigmoid(gb) * branch_b
    return merged @ w_out, new_buf, s_new.astype(gla_state.dtype)

def peer(h, wq, subkeys, u_tab, v_tab):
    b, t, d = h.shape
    n = b * t
    nb = -(-n // PEER_BLOCK)
    tokens = jnp.pad(h.reshape(n, d), ((0, nb * PEER_BLOCK - n), (0, 0))).reshape(nb, PEER_BLOCK, d)

    def block(xb):
        q = (xb @ wq).reshape(PEER_BLOCK, PEER_HEADS, 2, PEER_HALF)
        s = jnp.einsum('thpd,hpkd->thpk', q, subkeys)
        sv, si = lax.top_k(s, PEER_TOPK)
        cand = (sv[:, :, 0, :, None] + sv[:, :, 1, None, :]).reshape(PEER_BLOCK, PEER_HEADS, PEER_TOPK * PEER_TOPK)
        cand_id = (si[:, :, 0, :, None] * PEER_NKEYS + si[:, :, 1, None, :]).reshape(PEER_BLOCK, PEER_HEADS, PEER_TOPK * PEER_TOPK)
        top_v, top_i = lax.top_k(cand, PEER_TOPK)
        expert = jnp.take_along_axis(cand_id, top_i, axis=-1)
        gate = jax.nn.softmax(top_v.astype(jnp.float32), axis=-1).astype(xb.dtype)
        act = jax.nn.gelu(jnp.einsum('thkd,td->thk', u_tab[expert], xb))
        return jnp.einsum('thk,thkd->td', gate * act, v_tab[expert])

    out = lax.map(block, tokens)
    return out.reshape(nb * PEER_BLOCK, d)[:n].reshape(b, t, d)

def decoder_layer(x, c, conv_buf, gla_state, params):
    (n_mix_pre, n_mix_post, n_ffn_pre, n_ffn_post, w_ada, b_ada, w_in, conv_w, conv_b,
     w_alpha, b_alpha, gla_norm_w, w_proj_a, w_proj_b, w_out, peer_wq, peer_subkeys, peer_u, peer_v) = params
    mod = (jax.nn.silu(c) @ w_ada + b_ada)[:, None, :]
    sh1, sc1, g1, sh2, sc2, g2 = jnp.split(mod, N_MOD, axis=-1)
    h = rms_norm(x, n_mix_pre) * (1.0 + sc1) + sh1
    m, new_buf, new_state = mixer(h, conv_buf, gla_state, w_in, conv_w, conv_b, w_alpha, b_alpha,
                                  gla_norm_w, w_proj_a, w_proj_b, w_out)
    x = x + g1 * rms_norm(m, n_mix_post)
    h = rms_norm(x, n_ffn_pre) * (1.0 + sc2) + sh2
    x = x + g2 * rms_norm(peer(h, peer_wq, peer_subkeys, peer_u, peer_v), n_ffn_post)
    return x, new_buf, new_state

def setup_inputs(seed: int = 0) -> dict:
    key = jax.random.key(seed)
    ks = jax.random.split(key, 26)

    def nrm(k, shape, scale):
        return jax.random.normal(k, shape, jnp.float32) * scale

    def gain(k, width):
        return 1.0 + nrm(k, (DEPTH, width), 0.05)

    return {
        'x_prompt': nrm(ks[0], (BATCH, SEQ, D_MODEL), 1.0),
        'x_sample': nrm(ks[1], (DEC_BATCH, DEC_SEQ, D_MODEL), 1.0),
        'c_prompt': nrm(ks[2], (BATCH, D_MODEL), 1.0),
        'c_sample': nrm(ks[3], (DEC_BATCH, D_MODEL), 1.0),
        'state_conv': nrm(ks[4], (DEPTH, DEC_BATCH, CONV_W - 1, CONV_DIM), 1.0),
        'state_gla': nrm(ks[5], (DEPTH, DEC_BATCH, GLA_HEADS, GLA_HEAD_K, GLA_HEAD_V), 1.0),
        'norm_mix_pre': gain(ks[6], D_MODEL),
        'norm_mix_post': gain(ks[7], D_MODEL),
        'norm_ffn_pre': gain(ks[8], D_MODEL),
        'norm_ffn_post': gain(ks[9], D_MODEL),
        'w_ada': nrm(ks[10], (DEPTH, D_MODEL, N_MOD * D_MODEL), 0.5 * D_MODEL ** -0.5),
        'b_ada': nrm(ks[11], (DEPTH, N_MOD * D_MODEL), 0.02),
        'w_in': nrm(ks[12], (DEPTH, D_MODEL, W_IN_COLS), D_MODEL ** -0.5),
        'conv_w': nrm(ks[13], (DEPTH, CONV_W, CONV_DIM), CONV_W ** -0.5),
        'conv_b': nrm(ks[14], (DEPTH, CONV_DIM), 0.02),
        'w_alpha': nrm(ks[15], (DEPTH, GLA_GATE_RANK, GLA_DK), GLA_GATE_RANK ** -0.5),
        'b_alpha': nrm(ks[16], (DEPTH, GLA_DK), 0.1),
        'gla_norm_w': gain(ks[17], GLA_DV),
        'w_proj_a': nrm(ks[18], (DEPTH, CONV_DIM, D_MODEL), CONV_DIM ** -0.5),
        'w_proj_b': nrm(ks[19], (DEPTH, GLA_DV, D_MODEL), GLA_DV ** -0.5),
        'w_out': nrm(ks[20], (DEPTH, D_MODEL, D_MODEL), D_MODEL ** -0.5),
        'peer_wq': nrm(ks[21], (DEPTH, D_MODEL, PEER_HEADS * PEER_QDIM), D_MODEL ** -0.5),
        'peer_subkeys': nrm(ks[22], (DEPTH, PEER_HEADS, 2, PEER_NKEYS, PEER_HALF), PEER_HALF ** -0.5),
        'peer_u': nrm(ks[23], (DEPTH, PEER_EXPERTS, D_MODEL), D_MODEL ** -0.5),
        'peer_v': nrm(ks[24], (DEPTH, PEER_EXPERTS, D_MODEL), PEER_HEADS ** -0.5),
    }

def reference(x_prompt, x_sample, c_prompt, c_sample, state_conv, state_gla,
              norm_mix_pre, norm_mix_post, norm_ffn_pre, norm_ffn_post, w_ada, b_ada,
              w_in, conv_w, conv_b, w_alpha, b_alpha, gla_norm_w, w_proj_a, w_proj_b, w_out,
              peer_wq, peer_subkeys, peer_u, peer_v):
    yp, ys = x_prompt, x_sample
    conv_p, gla_p, conv_s, gla_s = [], [], [], []
    n_prompt = x_prompt.shape[0]
    for l in range(DEPTH):
        params = (norm_mix_pre[l], norm_mix_post[l], norm_ffn_pre[l], norm_ffn_post[l], w_ada[l], b_ada[l],
                  w_in[l], conv_w[l], conv_b[l], w_alpha[l], b_alpha[l], gla_norm_w[l],
                  w_proj_a[l], w_proj_b[l], w_out[l], peer_wq[l], peer_subkeys[l], peer_u[l], peer_v[l])
        buf0 = jnp.zeros((n_prompt, CONV_W - 1, CONV_DIM), state_conv.dtype)
        s0 = jnp.zeros((n_prompt, GLA_HEADS, GLA_HEAD_K, GLA_HEAD_V), state_gla.dtype)
        yp, bp, sp = decoder_layer(yp, c_prompt, buf0, s0, params)
        ys, bs, ss = decoder_layer(ys, c_sample, state_conv[l], state_gla[l], params)
        conv_p.append(bp)
        gla_p.append(sp)
        conv_s.append(bs)
        gla_s.append(ss)
    return (yp, ys, jnp.stack(conv_p), jnp.stack(gla_p), jnp.stack(conv_s), jnp.stack(gla_s))


_drawn_inputs = setup_inputs


def setup_inputs(seed=0):
    import zlib

    import numpy as np

    out = dict(_drawn_inputs(seed))
    spreads = {}
    factors = {'norm_ffn_post': 3.907, 'conv_b': 2.772}
    for name, (base, spread) in spreads.items():
        noise = np.random.default_rng([zlib.crc32(name.encode()), seed]).standard_normal(out[name].shape)
        drawn = base * np.exp(spread * noise) if base else spread * noise
        out[name] = __import__('jax').numpy.asarray(drawn.astype(out[name].dtype))
    for name, factor in factors.items():
        out[name] = (out[name] * factor).astype(out[name].dtype)
    return out
```

```python
import numpy as np
import concourse.bass as bass
from concourse import mybir
from concourse.alu_op_type import AluOpType as ALU
from contextlib import ExitStack

F32 = mybir.dt.float32
F32R = mybir.dt.float32r
U32 = mybir.dt.uint32
ACT = mybir.ActivationFunctionType
AX = mybir.AxisListType

P = 128
D = 1024
KD = D // P
SEQ = 1024
NSEQ, LSEQ = 8, 8
T = SEQ + NSEQ * LSEQ
NC = 1 + NSEQ
NT = -(-T // P)
TAIL = T - (NT - 1) * P
NST = NT - 1 + NSEQ
TB = [(0, 384), (384, 384), (768, 320)]
CC = D // 2 // P
CW = 3
H, DK, DV = 4, 128, 256
RANK = 16
TAU = 16.0
LV = 7
PH, NK, TOPK = 8, 128, 16
HK = PH * TOPK
GB = 64
NGB = T // GB
CP = 4
NSTEP = NK // CP
PICK_CHUNKS = 3
GATE_CHUNKS = 6
EPS = 1e-6
LOWEST = -3.0e38


class Steps:

    def __init__(self, eng, sem, base=0):
        self.eng, self.sem, self.base, self.n = eng, sem, base, 0

    def __call__(self, ins, passed=None):
        self.n += 1
        ins.then_inc(self.sem, 1)
        self.eng.wait_ge(self.sem, self.base + self.n)
        if passed is not None:
            self.eng.sem_inc(passed, 1)


def rows(t):
    return P if t < NT - 1 else TAIL


def per_sequence(ap):
    return ap[:, :, None].broadcast_to([P, NSEQ, LSEQ])


def chunk_masks():
    sums = np.zeros((2, LV + 2, P, P), np.float32)
    pairs = np.zeros((2, LV + 1, P, P), np.float32)
    j, i = np.arange(P)[:, None], np.arange(P)[None, :]
    for kind, (n, size) in enumerate([(P, P), (TAIL, LSEQ)]):
        ok = (j < n) & (i < n)
        for l in range(LV):
            half = 1 << l
            if 2 * half > size:
                continue
            mid = i // (2 * half) * (2 * half) + half
            sums[kind, l] = ok & (((i >= mid) & (j >= mid) & (j <= i)) | ((i < mid) & (j > i) & (j < mid)))
            pairs[kind, l] = ok & (i // (2 * half) == j // (2 * half)) & (i >= mid) & (j < mid)
        start = i // size * size
        sums[kind, LV] = ok & (j >= start) & (j <= i)
        sums[kind, LV + 1] = ok & (j > i) & (j < start + size)
        pairs[kind, LV] = ok & (i == j)
    return sums.transpose(2, 0, 1, 3).copy(), pairs.transpose(2, 0, 1, 3).copy()


class Scope:

    def __init__(self, nc, name):
        self.nc, self.name, self.tensors, self.engines, self.sems = nc, name, ExitStack(), ExitStack(), []

    def __enter__(self):
        return self

    def __exit__(self, *a):
        self.engines.close()
        if self.sems:
            self.nc.clear_and_free_semaphores(self.sems)
            self.nc.all_engine_barrier()
        self.tensors.close()

    def sb(self, name, shape, dt=F32):
        return self.tensors.enter_context(self.nc.sbuf_tensor(f"{self.name}_{name}", shape, dt))

    def ps(self, name, shape):
        return self.tensors.enter_context(self.nc.psum_tensor(f"{self.name}_{name}", shape, F32))

    def sem(self, name):
        self.sems.append(self.nc.alloc_semaphore(f"{self.name}_{name}"))
        return self.sems[-1]

    def block(self):
        return self.engines.enter_context(self.nc.Block())


def project(nc, banks, weights, rhs, nk):
    for bank, (t0, n) in zip(banks, TB):
        for k in range(nk):
            last = nc.tensor.matmul(bank[:, 0:n], weights[:, k, :], rhs[:, k, t0:t0 + n],
                                    start=(k == 0), stop=(k == nk - 1))
        yield last


def project3(nc, banks, w_hi, w_lo, rhs_hi, rhs_lo, nk):
    for bank, (t0, n) in zip(banks, TB):
        for k in range(nk):
            hi, lo = rhs_hi[:, k, t0:t0 + n], rhs_lo[:, k, t0:t0 + n]
            nc.tensor.matmul(bank[:, 0:n], w_hi[:, k, :], hi, start=(k == 0), stop=False)
            nc.tensor.matmul(bank[:, 0:n], w_hi[:, k, :], lo, start=False, stop=False)
            last = nc.tensor.matmul(bank[:, 0:n], w_lo[:, k, :], hi, start=False, stop=(k == nk - 1))
        yield last


def split(nc, pool, hi, lo, raw, high, low, count):
    nc.gpsimd.tensor_copy(hi, raw).then_inc(high, 1)
    pool.wait_ge(high, count)
    nc.gpsimd.tensor_tensor(lo, raw, hi.bitcast(F32), ALU.subtract).then_inc(low, 1)


def norm_squares(nc, act, s, src, sq):
    for k in range(KD):
        if k >= 2:
            act.wait_ge(s["summed"], k - 1)
        nc.scalar.activation(sq[:, k % 2, :], src[:, k, :], ACT.Square).then_inc(s["squared"], 1)


def norm_sums(nc, pe, s, ones, sq, banks):
    for k in range(KD):
        pe.wait_ge(s["squared"], k + 1)
        for bank, (t0, n) in zip(banks, TB):
            last = nc.tensor.matmul(bank[:, 0:n], ones[:, :], sq[:, k % 2, t0:t0 + n],
                                    start=(k == 0), stop=(k == KD - 1))
        last.then_inc(s["summed"], 1)


def norm_roots(nc, act, s, banks, root, eps):
    act.wait_ge(s["summed"], KD)
    for bank, (t0, n) in zip(banks, TB):
        nc.scalar.activation(root[:, t0:t0 + n], bank[:, 0:n], ACT.Sqrt, bias=eps[:, 0:1],
                             scale=1.0 / D).then_inc(s["rooted"], 1)


def norm_sems(sc, tag=""):
    return {n: sc.sem(tag + n) for n in ("squared", "summed", "rooted")}


def modulate(nc, step, out, src, rstd, tmp, gain, shift):
    for k in range(KD):
        step(nc.vector.tensor_tensor(tmp[:, :], src[:, k, :], rstd[:, :], ALU.mult))
        nc.vector.tensor_scalar(out[:, k, 0:SEQ], tmp[:, 0:SEQ], gain[:, k, 0:1], shift[:, k, 0:1],
                                ALU.mult, ALU.add)
        tail = tmp[:, SEQ:T].rearrange("p (s t) -> p s t", s=NSEQ)
        otail = out[:, k, SEQ:T].rearrange("p (s t) -> p s t", s=NSEQ)
        step(nc.vector.tensor_tensor(tail, tail, per_sequence(gain[:, k, 1:NC]), ALU.mult))
        step(nc.vector.tensor_tensor(otail, tail, per_sequence(shift[:, k, 1:NC]), ALU.add))


def residual(nc, step, x, m, rstd, tmp, gain):
    for k in range(KD):
        step(nc.vector.tensor_tensor(tmp[:, :], m[:, k, :], rstd[:, :], ALU.mult))
        tail = tmp[:, SEQ:T].rearrange("p (s t) -> p s t", s=NSEQ)
        step(nc.vector.tensor_tensor(tail, tail, per_sequence(gain[:, k, 1:NC]), ALU.mult))
        step(nc.vector.scalar_tensor_tensor(out=x[:, k, 0:SEQ], in0=tmp[:, 0:SEQ], scalar=gain[:, k, 0:1],
                                            in1=x[:, k, 0:SEQ], op0=ALU.mult, op1=ALU.add))
        step(nc.vector.tensor_tensor(x[:, k, SEQ:T], x[:, k, SEQ:T], tmp[:, SEQ:T], ALU.add))


def condition_phase(nc, A, G):
    with Scope(nc, "cond") as sc:
        NB = 4
        NL = 6 * KD // NB
        x = sc.sb("x", [P, KD, T])
        w = sc.sb("w", [P, 2, NB, KD, P])
        c = sc.sb("c", [P, KD, NC])
        sc_c = sc.sb("silu_c", [P, KD, NC])
        mod = sc.sb("mod", [P, 6 * KD, NC])
        bias = sc.sb("bias", [P, 6 * KD])
        gains = sc.sb("gains", [P, 4, KD])
        sq = sc.sb("sq", [P, 2, T])
        root = sc.sb("root", [P, T])
        tmp = sc.sb("tmp", [P, T])
        small_in, x_in, w_in = sc.sem("small_in"), sc.sem("x_in"), [sc.sem("w_in0"), sc.sem("w_in1")]
        sig, silu, w_used, mod_out, own, ready = (sc.sem(n) for n in ("sig", "silu", "w_used", "mod_out", "own", "ready"))
        ns = norm_sems(sc)
        PS = G["PS"]
        block = sc.block()

        @block.sync
        def _(sp):
            for dst, src in ((c, A["cond"]), (bias, A["ada_bias"]), (gains, A["gains"])):
                sp.dma_start(dst[:], src).then_inc(small_in, 16)
            for k in range(KD):
                sp.dma_start(x[:, k, :], A["x"][k]).then_inc(x_in, 16)
            for half in range(2):
                sp.dma_start(w[:, half], A["w_ada"][half]).then_inc(w_in[half], 16)
            with sp.Fori(1, NL // 2) as i:
                for half in range(2):
                    sp.wait_ge(w_used, 2 * i - 1 + half)
                    sp.dma_start(w[:, half], A["w_ada"][2 * i + half]).then_inc(w_in[half], 16)

        @block.gpsimd
        def _(pool):
            nc.gpsimd.memset(G["ones"][:, :], 1.0).then_inc(ready, 1)
            nc.gpsimd.memset(G["eps"][:, :], EPS).then_inc(ready, 1)
            nc.gpsimd.memset(G["one"][:, :], 1.0).then_inc(ready, 1)
            nc.gpsimd.memset(G["ident"][:, :], 0.0).then_inc(ready, 1)
            pool.wait_ge(ready, 4)
            nc.gpsimd.affine_select(out=G["ident"][:, :], in_=G["ident"][:, :], compare_op=ALU.not_equal,
                                    fill=1.0, base=0, pattern=[[-1, P]], channel_multiplier=1).then_inc(ready, 1)
            nc.gpsimd.iota(G["iota"][:, :], [[1, P]], base=0, channel_multiplier=0,
                           allow_small_or_imprecise_dtypes=True).then_inc(ready, 1)

        @block.scalar
        def _(act):
            act.wait_ge(small_in, 48)
            nc.scalar.activation(sc_c[:], c[:], ACT.Sigmoid).then_inc(sig, 1)
            act.wait_ge(x_in, 16 * KD)
            norm_squares(nc, act, ns, x, sq)
            act.wait_ge(ready, 6)
            norm_roots(nc, act, ns, [PS[:, b] for b in (2, 3, 4)], root, G["eps"])

        @block.tensor
        def _(pe):
            pe.wait_ge(ready, 6)
            norm_sums(nc, pe, ns, G["ones"], sq, [PS[:, b] for b in (2, 3, 4)])
            pe.wait_ge(silu, 1)
            with pe.Fori(0, NL // 2) as i:
                for half in range(2):
                    pe.wait_ge(w_in[half], 16 * i + 16)
                    pe.wait_ge(mod_out, 2 * i + half + 1)
                    for b in range(NB):
                        for k in range(KD):
                            last = nc.tensor.matmul(PS[:, half, b * NC:(b + 1) * NC], w[:, half, b, k, :],
                                                    sc_c[:, k, :], start=(k == 0), stop=(k == KD - 1))
                    last.then_inc(w_used, 1)

        @block.vector
        def _(dve):
            dve.sem_inc(mod_out, 2)
            step = Steps(dve, own)
            dve.wait_ge(sig, 1)
            nc.vector.tensor_tensor(sc_c[:], sc_c[:], c[:], ALU.mult).then_inc(silu, 1)
            dve.wait_ge(small_in, 48)
            with dve.Fori(0, NL // 2) as i:
                for half in range(2):
                    at = (2 * i + half) * NB
                    dve.wait_ge(w_used, 2 * i + half + 1)
                    nc.vector.tensor_tensor(mod[:, bass.ds(at, NB), :],
                                            PS[:, half, 0:NB * NC].rearrange("p (b c) -> p b c", c=NC),
                                            bias[:, bass.ds(at, NB)][:, :, None].broadcast_to([P, NB, NC]),
                                            ALU.add).then_inc(mod_out, 1)
            dve.wait_ge(mod_out, 2 + NL)
            for n, (shift, scale, gate) in enumerate(((0, 1, 2), (3, 4, 5))):
                seg = lambda q: mod[:, q * KD:(q + 1) * KD, :]
                g = lambda q: gains[:, q, :][:, :, None].broadcast_to([P, KD, NC])
                step(nc.vector.scalar_tensor_tensor(out=G["gain"][:, n], in0=seg(scale), scalar=1.0, in1=g(2 * n),
                                                    op0=ALU.add, op1=ALU.mult))
                step(nc.vector.tensor_tensor(G["gate"][:, n], seg(gate), g(2 * n + 1), ALU.mult))
                step(nc.vector.tensor_copy(G["shift"][:, n], seg(shift)))
            dve.wait_ge(ns["rooted"], 3)
            step(nc.vector.reciprocal(root[:, :], root[:, :]))
            modulate(nc, step, G["h"], x, root, tmp, G["gain"][:, 0], G["shift"][:, 0])


def heads_phase(nc, A, G):
    with Scope(nc, "gla") as sc:
        NW = 6
        h, ob, PS = G["h"], G["ob"], G["PS"]
        w = sc.sb("w", [P, NW, KD, P])
        w_low = sc.sb("w_low", [P, KD, RANK])
        low = sc.sb("low", [RANK + 1, NT * P])
        w_alpha = sc.sb("w_alpha", [RANK + 1, H * DK])
        gnorm = sc.sb("gnorm", [P, 2 * H])
        q, k = sc.sb("q", [P, T]), sc.sb("k", [P, T])
        v = sc.sb("v", [P, NT, DV])
        g = sc.sb("g", [P, NT, DK])
        soft = sc.sb("soft", [P, NT, DK])
        r = sc.sb("r", [P, 2, T])
        sg = sc.sb("sg", [P, 2, 384])
        o = sc.sb("o", [P, 2, T])
        E = sc.sb("E", [P, 2, LV + 2, P])
        Q = sc.sb("Q", [P, LV + 1, P])
        K = sc.sb("K", [P, LV + 1, P])
        sT = sc.sb("sT", [P, P])
        prod = sc.sb("prod", [P, LV + 1, P])
        kT = sc.sb("kT", [P, P])
        kTs = sc.sb("kTs", [TAIL, NSEQ, P])
        seq_rows = sc.sb("seq_rows", [TAIL, NSEQ])
        S = sc.sb("S", [P, DV])
        sums = sc.sb("sums", [P, 2, LV + 2, P])
        pairs = sc.sb("pairs", [P, 2, LV + 1, P])
        Ss = sc.sb("Ss", [P, NSEQ, DV])
        names = ("small_in low_ready q_out k_out z_mm z_min z_abs g_ready v_mm v_out r_mm r_sig r_out "
                 "e_mm e_exp qk s_mm s_red t_mm t_out o_mm o_out st_mm st_out kts st_in st_saved st_free "
                 "lin sq_ready sums rooted normed own act_own").split()
        M = {n: sc.sem(n) for n in names}
        w_in = [sc.sem(f"w_in{b}") for b in range(NW)]
        block = sc.block()
        bank = lambda b: PS[:, b]
        tiles = [(t, rows(t), 0 if t < NT - 1 else 1) for t in range(NT)]

        @block.sync
        def _(sp):
            sp.sem_inc(M["st_free"], 1)
            for dst, src in ((w_low, A["w_low"]), (w_alpha, A["w_alpha"]), (gnorm, A["gla_norm"]),
                             (seq_rows, A["seq_rows"]), (sums, A["mask_sums"]), (pairs, A["mask_pairs"])):
                sp.dma_start(dst[:], src).then_inc(M["small_in"], 16)
            for b in range(NW):
                sp.dma_start(w[:, b], A["w_heads"][0, b]).then_inc(w_in[b], 16)
            sp.dma_start(Ss[:], A["state"][0]).then_inc(M["st_in"], 16)
            with sp.Fori(1, H) as i:
                for b in range(NW):
                    if b < 2:
                        sp.wait_ge(M["lin"], 6 * (i - 1) + 3 * b + 4)
                    elif b < 4:
                        sp.wait_ge(M["v_mm"], NT * i)
                    else:
                        sp.wait_ge(M["r_mm"], 6 * (i - 1) + 3 * (b - 4) + 3)
                    sp.dma_start(w[:, b], A["w_heads"][i, b]).then_inc(w_in[b], 16)
                sp.wait_ge(M["st_out"], i * NST)
                sp.dma_start(A["out_gla_p"][i - 1], S[:]).then_inc(M["st_saved"], 16)
                sp.dma_start(A["out_gla_s"][i - 1], Ss[:]).then_inc(M["st_saved"], 16)
                sp.wait_ge(M["st_saved"], 32 * i)
                sp.sem_inc(M["st_free"], 1)
                sp.dma_start(Ss[:], A["state"][i]).then_inc(M["st_in"], 16)
            sp.wait_ge(M["st_out"], H * NST)
            sp.dma_start(A["out_gla_p"][H - 1], S[:]).then_inc(M["st_saved"], 16)
            sp.dma_start(A["out_gla_s"][H - 1], Ss[:]).then_inc(M["st_saved"], 16)
            sp.wait_ge(M["st_saved"], 32 * H)

        @block.tensor
        def _(pe):
            pe.wait_ge(M["small_in"], 96)
            for b, (t0, n) in enumerate(TB):
                for kk in range(KD):
                    last = nc.tensor.matmul(PS[0:RANK, b, 0:n], w_low[:, kk, :], h[:, kk, t0:t0 + n],
                                            start=(kk == 0), stop=(kk == KD - 1))
            last.then_inc(M["lin"], 1)
            pe.wait_ge(M["low_ready"], 1)
            with pe.Fori(0, H) as i:
                pe.wait_ge(w_in[0], 16 * i + 16)
                pe.wait_ge(M["rooted"], 3 * i + 3)
                for last in project(nc, [bank(0), bank(1), bank(2)], w[:, 0], h, KD):
                    last.then_inc(M["lin"], 1)
                pe.wait_ge(w_in[1], 16 * i + 16)
                pe.wait_ge(M["s_red"], NT * i + 1)
                pe.wait_ge(M["t_out"], NT * i + 1)
                for last in project(nc, [bank(3), bank(4), bank(5)], w[:, 1], h, KD):
                    last.then_inc(M["lin"], 1)
                pe.wait_ge(M["q_out"], 3 * i + 3)
                for t, n, _ in tiles:
                    last = nc.tensor.matmul(PS[:, t // 4, t % 4 * DK:(t % 4 + 1) * DK],
                                            low[:, t * P:(t + 1) * P], w_alpha[:, bass.ds(i * DK, DK)],
                                            start=True, stop=True)
                last.then_inc(M["z_mm"], 1)
                pe.wait_ge(w_in[2], 16 * i + 16)
                pe.wait_ge(w_in[3], 16 * i + 16)
                pe.wait_ge(M["k_out"], 3 * i + 3)
                for t, n, _ in tiles:
                    if t >= 3:
                        pe.wait_ge(M["v_out"], NT * i + t - 2)
                    for half in range(2):
                        for kk in range(KD):
                            last = nc.tensor.matmul(PS[0:n, 3 + t % 3, half * P:(half + 1) * P],
                                                    h[:, kk, t * P:t * P + n], w[:, 2 + half, kk, :],
                                                    start=(kk == 0), stop=(kk == KD - 1))
                    last.then_inc(M["v_mm"], 1)
                for b in range(2):
                    pe.wait_ge(w_in[4 + b], 16 * i + 16)
                    if b == 0:
                        pe.wait_ge(M["z_abs"], 2 * i + 2)
                    else:
                        pe.wait_ge(M["v_out"], NT * i + NT)
                    for last in project(nc, [bank(3 * b), bank(3 * b + 1), bank(3 * b + 2)], w[:, 4 + b], h, KD):
                        last.then_inc(M["r_mm"], 1)
                pe.wait_ge(M["r_out"], 6 * i + 6)
                pe.wait_ge(M["g_ready"], 2 * i + 2)

                def exponents(t, n, kind):
                    if t >= 1:
                        pe.wait_ge(M["e_exp"], NT * i + t)
                    for b in range(3):
                        last = nc.tensor.matmul(PS[:, b, 0:384].rearrange("p (l i) -> p l i", l=3)[:, :, 0:n],
                                                g[0:n, t, :], sums[0:n, kind, 3 * b:3 * b + 3, 0:n],
                                                start=True, stop=True)
                    last.then_inc(M["e_mm"], 1)

                exponents(*tiles[0])
                for t, n, kind in tiles:
                    if t + 1 < NT:
                        exponents(*tiles[t + 1])
                    pe.wait_ge(M["qk"], 2 * (NT * i + t) + 2)
                    if t >= 1:
                        pe.wait_ge(M["s_red"], NT * i + t + 1)
                        pe.wait_ge(M["t_out"], NT * i + t + 1)
                    for l in range(LV + 1):
                        lhs = K[:, l, 0:n] if l < LV else k[:, t * P:t * P + n]
                        rhs = Q[:, l, 0:n] if l < LV else q[:, t * P:t * P + n]
                        last = nc.tensor.matmul(PS[0:n, 3 + l // 4, l % 4 * P:l % 4 * P + n], lhs, rhs,
                                                start=True, stop=True)
                    last.then_inc(M["s_mm"], 1)
                    nc.tensor.transpose(PS[0:n, 5, 0:DK], K[:, LV, 0:n], G["ident"][:, :]).then_inc(M["t_mm"], 1)
                    pe.wait_ge(M["s_red"], NT * i + t + 2)
                    pe.wait_ge(M["o_out"], NT * i + t + 1)
                    if t < NT - 1:
                        if t >= 1:
                            pe.wait_ge(M["st_out"], NST * i + t)
                        for e in range(2):
                            last = nc.tensor.matmul(PS[:, 6, e * P:e * P + n], v[0:n, t, e * P:(e + 1) * P],
                                                    sT[0:n, 0:n], start=True, stop=(t == 0))
                            if t >= 1:
                                last = nc.tensor.matmul(PS[:, 6, e * P:e * P + n], S[:, e * P:(e + 1) * P],
                                                        Q[:, LV, 0:n], start=False, stop=True)
                        last.then_inc(M["o_mm"], 1)
                        pe.wait_ge(M["t_out"], NT * i + t + 2)
                        nc.tensor.matmul(PS[:, 7, 0:DV], kT[0:n, :], v[0:n, t, :],
                                         start=True, stop=True).then_inc(M["st_mm"], 1)
                    else:
                        pe.wait_ge(M["st_in"], 16 * i + 16)
                        for e in range(2):
                            last = nc.tensor.matmul(PS[:, 6, e * P:e * P + n], v[0:n, t, e * P:(e + 1) * P],
                                                    sT[0:n, 0:n], start=True, stop=False)
                            for s in range(NSEQ):
                                last = nc.tensor.matmul(PS[:, 6, e * P + s * LSEQ:e * P + (s + 1) * LSEQ],
                                                        Ss[:, s, e * P:(e + 1) * P],
                                                        Q[:, LV, s * LSEQ:(s + 1) * LSEQ],
                                                        start=False, stop=(s == NSEQ - 1))
                        last.then_inc(M["o_mm"], 1)
                        pe.wait_ge(M["kts"], i + 1)
                        for s in range(NSEQ):
                            pe.wait_ge(M["st_out"], NST * i + NT - 1 + s)
                            nc.tensor.matmul(PS[:, 7, 0:DV], kTs[0:n, s, :], v[0:n, t, :],
                                             start=True, stop=True).then_inc(M["st_mm"], 1)
                pe.wait_ge(M["sq_ready"], i + 1)
                for b, (t0, n) in enumerate(TB):
                    for e, src in enumerate((q, k)):
                        last = nc.tensor.matmul(PS[:, b, 0:n], G["ones"][:, :], src[:, t0:t0 + n],
                                                start=(e == 0), stop=(e == 1))
                last.then_inc(M["sums"], 1)

        @block.scalar
        def _(act):
            act.sem_inc(M["rooted"], 3)
            act.sem_inc(M["t_out"], 1)
            act.sem_inc(M["o_out"], 1)
            with act.Fori(0, H) as i:
                for b, (t0, n) in enumerate(TB):
                    act.wait_ge(M["lin"], 6 * i + 2 + b)
                    nc.scalar.activation(q[:, t0:t0 + n], PS[:, b, 0:n], ACT.Copy,
                                         scale=float(DK) ** -0.5).then_inc(M["q_out"], 1)
                steps = Steps(act, M["act_own"], 4 * i)
                act.wait_ge(M["z_min"], 2 * i + 2)
                full = PS[:, 0:2, :].rearrange("p b (t d) -> p (b t) d", d=DK)
                nc.scalar.activation(soft[:, 0:NT - 1, :], full, ACT.Abs).then_inc(M["z_abs"], 1)
                nc.scalar.activation(soft[0:TAIL, NT - 1, :], PS[0:TAIL, 2, 0:DK], ACT.Abs).then_inc(M["z_abs"], 1)
                act.wait_ge(M["z_abs"], 2 * i + 2)
                for part in (soft[:, 0:NT - 1, :], soft[0:TAIL, NT - 1, :]):
                    steps(nc.scalar.activation(part, part, ACT.Exp, scale=-1.0))
                for n, part in ((P, soft[:, 0:NT - 1, :]), (TAIL, soft[0:TAIL, NT - 1, :])):
                    steps(nc.scalar.activation(part, part, ACT.Ln, bias=G["one"][0:n, 0:1]))
                for t, n, _ in tiles:
                    act.wait_ge(M["v_mm"], NT * i + t + 1)
                    nc.scalar.activation(v[0:n, t, :], PS[0:n, 3 + t % 3, 0:DV], ACT.Copy).then_inc(M["v_out"], 1)
                for b in range(6):
                    act.wait_ge(M["r_mm"], 6 * i + b + 1)
                    if b >= 2:
                        act.wait_ge(M["r_out"], 6 * i + b - 1)
                    n = TB[b % 3][1]
                    nc.scalar.activation(sg[:, b % 2, 0:n], PS[:, b, 0:n], ACT.Sigmoid).then_inc(M["r_sig"], 1)
                for t, n, kind in tiles:
                    act.wait_ge(M["e_mm"], NT * i + t + 1)
                    if t >= 2:
                        act.wait_ge(M["st_out"], NST * i + t - 1)
                    src = PS[:, 0:3, 0:384].rearrange("p b (l i) -> p b l i", l=3)[:, :, :, 0:n]
                    dst = E[:, t % 2].rearrange("p (b l) i -> p b l i", l=3)[:, :, :, 0:n]
                    nc.scalar.activation(dst, src, ACT.Exp).then_inc(M["e_exp"], 1)
                    act.wait_ge(M["t_mm"], NT * i + t + 1)
                    if t >= 1:
                        act.wait_ge(M["st_mm"], NST * i + t)
                    nc.scalar.activation(kT[0:n, :], PS[0:n, 5, 0:DK], ACT.Copy).then_inc(M["t_out"], 1)
                    act.wait_ge(M["o_mm"], NT * i + t + 1)
                    nc.scalar.activation(o[:, :, t * P:t * P + n],
                                         PS[:, 6, 0:2 * P].rearrange("p (e i) -> p e i", e=2)[:, :, 0:n],
                                         ACT.Copy).then_inc(M["o_out"], 1)
                act.wait_ge(M["o_out"], NT * i + NT + 1)
                nc.scalar.activation(q[:, :], o[:, 0, :], ACT.Square)
                nc.scalar.activation(k[:, :], o[:, 1, :], ACT.Square).then_inc(M["sq_ready"], 1)
                act.wait_ge(M["sums"], i + 1)
                for b, (t0, n) in enumerate(TB):
                    nc.scalar.activation(soft[:].rearrange("p t d -> p (t d)")[:, t0:t0 + n], PS[:, b, 0:n],
                                         ACT.Sqrt, bias=G["eps"][:, 0:1], scale=1.0 / DV).then_inc(M["rooted"], 1)

        @block.vector
        def _(dve):
            dve.sem_inc(M["s_red"], 1)
            dve.wait_ge(M["small_in"], 96)
            nc.vector.memset(low[:, :], 1.0).then_inc(M["own"], 1)
            dve.wait_ge(M["own"], 1)
            dve.wait_ge(M["lin"], 1)
            for b, (t0, n) in enumerate(TB):
                last = nc.vector.tensor_copy(low[0:RANK, t0:t0 + n], PS[0:RANK, b, 0:n])
            last.then_inc(M["low_ready"], 1)
            own_per_head = NT + 3
            with dve.Fori(0, H) as i:
                step = Steps(dve, M["own"], own_per_head * i + 1)
                for b, (t0, n) in enumerate(TB):
                    dve.wait_ge(M["lin"], 6 * i + 5 + b)
                    nc.vector.tensor_copy(k[:, t0:t0 + n], PS[:, 3 + b, 0:n]).then_inc(M["k_out"], 1)
                dve.wait_ge(M["z_mm"], i + 1)
                full = PS[:, 0:2, :].rearrange("p b (t d) -> p (b t) d", d=DK)
                nc.vector.tensor_scalar(g[:, 0:NT - 1, :], full, 0.0, 1.0 / TAU, ALU.min, ALU.mult).then_inc(M["z_min"], 1)
                nc.vector.tensor_scalar(g[0:TAIL, NT - 1, :], PS[0:TAIL, 2, 0:DK], 0.0, 1.0 / TAU,
                                        ALU.min, ALU.mult).then_inc(M["z_min"], 1)
                dve.wait_ge(M["z_min"], 2 * i + 2)
                dve.wait_ge(M["act_own"], 4 * i + 4)
                for gg, ss in ((g[:, 0:NT - 1, :], soft[:, 0:NT - 1, :]), (g[0:TAIL, NT - 1, :], soft[0:TAIL, NT - 1, :])):
                    nc.vector.scalar_tensor_tensor(out=gg, in0=ss, scalar=-1.0 / TAU, in1=gg, op0=ALU.mult,
                                                   op1=ALU.add).then_inc(M["g_ready"], 1)
                for b in range(6):
                    dve.wait_ge(M["r_sig"], 6 * i + b + 1)
                    t0, n = TB[b % 3]
                    nc.vector.tensor_tensor(r[:, b // 3, t0:t0 + n], PS[:, b, 0:n], sg[:, b % 2, 0:n],
                                            ALU.mult).then_inc(M["r_out"], 1)
                for t, n, kind in tiles:
                    tok = slice(t * P, t * P + n)
                    dve.wait_ge(M["e_exp"], NT * i + t + 1)
                    Et = E[:, t % 2]
                    if t >= 1:
                        dve.wait_ge(M["st_mm"], NST * i + t)
                    nc.vector.tensor_tensor(Q[:, :, 0:n], Et[:, 0:LV + 1, 0:n],
                                            q[:, None, tok].broadcast_to([P, LV + 1, n]), ALU.mult).then_inc(M["qk"], 1)
                    nc.vector.tensor_tensor(K[:, 0:LV, 0:n], Et[:, 0:LV, 0:n],
                                            k[:, None, tok].broadcast_to([P, LV, n]), ALU.mult)
                    nc.vector.tensor_tensor(K[:, LV, 0:n], Et[:, LV + 1, 0:n], k[:, tok], ALU.mult).then_inc(M["qk"], 1)
                    dve.wait_ge(M["s_mm"], NT * i + t + 1)
                    step(nc.vector.tensor_tensor(prod[0:n, :, 0:n],
                                                 PS[0:n, 3:5, :].rearrange("p b (l i) -> p (b l) i", i=P)[:, :, 0:n],
                                                 pairs[0:n, kind, :, 0:n], ALU.mult))
                    nc.vector.tensor_reduce(sT[0:n, 0:n], prod[0:n, :, 0:n].rearrange("p l i -> p i l"), AX.X,
                                            ALU.add).then_inc(M["s_red"], 1)
                    if t < NT - 1:
                        dve.wait_ge(M["st_mm"], NST * i + t + 1)
                        if t == 0:
                            dve.wait_ge(M["st_free"], i + 1)
                            nc.vector.tensor_copy(S[:, :], PS[:, 7, 0:DV]).then_inc(M["st_out"], 1)
                        else:
                            dve.wait_ge(M["st_out"], NST * i + t)
                            nc.vector.scalar_tensor_tensor(out=S[:, :], in0=S[:, :], scalar=Et[:, LV, n - 1:n],
                                                           in1=PS[:, 7, 0:DV], op0=ALU.mult,
                                                           op1=ALU.add).then_inc(M["st_out"], 1)
                    else:
                        dve.wait_ge(M["t_out"], NT * i + NT + 1)
                        nc.vector.tensor_tensor(kTs[:, :, :], kT[0:n, None, :].broadcast_to([n, NSEQ, DK]),
                                                seq_rows[:, :, None].broadcast_to([n, NSEQ, DK]),
                                                ALU.mult).then_inc(M["kts"], 1)
                        for s in range(NSEQ):
                            dve.wait_ge(M["st_mm"], NST * i + NT + s)
                            nc.vector.scalar_tensor_tensor(out=Ss[:, s, :], in0=Ss[:, s, :],
                                                           scalar=Et[:, LV, (s + 1) * LSEQ - 1:(s + 1) * LSEQ],
                                                           in1=PS[:, 7, 0:DV], op0=ALU.mult,
                                                           op1=ALU.add).then_inc(M["st_out"], 1)
                dve.wait_ge(M["rooted"], 3 * i + 6)
                rs = soft[:].rearrange("p t d -> p (t d)")[:, 0:T]
                step(nc.vector.reciprocal(rs, rs))
                for e in range(2):
                    step(nc.vector.tensor_tensor(o[:, e, :], o[:, e, :], rs, ALU.mult))
                    nc.vector.scalar_tensor_tensor(out=ob[:, bass.ds(2 * i + e, 1), :].rearrange("p a t -> p (a t)"),
                                                   in0=o[:, e, :], scalar=gnorm[:, bass.ds(2 * i + e, 1)],
                                                   in1=r[:, e, :], op0=ALU.mult, op1=ALU.mult).then_inc(M["normed"], 1)
                assert step.n == own_per_head


def stream_weights(sp, steps, w, w_in, used, sources):
    for b, src in enumerate(sources):
        sp.dma_start(w[:, b, 0:src(0).shape[1]], src(0)).then_inc(w_in[b], 16)
    with sp.Fori(1, steps) as i:
        for b, src in enumerate(sources):
            mm, first, more = used(b)
            sp.wait_ge(mm, more * (i - 1) + first)
            sp.dma_start(w[:, b, 0:src(0).shape[1]], src(i)).then_inc(w_in[b], 16)


def conv_phase(nc, A, G):
    with Scope(nc, "conv") as sc:
        NB = 6
        h, a_in, PS = G["h"], G["a_in"], G["PS"]
        w = sc.sb("w", [P, NB, KD, P])
        cg, bg, y = (sc.sb(n, [P, T]) for n in ("cg", "bg", "y"))
        up = sc.sb("up", [P, CW - 1 + SEQ])
        us = sc.sb("us", [P, NSEQ, CW - 1 + LSEQ])
        taps, cbias = sc.sb("taps", [P, CW, CC]), sc.sb("cbias", [P, CC])
        past = sc.sb("past", [P, CC, NSEQ, CW - 1])
        last_p, last_s = sc.sb("last_p", [P, CC, CW - 1]), sc.sb("last_s", [P, CC, NSEQ, CW - 1])
        w_in = [sc.sem(f"w_in{b}") for b in range(NB)]
        small_in, c_mm, h_mm, b_mm, c_out, u_out, b_out, conv_out, own, saved = (sc.sem(n) for n in (
            "small_in c_mm h_mm b_mm c_out u_out b_out conv_out own saved").split())
        block = sc.block()
        sets = lambda n: [PS[:, 3 * (n % 2) + b] for b in range(3)]
        OPS = 3 + 2 * CW

        @block.sync
        def _(sp):
            for dst, src in ((taps, A["conv_w"]), (cbias, A["conv_b"]), (past, A["conv_state"])):
                sp.dma_start(dst[:], src).then_inc(small_in, 16)
            stream_weights(sp, CC // 2, w, w_in, lambda b: ((c_mm, h_mm, b_mm)[b % 3], 3 * (b // 3) + 3, 6), [lambda i, b=b: A["w_conv"][i, b] for b in range(NB)])
            sp.wait_ge(conv_out, CC + 1)
            sp.dma_start(A["out_conv_p"], last_p[:]).then_inc(saved, 16)
            sp.dma_start(A["out_conv_s"], last_s[:]).then_inc(saved, 16)
            sp.wait_ge(saved, 32)

        @block.tensor
        def _(pe):
            with pe.Fori(0, CC // 2) as i:
                for n in range(NB):
                    c, kind = n // 3, n % 3
                    pe.wait_ge(w_in[n], 16 * i + 16)
                    if kind == 0:
                        pe.wait_ge(u_out, 6 * i + 3 * c + 3)
                    elif kind == 1:
                        pe.wait_ge(b_out, 6 * i + 3 * c + 3)
                    else:
                        pe.wait_ge(c_out, 6 * i + 3 * c + 3)
                    for last in project(nc, sets(n), w[:, n], h, KD):
                        last.then_inc((c_mm, h_mm, b_mm)[kind], 1)

        @block.scalar
        def _(act):
            act.sem_inc(b_out, 3)
            with act.Fori(0, CC // 2) as i:
                for n in (0, 2, 3, 5):
                    c = n // 3
                    mm, out, dst = (c_mm, c_out, cg) if n % 3 == 0 else (b_mm, b_out, bg)
                    if n % 3 == 0:
                        act.wait_ge(u_out, 6 * i + 3 * c + 3)
                    else:
                        act.wait_ge(conv_out, 2 * i + c + 1)
                    for b, (t0, m) in enumerate(TB):
                        act.wait_ge(mm, 6 * i + 3 * c + b + 1)
                        nc.scalar.activation(dst[:, t0:t0 + m], sets(n)[b][:, 0:m], ACT.Copy).then_inc(out, 1)

        @block.vector
        def _(dve):
            dve.sem_inc(u_out, 3)
            dve.sem_inc(conv_out, 1)
            dve.wait_ge(small_in, 48)
            step = Steps(dve, own)
            step(nc.vector.memset(up[:, 0:CW - 1], 0.0))
            with dve.Fori(0, CC // 2) as i:
                step = Steps(dve, own, 2 * OPS * i + 1)
                for c in range(2):
                    ch = bass.ds(2 * i + c, 1)
                    step(nc.vector.tensor_copy(us[:, :, 0:CW - 1], past[:, ch].rearrange("p a s w -> p (a s) w")))
                    for b, (t0, m) in enumerate(TB):
                        dve.wait_ge(h_mm, 6 * i + 3 * c + b + 1)
                        dve.wait_ge(c_out, 6 * i + 3 * c + b + 1)
                        src = sets(3 * c + 1)[b]
                        n = min(m, SEQ - t0)
                        ins = nc.vector.tensor_tensor(up[:, CW - 1 + t0:CW - 1 + t0 + n], src[:, 0:n],
                                                      cg[:, t0:t0 + n], ALU.mult)
                        if n < m:
                            ins = nc.vector.tensor_tensor(us[:, :, CW - 1:], src[:, n:m].rearrange("p (s t) -> p s t", s=NSEQ),
                                                          cg[:, SEQ:T].rearrange("p (s t) -> p s t", s=NSEQ), ALU.mult)
                        ins.then_inc(u_out, 1)
                    dve.wait_ge(u_out, 6 * i + 3 * c + 6)
                    ys = y[:, SEQ:T].rearrange("p (s t) -> p s t", s=NSEQ)
                    tap = lambda n: taps[:, n, ch]
                    step(nc.vector.tensor_copy(last_p[:, ch].rearrange("p a w -> p (a w)"), up[:, SEQ:]))
                    step(nc.vector.tensor_copy(last_s[:, ch].rearrange("p a s w -> p (a s) w"), us[:, :, LSEQ:]))
                    for full, out, n in ((up, y[:, 0:SEQ], SEQ), (us, ys, LSEQ)):
                        at = lambda q: full[:, q:q + n] if full is up else full[:, :, q:q + n]
                        step(nc.vector.tensor_scalar(out, at(CW - 1), tap(CW - 1), cbias[:, ch], ALU.mult, ALU.add))
                        for q in range(CW - 1):
                            step(nc.vector.scalar_tensor_tensor(out=out, in0=at(q), scalar=tap(q), in1=out,
                                                                op0=ALU.mult, op1=ALU.add))
                    dve.wait_ge(b_out, 6 * i + 3 * c + 6)
                    nc.vector.tensor_tensor(a_in[:, ch].rearrange("p a t -> p (a t)"), y[:, :], bg[:, :],
                                            ALU.mult).then_inc(conv_out, 1)
                    dve.wait_ge(conv_out, 2 * i + c + 2)
                    assert step.n == OPS * (c + 1)


def merge_phase(nc, A, G):
    with Scope(nc, "merge") as sc:
        NB = 4
        PS, merged = G["PS"], G["merged"]
        w = sc.sb("w", [P, NB, KD, P])
        sa, sb_, ma, mb = (sc.sb(n, [P, T]) for n in ("sig_a", "sig_b", "part_a", "part_b"))
        w_in = [sc.sem(f"w_in{b}") for b in range(NB)]
        mm, sig, part, done = (sc.sem(n) for n in "mm sig part done".split())
        block = sc.block()
        sets = lambda n: [PS[:, 3 * (n % 2) + b] for b in range(3)]

        @block.sync
        def _(sp):
            stream_weights(sp, KD, w, w_in, lambda b: (mm, 3 * b + 3, 3 * NB), [lambda i: A["w_gate_ab"][i, 0], lambda i: A["w_gate_ab"][i, 1],
                                                     lambda i: A["w_proj_a"][i], lambda i: A["w_proj_b"][i]])

        @block.tensor
        def _(pe):
            with pe.Fori(0, KD) as i:
                for n, (rhs, nk) in enumerate(((G["h"], KD), (G["h"], KD), (G["a_in"], CC), (G["ob"], KD))):
                    pe.wait_ge(w_in[n], 16 * i + 16)
                    if n < 2:
                        pe.wait_ge(part, 6 * i + 3 * n + 3)
                    else:
                        pe.wait_ge(sig, 6 * i + 3 * (n - 2) + 3)
                    for last in project(nc, sets(n), w[:, n], rhs, nk):
                        last.then_inc(mm, 1)

        @block.scalar
        def _(act):
            with act.Fori(0, KD) as i:
                for n, dst in enumerate((sa, sb_)):
                    for b, (t0, m) in enumerate(TB):
                        act.wait_ge(mm, 12 * i + 3 * n + b + 1)
                        act.wait_ge(part, 6 * i + 3 * n + b + 1)
                        nc.scalar.activation(dst[:, t0:t0 + m], sets(n)[b][:, 0:m], ACT.Sigmoid).then_inc(sig, 1)

        @block.vector
        def _(dve):
            dve.sem_inc(part, 6)
            with dve.Fori(0, KD) as i:
                for n, (s, dst) in enumerate(((sa, ma), (sb_, mb))):
                    for b, (t0, m) in enumerate(TB):
                        dve.wait_ge(mm, 12 * i + 6 + 3 * n + b + 1)
                        dve.wait_ge(sig, 6 * i + 3 * n + b + 1)
                        nc.vector.tensor_tensor(dst[:, t0:t0 + m], sets(n)[b][:, 0:m], s[:, t0:t0 + m],
                                                ALU.mult).then_inc(part, 1)
                dve.wait_ge(part, 6 * i + 12)
                nc.vector.tensor_tensor(merged[:, bass.ds(i, 1)].rearrange("p a t -> p (a t)"), ma[:, :], mb[:, :],
                                        ALU.add).then_inc(done, 1)
                dve.wait_ge(done, i + 1)


def out_phase(nc, A, G):
    with Scope(nc, "out") as sc:
        NB = 2
        PS, merged, x, m = G["PS"], G["merged"], G["h"], G["ob"]
        w = sc.sb("w", [P, NB, KD, P])
        sq = sc.sb("sq", [P, 2, T])
        root, tmp = sc.sb("root", [P, T]), sc.sb("tmp", [P, T])
        w_in = [sc.sem(f"w_in{b}") for b in range(NB)]
        x_in, mm, m_out, own, saved = (sc.sem(n) for n in "x_in mm m_out own saved".split())
        x2_done, h2_done = sc.sem("x2_done"), sc.sem("h2_done")
        n1, n2 = norm_sems(sc, "post_"), norm_sems(sc, "pre_")
        block = sc.block()
        sets = lambda n: [PS[:, 3 * (n % 2) + b] for b in range(3)]

        @block.sync
        def _(sp):
            for k in range(KD):
                sp.dma_start(x[:, k, :], A["x"][k]).then_inc(x_in, 16)
            stream_weights(sp, KD // NB, w, w_in, lambda b: (mm, 3 * b + 3, 3 * NB), [lambda i, b=b: A["w_out"][2 * i + b] for b in range(NB)])
            sp.wait_ge(x2_done, 1)
            sp.dma_start(A["x2"], x[:]).then_inc(saved, 16)
            sp.wait_ge(h2_done, 1)
            sp.dma_start(A["h2"], m[:]).then_inc(saved, 16)
            sp.wait_ge(saved, 32)

        @block.tensor
        def _(pe):
            with pe.Fori(0, KD // NB) as i:
                for n in range(NB):
                    pe.wait_ge(w_in[n], 16 * i + 16)
                    pe.wait_ge(m_out, 6 * i + 3 * n + 3)
                    for last in project(nc, sets(n), w[:, n], merged, KD):
                        last.then_inc(mm, 1)
            pe.wait_ge(m_out, 6 + 3 * KD)
            norm_sums(nc, pe, n1, G["ones"], sq, sets(0))
            norm_sums(nc, pe, n2, G["ones"], sq, sets(1))

        @block.scalar
        def _(act):
            act.sem_inc(m_out, 6)
            with act.Fori(0, KD // NB) as i:
                for n in range(NB):
                    for b, (t0, q) in enumerate(TB):
                        act.wait_ge(mm, 6 * i + 3 * n + b + 1)
                        nc.scalar.activation(m[:, bass.ds(2 * i + n, 1), t0:t0 + q].rearrange("p a t -> p (a t)"),
                                             sets(n)[b][:, 0:q], ACT.Copy).then_inc(m_out, 1)
            act.wait_ge(m_out, 6 + 3 * KD)
            norm_squares(nc, act, n1, m, sq)
            norm_roots(nc, act, n1, sets(0), root, G["eps"])
            act.wait_ge(x2_done, 1)
            norm_squares(nc, act, n2, x, sq)
            norm_roots(nc, act, n2, sets(1), root, G["eps"])

        @block.vector
        def _(dve):
            step = Steps(dve, own)
            dve.wait_ge(x_in, 16 * KD)
            dve.wait_ge(n1["rooted"], 3)
            step(nc.vector.reciprocal(root[:, :], root[:, :]))
            residual(nc, step, x, m, root, tmp, G["gate"][:, 0])
            dve.sem_inc(x2_done, 1)
            dve.wait_ge(n2["rooted"], 3)
            step(nc.vector.reciprocal(root[:, :], root[:, :]))
            modulate(nc, step, m, x, root, tmp, G["gain"][:, 1], G["shift"][:, 1])
            dve.sem_inc(h2_done, 1)


def keys_phase(nc, A, G):
    with Scope(nc, "keys") as sc:
        NB = 2
        PS = G["PS"]
        h_hi, h_lo = G["h_hi"], G["h_lo"]
        h2 = sc.sb("h2", [P, KD, T])
        w = sc.sb("w", [P, NB, KD, P])
        w_hi, w_lo = sc.sb("w_hi", [P, NB, KD, P], F32R), sc.sb("w_lo", [P, NB, KD, P], F32R)
        sub = sc.sb("sub", [P, 2 * PH, NK])
        qT = sc.sb("qT", [P, NB, T])
        s1 = sc.sb("s1", [P, NB, NT, NK])
        s2 = sc.sb("s2", [P, NT, NK])
        best, place = sc.sb("best", [P, NT, TOPK]), sc.sb("place", [P, NT, TOPK], U32)
        w_in = [sc.sem(f"w_in{b}") for b in range(NB)]
        h_in = [sc.sem(f"h_in{k}") for k in range(KD)]
        sub_in, q_mm, q_out, s_mm, s_out, own, listed, passed, high, low, h_high, h_low, q_free, passed_pool = (sc.sem(n) for n in (
            "sub_in q_mm q_out s_mm s_out own listed passed high low h_high h_low q_free passed_pool").split())
        block = sc.block()
        sets = lambda n: [PS[:, 3 * (n % 2) + b] for b in range(3)]
        SB = ((6, 0), (1, 3))
        pairbank = lambda n: (PS[:, 6:8, :], PS[:, 1:3, :])[n].rearrange("p b (t d) -> p (b t) d", d=NK)
        lone = lambda n: PS[0:TAIL, (0, 3)[n], 0:NK]
        OPS = 5

        @block.sync
        def _(sp):
            for k in range(KD):
                sp.dma_start(h2[:, k, :], A["h2"][:, k, :]).then_inc(h_in[k], 16)
            sp.dma_start(sub[:], A["subkeys"]).then_inc(sub_in, 16)
            stream_weights(sp, PH, w, w_in, lambda b: (low, b + 1, NB), [lambda i, b=b: A["w_query"][2 * i + b] for b in range(NB)])

        @block.tensor
        def _(pe):
            pe.wait_ge(h_low, KD)
            pe.wait_ge(sub_in, 16)
            with pe.Fori(0, PH) as i:
                for n in range(NB):
                    pe.wait_ge(low, NB * i + n + 1)
                    pe.wait_ge(s_out, 4 * i + 4)
                    for last in project3(nc, sets(n), w_hi[:, n], w_lo[:, n], h_hi, h_lo, KD):
                        last.then_inc(q_mm, 1)
                for n in range(NB):
                    pe.wait_ge(q_out, 6 * i + (3, 6)[n])
                    for t in range(NT):
                        out = pairbank(n)[:, t, :] if t < NT - 1 else lone(n)
                        last = nc.tensor.matmul(out, qT[:, n, t * P:t * P + rows(t)],
                                                sub[:, bass.ds(2 * i + n, 1), :].rearrange("p a k -> p (a k)"),
                                                start=True, stop=True)
                    last.then_inc(s_mm, 1)

        @block.gpsimd
        def _(pool):
            with pool.Fori(0, PH) as i:
                for n in range(NB):
                    pool.wait_ge(w_in[n], 16 * i + 16)
                    pool.wait_ge(q_free, NB * i + n + 1)
                    pool.sem_inc(passed_pool, 1)
                    split(nc, pool, w_hi[:, n], w_lo[:, n], w[:, n], high, low, NB * i + n + 1)

        @block.scalar
        def _(act):
            act.sem_inc(s_out, 4)
            act.sem_inc(q_free, 2)
            for k in range(KD):
                act.wait_ge(h_in[k], 16)
                nc.scalar.activation(h_hi[:, k, :], h2[:, k, :], ACT.Copy).then_inc(h_high, 1)
            with act.Fori(0, PH) as i:
                for n in range(NB):
                    for b, (t0, m) in enumerate(TB):
                        act.wait_ge(q_mm, 6 * i + 3 * n + b + 1)
                        nc.scalar.activation(qT[:, n, t0:t0 + m], sets(n)[b][:, 0:m], ACT.Copy).then_inc(q_out, 1)
                    act.sem_inc(q_free, 1)
                for n in range(NB):
                    act.wait_ge(s_mm, 2 * i + n + 1)
                    act.wait_ge(listed, 2 * i + n + 1)
                    nc.scalar.activation(s1[:, n, 0:NT - 1, :], pairbank(n), ACT.Copy).then_inc(s_out, 1)
                    nc.scalar.activation(s1[0:TAIL, n, NT - 1, :], lone(n), ACT.Copy).then_inc(s_out, 1)

        @block.vector
        def _(dve):
            dve.sem_inc(listed, 2)
            step = Steps(dve, own)
            step(nc.vector.memset(G["best"][:], 0.0))
            step(nc.vector.memset(G["place"][:], 0.0))
            for k in range(KD):
                dve.wait_ge(h_high, k + 1)
                nc.vector.tensor_tensor(h_lo[:, k, :], h2[:, k, :], h_hi[:, k, :].bitcast(F32),
                                        ALU.subtract).then_inc(h_low, 1)
            with dve.Fori(0, PH) as i:
                for n in range(NB):
                    step = Steps(dve, own, OPS * (NB * i + n) + 2)
                    dve.wait_ge(s_out, 4 * i + 2 * n + 6)
                    dve.sem_inc(passed, 1)
                    for t in range(NT):
                        last = nc.vector.max(best[0:rows(t), t, 0:8], s1[0:rows(t), n, t, :])
                    step(last, passed)
                    for t in range(NT):
                        nc.vector.max_index(place[0:rows(t), t, 0:8], best[0:rows(t), t, 0:8], s1[0:rows(t), n, t, :])
                        last = nc.vector.match_replace(s2[0:rows(t), t, :], best[0:rows(t), t, 0:8],
                                                       s1[0:rows(t), n, t, :], LOWEST)
                    step(last, passed)
                    for t in range(NT):
                        last = nc.vector.max(best[0:rows(t), t, 8:16], s2[0:rows(t), t, :])
                    step(last, passed)
                    for t in range(NT):
                        last = nc.vector.max_index(place[0:rows(t), t, 8:16], best[0:rows(t), t, 8:16], s2[0:rows(t), t, :])
                    step(last)
                    side = bass.ds(2 * i + n, 1)
                    for dst, src in ((G["best"], best), (G["place"], place)):
                        last = nc.vector.tensor_copy(dst[:, 0:NT - 1, side, :].rearrange("p t a k -> p t (a k)"), src[:, 0:NT - 1, :])
                        last = nc.vector.tensor_copy(dst[0:TAIL, NT - 1, side, :].rearrange("p a k -> p (a k)"), src[0:TAIL, NT - 1, :])
                    step(last)
                    dve.sem_inc(listed, 1)


class Hidden:

    def __init__(self, sc, A, G, slots, banks, first):
        self.A, self.G, self.slots, self.banks, self.first, self.PS = A, G, slots, banks, first, G["PS"]
        self.u = sc.sb("u", [P, slots, KD, P])
        self.hi, self.lo = sc.sb("u_hi", [P, slots, KD, P], F32R), sc.sb("u_lo", [P, slots, KD, P], F32R)
        self.ge = sc.sb("ge", [P, slots, T])
        names = "u_in u_high u_low u_mm ge_out u_passed ge_free hid_saved".split()
        (_, self.high, self.low, self.mm, self.out, self.passed, self.free, _) = (sc.sem(n) for n in names)
        self.u_in = [sc.sem(f"u_in_{b}") for b in range(slots)]
        self.saved = [sc.sem(f"saved_{b}") for b in range(slots)]

    def bring(self, sp, n, slot, turn, reuse=True):
        if reuse:
            sp.wait_ge(self.low, n - self.slots + 1)
        sp.dma_start(self.u[:, slot], self.A["u"][self.first + n]).then_inc(self.u_in[slot], 16)

    def split(self, nc, pool, n, slot, turn):
        pool.wait_ge(self.u_in[slot], 16 * turn + 16)
        pool.wait_ge(self.out, 3 * n + 3)
        pool.sem_inc(self.passed, 1)
        split(nc, pool, self.hi[:, slot], self.lo[:, slot], self.u[:, slot], self.high, self.low, n + 1)

    def multiply(self, nc, pe, n, slot, b):
        t0, m = TB[b]
        if b == 0:
            pe.wait_ge(self.low, n + 1)
        pe.wait_ge(self.out, 3 * n + b + 3 * self.slots - len(self.banks) + 1)
        out, h_hi, h_lo = self.PS[:, self.banks[b], 0:m], self.G["h_hi"], self.G["h_lo"]
        for k in range(KD):
            hi, lo = h_hi[:, k, t0:t0 + m], h_lo[:, k, t0:t0 + m]
            nc.tensor.matmul(out, self.hi[:, slot, k, :], hi, start=(k == 0), stop=False)
            nc.tensor.matmul(out, self.hi[:, slot, k, :], lo, start=False, stop=False)
            last = nc.tensor.matmul(out, self.lo[:, slot, k, :], hi, start=False, stop=(k == KD - 1))
        last.then_inc(self.mm, 1)

    def gelu(self, nc, act, n, slot, b):
        t0, m = TB[b]
        if b == 0:
            act.wait_ge(self.free, n + 1)
        act.wait_ge(self.mm, 3 * n + b + 1)
        nc.scalar.activation(self.ge[:, slot, t0:t0 + m], self.PS[:, self.banks[b], 0:m],
                             ACT.Gelu_apprx_tanh).then_inc(self.out, 1)

    def credits(self, act, sp):
        if act is not None:
            act.sem_inc(self.out, 3 * self.slots)
        if sp is not None:
            sp.sem_inc(self.free, self.slots)

    def put(self, sp, n, slot):
        sp.wait_ge(self.out, 3 * n + 3 + 3 * self.slots)
        sp.dma_start(self.A["hid"][self.first + n], self.ge[:, slot]).then_inc(self.saved[slot], 16)

    def landed(self, sp, slot, turn):
        sp.wait_ge(self.saved[slot], 16 * turn + 16)
        sp.sem_inc(self.free, 1)


def pick_phase(nc, A, G):
    with Scope(nc, "pick") as sc:
        PS = G["PS"]
        sums = sc.sb("sums", [P, PH, TOPK * TOPK])
        sums2 = sc.sb("sums2", [P, PH, TOPK * TOPK])
        top, at = sc.sb("top", [P, PH, TOPK]), sc.sb("at", [P, PH, TOPK], U32)
        half = [sc.sb(f"half{s}", [P, HK], U32) for s in range(2)]
        halff = [sc.sb(f"halff{s}", [P, HK]) for s in range(2)]
        eq = [sc.sb(f"eq{s}", [P, HK, TOPK]) for s in range(2)]
        route = sc.sb("route", [P, 3, HK])
        diff, total = sc.sb("diff", [P, PH, TOPK]), sc.sb("total", [P, PH])
        own, t_mm, t_out, d_out, e_out, passed = (sc.sem(n) for n in "own t_mm t_out d_out e_out passed".split())
        NS = PICK_CHUNKS
        hid = Hidden(sc, A, G, NS, (1, 2, 3), 0)
        block = sc.block()
        OPS = 18

        def tiles(eng, body):
            with eng.Fori(0, NT - 1) as i:
                body(i, NS)
            body(NT - 1, NS - 1)

        @block.sync
        def _(sp):
            hid.credits(None, sp)
            for c in range(NS):
                hid.bring(sp, c, c, 0, reuse=False)

            def move(i, chunks):
                if chunks == NS:
                    for c in range(NS - 1):
                        hid.bring(sp, NS * (i + 1) + c, c, None)
                for c in range(chunks):
                    hid.put(sp, NS * i + c, c)
                    if c == 0 and chunks == NS:
                        pass
                if chunks == NS:
                    hid.bring(sp, NS * (i + 1) + NS - 1, NS - 1, None)
                for c in range(chunks):
                    hid.landed(sp, c, i)
            tiles(sp, move)

        @block.gpsimd
        def _(pool):
            def parts(i, chunks):
                for c in range(chunks):
                    hid.split(nc, pool, NS * i + c, c, i)
            tiles(pool, parts)

        @block.tensor
        def _(pe):
            def work(i, chunks):
                for c in range(chunks):
                    for b in range(len(TB)):
                        hid.multiply(nc, pe, NS * i + c, c, b)
                pe.wait_ge(own, OPS * i + OPS)
                pe.wait_ge(t_out, i + 1)
                for n in range(3):
                    last = nc.tensor.transpose(PS[:, 0, n * P:(n + 1) * P], route[:, n, :], G["ident"][:, :])
                last.then_inc(t_mm, 1)
            tiles(pe, work)

        @block.scalar
        def _(act):
            act.sem_inc(t_out, 1)
            hid.credits(act, None)

            def work(i, chunks):
                for c in range(chunks):
                    for b in range(len(TB)):
                        hid.gelu(nc, act, NS * i + c, c, b)
                    if c == 1:
                        act.wait_ge(d_out, i + 1)
                        nc.scalar.activation(diff[:], diff[:], ACT.Exp).then_inc(e_out, 1)
                act.wait_ge(t_mm, i + 1)
                nc.scalar.activation(G["routeT"][:, :, bass.ds(i * P, P)],
                                     PS[:, 0, 0:3 * P].rearrange("p (n t) -> p n t", n=3), ACT.Copy).then_inc(t_out, 1)
            tiles(act, work)

        @block.vector
        def _(dve):
            with dve.Fori(0, NT) as i:
                step = Steps(dve, own, OPS * i)
                sv = G["best"][:, bass.ds(i, 1)].rearrange("p a (h s) k -> p (a h) s k", s=2)
                si = G["place"][:, bass.ds(i, 1)].rearrange("p a (h s) k -> p (a h) s k", s=2)
                step(nc.vector.tensor_tensor(sums[:].rearrange("p h (a b) -> p h a b", a=TOPK),
                                             sv[:, :, 0, :, None].broadcast_to([P, PH, TOPK, TOPK]),
                                             sv[:, :, 1, None, :].broadcast_to([P, PH, TOPK, TOPK]), ALU.add), passed)
                for hh in range(PH):
                    last = nc.vector.max(top[:, hh, 0:8], sums[:, hh, :])
                step(last, passed)
                for hh in range(PH):
                    nc.vector.max_index(at[:, hh, 0:8], top[:, hh, 0:8], sums[:, hh, :])
                    last = nc.vector.match_replace(sums2[:, hh, :], top[:, hh, 0:8], sums[:, hh, :], LOWEST)
                step(last, passed)
                for hh in range(PH):
                    last = nc.vector.max(top[:, hh, 8:16], sums2[:, hh, :])
                step(last, passed)
                for hh in range(PH):
                    last = nc.vector.max_index(at[:, hh, 8:16], top[:, hh, 8:16], sums2[:, hh, :])
                step(last)
                nc.vector.tensor_tensor(diff[:], top[:], top[:, :, 0:1].broadcast_to([P, PH, TOPK]),
                                        ALU.subtract).then_inc(d_out, 1)
                atf = at[:].rearrange("p h k -> p (h k)")
                step(nc.vector.tensor_scalar(half[0][:, :], atf, 4, None, ALU.logical_shift_right))
                step(nc.vector.tensor_scalar(half[1][:, :], atf, TOPK - 1, None, ALU.bitwise_and))
                for n in range(2):
                    step(nc.vector.tensor_copy(halff[n][:, :], half[n][:, :]))
                for n in range(2):
                    step(nc.vector.tensor_tensor(eq[n][:], halff[n][:, :, None].broadcast_to([P, HK, TOPK]),
                                                 G["iota"][:, None, 0:TOPK].broadcast_to([P, HK, TOPK]), ALU.is_equal))
                    e4 = eq[n][:].rearrange("p (h k) a -> p h k a", h=PH)
                    step(nc.vector.tensor_tensor(e4, e4, si[:, :, n, None, :].broadcast_to([P, PH, TOPK, TOPK]), ALU.mult))
                dve.wait_ge(t_out, i + 1)
                for n in range(2):
                    step(nc.vector.tensor_reduce(route[:, n, :], eq[n][:], AX.X, ALU.add))
                dve.wait_ge(e_out, i + 1)
                step(nc.vector.tensor_reduce(total[:, :], diff[:], AX.X, ALU.add))
                step(nc.vector.reciprocal(total[:, :], total[:, :]))
                step(nc.vector.tensor_tensor(route[:, 2, :].rearrange("p (h k) -> p h k", h=PH), diff[:],
                                             total[:, :, None].broadcast_to([P, PH, TOPK]), ALU.mult))
                assert step.n == OPS


def gates_phase(nc, A, G):
    with Scope(nc, "gates") as sc:
        PS, routeT = G["PS"], G["routeT"]
        NG, TG = 4, 4
        hot_i, hot_j = sc.sb("hot_i", [P, NG, TG, NK]), sc.sb("hot_j", [P, NG, TG, NK])
        part = sc.sb("part", [P, 2, 3, GB])
        gm = sc.sb("gm", [P, 2, NK, GB])
        hot, mm, out, saved, gm_free, own = (sc.sem(n) for n in "hot mm out saved gm_free own".split())
        NB = 4
        hid = Hidden(sc, A, G, 2, (4, 5, 6), PICK_CHUNKS * NT - 1)
        block = sc.block()
        PER = GB // TG
        units = [(c, b) for c in range(GATE_CHUNKS) for b in range(len(TB))]
        after = [units[len(units) * g // PER:len(units) * (g + 1) // PER] for g in range(PER)]
        assert PICK_CHUNKS * NT - 1 + GATE_CHUNKS * NGB == NK

        def blocks(eng, body):
            with eng.Fori(0, NGB // 2) as i:
                for b in range(2):
                    body(2 * i + b, b)
            assert NGB % 2
            body(NGB - 1, 0, True)

        @block.sync
        def _(sp):
            sp.sem_inc(gm_free, 2)
            hid.credits(None, sp)
            for c in range(2):
                hid.bring(sp, c, c, None, reuse=False)

            def move(blk, b, last=False):
                for c in range(GATE_CHUNKS):
                    n = GATE_CHUNKS * blk + c
                    if not (last and c >= GATE_CHUNKS - 2):
                        hid.bring(sp, n + 2, c % 2, None)
                    hid.put(sp, n, c % 2)
                    hid.landed(sp, c % 2, GATE_CHUNKS // 2 * blk + c // 2)
                sp.wait_ge(out, PER * blk + PER + NB)
                sp.dma_start(A["gm"][blk], gm[:, b]).then_inc(saved, 16)
                sp.wait_ge(saved, 16 * blk + 16)
                sp.sem_inc(gm_free, 1)
            blocks(sp, move)

        @block.gpsimd
        def _(pool):
            def parts(blk, b, last=False):
                for c in range(GATE_CHUNKS):
                    hid.split(nc, pool, GATE_CHUNKS * blk + c, c % 2, GATE_CHUNKS // 2 * blk + c // 2)
            blocks(pool, parts)

        @block.vector
        def _(dve):
            def build(blk, b, last=False):
                nc.vector.tensor_copy(part[:, b], routeT[:, :, bass.ds(blk * GB, GB)]).then_inc(own, 1)
                dve.wait_ge(own, blk + 1)
                for g in range(PER):
                    dve.wait_ge(mm, PER * blk + g + 1)
                    for t in range(TG):
                        at = g * TG + t
                        nc.vector.tensor_scalar(hot_i[:, g % NG, t, :], G["iota"][:, :], part[:, b, 0, at:at + 1],
                                                None, ALU.is_equal)
                        last = nc.vector.tensor_scalar(hot_j[:, g % NG, t, :], G["iota"][:, :],
                                                       part[:, b, 1, at:at + 1], part[:, b, 2, at:at + 1],
                                                       ALU.is_equal, ALU.mult)
                    last.then_inc(hot, 1)
            blocks(dve, build)

        @block.tensor
        def _(pe):
            pe.sem_inc(mm, NG)
            def multiply(blk, b, last=False):
                for g in range(PER):
                    pe.wait_ge(hot, PER * blk + g + 1)
                    pe.wait_ge(out, PER * blk + g + 1)
                    for t in range(TG):
                        last = nc.tensor.matmul(PS[:, g % NB, t * NK:(t + 1) * NK], hot_i[:, g % NG, t, :],
                                                hot_j[:, g % NG, t, :], start=True, stop=True)
                    last.then_inc(mm, 1)
                    for c, q in after[g]:
                        hid.multiply(nc, pe, GATE_CHUNKS * blk + c, c % 2, q)
            blocks(pe, multiply)

        @block.scalar
        def _(act):
            act.sem_inc(out, NB)
            hid.credits(act, None)

            def empty(blk, b, last=False):
                act.wait_ge(gm_free, blk + 1)
                for g in range(PER):
                    act.wait_ge(mm, PER * blk + g + 1 + NG)
                    nc.scalar.activation(gm[:, b, :, g * TG:(g + 1) * TG].rearrange("p j t -> p t j"),
                                         PS[:, g % NB, :].rearrange("p (t j) -> p t j", t=TG), ACT.Copy).then_inc(out, 1)
                    for c, q in after[g]:
                        hid.gelu(nc, act, GATE_CHUNKS * blk + c, c % 2, q)
            blocks(act, empty)


def experts_phase(nc, A, G):
    with Scope(nc, "exp") as sc:
        PS, acc = G["PS"], G["acc"]
        v, v_hi, v_lo = sc.sb("v", [P, CP, D]), sc.sb("v_hi", [P, CP, D], F32R), sc.sb("v_lo", [P, CP, D], F32R)
        hid, gm = sc.sb("hid", [P, CP, T]), sc.sb("gm", [P, CP, NGB, GB])
        pr = sc.sb("pr", [P, 3, 384])
        w_hi, w_lo = sc.sb("w_hi", [P, 2, CP, T], F32R), sc.sb("w_lo", [P, 2, CP, T], F32R)
        v_in, v_high, v_low, pr_out, w_high, w_low, v_mm, acc_out = (sc.sem(n) for n in (
            "v_in v_high v_low pr_out w_high w_low v_mm acc_out").split())
        c_in = [sc.sem(f"c_in{c}") for c in range(CP)]
        block = sc.block()
        NW, NV, NBANK = CP * len(TB), KD * len(TB), 8
        w_tiles = [(c, t0, n) for c in range(CP) for t0, n in TB]
        v_tiles = [(d, t0, n) for d in range(KD) for t0, n in TB]
        slices = [slice(d * P, (d + 1) * P) for d in range(KD)]

        def steps(eng, body):
            with eng.Fori(0, NSTEP // 2 - 1) as i:
                for par in range(2):
                    body(2 * i + par, par, False)
            body(NSTEP - 2, 0, False)
            body(NSTEP - 1, 1, True)

        @block.sync
        def _(sp):
            def chunk(i, c):
                sp.dma_start(hid[:, c], A["hid"][CP * i + c]).then_inc(c_in[c], 16)
                sp.dma_start(gm[:, c], A["gm"][:, :, bass.ds(CP * i + c, 1), :].rearrange("b p a t -> p b (a t)")
                             ).then_inc(c_in[c], 16)
            for c in range(CP):
                chunk(0, c)
            sp.dma_start(v[:], A["v"][0]).then_inc(v_in, 16)

            def ahead(i):
                for c in range(CP):
                    sp.wait_ge(pr_out, NW * (i - 1) + len(TB) * (c + 1) + 3)
                    chunk(i, c)
                sp.wait_ge(v_low, KD * (i - 1) + KD)
                sp.dma_start(v[:], A["v"][i]).then_inc(v_in, 16)
            with sp.Fori(1, NSTEP) as i:
                ahead(i)

        @block.tensor
        def _(pe):
            def step(i, par, last_step):
                pe.wait_ge(w_low, NW * i + NW + 3)
                for m, (d, t0, n) in enumerate(v_tiles):
                    if m % len(TB) == 0:
                        pe.wait_ge(v_low, KD * i + d + 1)
                    pe.wait_ge(acc_out, NV * i + m + 1)
                    out = PS[:, m % NBANK, 0:n]
                    for c in range(CP):
                        hi, lo = w_hi[:, par, c, t0:t0 + n], w_lo[:, par, c, t0:t0 + n]
                        nc.tensor.matmul(out, v_hi[:, c, slices[d]], hi, start=(c == 0), stop=False)
                        nc.tensor.matmul(out, v_hi[:, c, slices[d]], lo, start=False, stop=False)
                        last = nc.tensor.matmul(out, v_lo[:, c, slices[d]], hi, start=False, stop=(c == CP - 1))
                    last.then_inc(v_mm, 1)
            steps(pe, step)

        @block.scalar
        def _(act):
            def high_w(i, m, par):
                c, t0, n = w_tiles[m]
                act.wait_ge(pr_out, NW * i + m + 1 + 3)
                nc.scalar.activation(w_hi[:, par, c, t0:t0 + n], pr[:, m % 3, 0:n], ACT.Copy).then_inc(w_high, 1)

            def high_v(d):
                nc.scalar.activation(v_hi[:, :, slices[d]], v[:, :, slices[d]], ACT.Copy).then_inc(v_high, 1)
            act.wait_ge(v_in, 16)
            for d in range(KD):
                high_v(d)
            for m in range(NW):
                high_w(0, m, 0)

            def step(i, par, last_step):
                if last_step:
                    return
                for d in range(KD):
                    for m in range(NW * d // KD, NW * (d + 1) // KD):
                        high_w(i + 1, m, 1 - par)
                    act.wait_ge(v_in, 16 * i + 32)
                    act.wait_ge(v_mm, NV * i + len(TB) * (d + 1))
                    high_v(d)
            steps(act, step)

        @block.gpsimd
        def _(pool):
            def low_v(d):
                nc.gpsimd.tensor_tensor(v_lo[:, :, slices[d]], v[:, :, slices[d]], v_hi[:, :, slices[d]].bitcast(F32),
                                        ALU.subtract).then_inc(v_low, 1)
            for d in range(KD):
                pool.wait_ge(v_high, d + 1)
                low_v(d)
            with pool.Fori(1, NSTEP) as i:
                for d in range(KD):
                    pool.wait_ge(v_high, KD * i + d + 1)
                    low_v(d)

        @block.vector
        def _(dve):
            dve.sem_inc(pr_out, 3)
            dve.sem_inc(w_low, 3)
            nc.vector.memset(acc[:], 0.0).then_inc(acc_out, NBANK)

            def product(i, m):
                c, t0, n = w_tiles[m]
                if m % len(TB) == 0:
                    dve.wait_ge(c_in[c], 32 * i + 32)
                dve.wait_ge(w_low, NW * i + m + 1)
                nc.vector.tensor_tensor(pr[:, m % 3, 0:n], hid[:, c, t0:t0 + n],
                                        gm[:, c].rearrange("p b t -> p (b t)")[:, t0:t0 + n], ALU.mult).then_inc(pr_out, 1)

            def low_w(i, m, par):
                c, t0, n = w_tiles[m]
                dve.wait_ge(w_high, NW * i + m + 1)
                nc.vector.tensor_tensor(w_lo[:, par, c, t0:t0 + n], pr[:, m % 3, 0:n],
                                        w_hi[:, par, c, t0:t0 + n].bitcast(F32), ALU.subtract).then_inc(w_low, 1)
            for m in range(NW):
                product(0, m)
                if m:
                    low_w(0, m - 1, 0)
            low_w(0, NW - 1, 0)

            def step(i, par, last_step):
                dve.wait_ge(acc_out, NV * i + NBANK)
                for m, (d, t0, n) in enumerate(v_tiles):
                    if m % 2 == 0 and not last_step:
                        product(i + 1, m // 2)
                        if m:
                            low_w(i + 1, m // 2 - 1, 1 - par)
                    dve.wait_ge(v_mm, NV * i + m + 1)
                    nc.vector.tensor_tensor(acc[:, d, t0:t0 + n], acc[:, d, t0:t0 + n], PS[:, m % NBANK, 0:n],
                                            ALU.add).then_inc(acc_out, 1)
                if not last_step:
                    low_w(i + 1, NW - 1, 1 - par)
            steps(dve, step)


def final_phase(nc, A, G):
    with Scope(nc, "fin") as sc:
        PS, acc = G["PS"], G["acc"]
        x = sc.sb("x", [P, KD, T])
        sq = sc.sb("sq", [P, 2, T])
        root, tmp = sc.sb("root", [P, T]), sc.sb("tmp", [P, T])
        x_in, own, done, saved = (sc.sem(n) for n in "x_in own done saved".split())
        ns = norm_sems(sc)
        block = sc.block()
        banks = [PS[:, b] for b in range(3)]

        @block.sync
        def _(sp):
            sp.dma_start(x[:], A["x2"]).then_inc(x_in, 16)
            sp.wait_ge(done, 1)
            sp.dma_start(A["out_y"], x[:]).then_inc(saved, 16)
            sp.wait_ge(saved, 16)

        @block.scalar
        def _(act):
            norm_squares(nc, act, ns, acc, sq)
            norm_roots(nc, act, ns, banks, root, G["eps"])

        @block.tensor
        def _(pe):
            norm_sums(nc, pe, ns, G["ones"], sq, banks)

        @block.vector
        def _(dve):
            step = Steps(dve, own)
            dve.wait_ge(x_in, 16)
            dve.wait_ge(ns["rooted"], 3)
            step(nc.vector.reciprocal(root[:, :], root[:, :]))
            residual(nc, step, x, acc, root, tmp, G["gate"][:, 1])
            dve.sem_inc(done, 1)


def hybrid_decoder(nc, A):
    with Scope(nc, "all") as top:
        G = {"PS": top.ps("PS", [P, 8, 512])}
        for name, shape in (("ones", [P, P]), ("ident", [P, P]), ("iota", [P, NK]), ("eps", [P, 1]), ("one", [P, 1]),
                            ("gain", [P, 2, KD, NC]), ("shift", [P, 2, KD, NC]), ("gate", [P, 2, KD, NC])):
            G[name] = top.sb(name, shape)
        with Scope(nc, "mix") as mix:
            G["h"] = mix.sb("h", [P, KD, T])
            condition_phase(nc, A, G)
            G["ob"] = mix.sb("ob", [P, KD, T])
            heads_phase(nc, A, G)
            G["merged"] = mix.sb("merged", [P, KD, T])
            G["a_in"] = mix.sb("a_in", [P, CC, T])
            conv_phase(nc, A, G)
            merge_phase(nc, A, G)
            out_phase(nc, A, G)
        with Scope(nc, "route") as route:
            G["h_hi"], G["h_lo"] = route.sb("h_hi", [P, KD, T], F32R), route.sb("h_lo", [P, KD, T], F32R)
            G["routeT"] = route.sb("routeT", [P, 3, NT * P])
            with Scope(nc, "lists") as lists:
                G["best"] = lists.sb("best", [P, NT, 2 * PH, TOPK])
                G["place"] = lists.sb("place", [P, NT, 2 * PH, TOPK])
                keys_phase(nc, A, G)
                pick_phase(nc, A, G)
            gates_phase(nc, A, G)
        G["acc"] = top.sb("acc", [P, KD, T])
        experts_phase(nc, A, G)
        final_phase(nc, A, G)


def chunked(a):
    a = np.asarray(a)
    a = a.reshape(a.shape[:-1] + (-1, P))
    return np.ascontiguousarray(np.moveaxis(a, -1, 0))


def blocks_of(w):
    k, n = w.shape
    return np.ascontiguousarray(w.reshape(k // P, P, n // P, P).transpose(2, 1, 0, 3))


def arrange(i):
    i = {k: np.asarray(v) for k, v in i.items()}
    sizes = (D // 2, D // 2, D // 2, H * DK, H * DK, H * DV, H * DV, D, D, RANK)
    cuts = np.cumsum((0,) + sizes)
    part = [i["w_in"][0][:, a:b] for a, b in zip(cuts[:-1], cuts[1:])]
    bg, cg, hin, q, k, v, r, ga, gb = (blocks_of(p) for p in part[:9])
    x = np.concatenate([i["x_prompt"].reshape(SEQ, D), i["x_sample"].reshape(NSEQ * LSEQ, D)]).T
    sums, pairs = chunk_masks()
    seq_rows = (np.arange(TAIL)[:, None] // LSEQ == np.arange(NSEQ)[None, :]).astype(np.float32)
    u = i["peer_u"][0].reshape(NK, NK, KD, P)
    a = {
        "x": x.reshape(KD, P, T),
        "cond": chunked(np.concatenate([i["c_prompt"], i["c_sample"]])).transpose(0, 2, 1),
        "ada_bias": chunked(i["b_ada"][0]),
        "gains": chunked(np.concatenate([i["norm_mix_pre"], i["norm_mix_post"], i["norm_ffn_pre"], i["norm_ffn_post"]])),
        "w_ada": blocks_of(i["w_ada"][0]).reshape(12, 4, P, KD, P).transpose(0, 2, 1, 3, 4),
        "w_low": part[9].reshape(KD, P, RANK).transpose(1, 0, 2),
        "w_alpha": np.concatenate([i["w_alpha"][0], i["b_alpha"]]),
        "gla_norm": chunked(i["gla_norm_w"][0]),
        "seq_rows": seq_rows, "mask_sums": sums, "mask_pairs": pairs,
        "w_heads": np.stack([q, k, v[0::2], v[1::2], r[0::2], r[1::2]], 1),
        "state": i["state_gla"][0].transpose(1, 2, 0, 3),
        "conv_w": chunked(i["conv_w"][0]), "conv_b": chunked(i["conv_b"][0]),
        "conv_state": chunked(i["state_conv"][0]).transpose(0, 3, 1, 2),
        "w_conv": np.stack([cg, hin, bg], 1).reshape(CC // 2, 6, P, KD, P),
        "w_gate_ab": np.stack([ga, gb], 1),
        "w_proj_a": blocks_of(i["w_proj_a"][0]), "w_proj_b": blocks_of(i["w_proj_b"][0]),
        "w_out": blocks_of(i["w_out"][0]), "w_query": blocks_of(i["peer_wq"][0]),
        "subkeys": i["peer_subkeys"][0].reshape(2 * PH, NK, P).transpose(2, 0, 1),
        "u": u.transpose(1, 3, 2, 0),
        "v": i["peer_v"][0].reshape(NK, NSTEP, CP, D).transpose(1, 0, 2, 3),
    }
    return {n: np.ascontiguousarray(v) for n, v in a.items()}


_OUTS = {"out_y": (P, KD, T), "out_conv_p": (P, CC, CW - 1), "out_conv_s": (P, CC, NSEQ, CW - 1),
         "out_gla_p": (H, DK, DV), "out_gla_s": (H, DK, NSEQ, DV)}
_SCRATCH = {"x2": (P, KD, T), "h2": (P, KD, T), "gm": (NGB, P, NK, GB), "hid": (NK, P, T)}


def kernel(**inputs):
    import concourse.bacc as bacc
    from concourse.bass_utils import run_bass_kernel_spmd

    nc = bacc.Bacc("TRN2", target_bir_lowering=False, num_devices=1)
    arrays, A = {}, {}
    for name, a in arrange(inputs).items():
        arrays[f"in_{name}"] = a
        A[name] = nc.dram_tensor(f"in_{name}", a.shape, F32, kind="ExternalInput").ap()
    for name, shape in _OUTS.items():
        A[name] = nc.dram_tensor(name, shape, F32, kind="ExternalOutput").ap()
    for name, shape in _SCRATCH.items():
        A[name] = nc.dram_tensor(f"scratch_{name}", shape, F32, kind="Internal").ap()
    hybrid_decoder(nc, A)
    got = run_bass_kernel_spmd(nc, [arrays], core_ids=[0]).results[0]
    y = got["out_y"].transpose(2, 1, 0).reshape(T, D)
    conv_p = got["out_conv_p"].transpose(2, 1, 0).reshape(1, 1, CW - 1, D // 2)
    conv_s = got["out_conv_s"].transpose(2, 3, 1, 0).reshape(1, NSEQ, CW - 1, D // 2)
    gla_p = got["out_gla_p"].reshape(1, 1, H, DK, DV)
    gla_s = got["out_gla_s"].transpose(2, 0, 1, 3).reshape(1, NSEQ, H, DK, DV)
    return (y[:SEQ].reshape(1, SEQ, D), y[SEQ:].reshape(NSEQ, LSEQ, D), conv_p, gla_p, conv_s, gla_s)
```

```python
import numpy as np
import concourse.bass as bass
from concourse import mybir
from concourse.alu_op_type import AluOpType as ALU
from contextlib import ExitStack

F32 = mybir.dt.float32
F32R = mybir.dt.float32r
U32 = mybir.dt.uint32
ACT = mybir.ActivationFunctionType
AX = mybir.AxisListType

P = 128
D = 1024
KD = D // P
SEQ = 1024
NSEQ, LSEQ = 8, 8
T = SEQ + NSEQ * LSEQ
NC = 1 + NSEQ
NT = -(-T // P)
TAIL = T - (NT - 1) * P
NST = NT - 1 + NSEQ
TB = [(0, 384), (384, 384), (768, 320)]
CC = D // 2 // P
CW = 3
H, DK, DV = 4, 128, 256
RANK = 16
TAU = 16.0
LV = 7
PH, NK, TOPK = 8, 128, 16
HK = PH * TOPK
GB = 64
NGB = T // GB
CP = 4
NSTEP = NK // CP
PICK_CHUNKS = 3
GATE_CHUNKS = 6
EPS = 1e-6
LOWEST = -3.0e38


class Steps:

    def __init__(self, eng, sem, base=0):
        self.eng, self.sem, self.base, self.n = eng, sem, base, 0

    def __call__(self, ins, passed=None):
        self.n += 1
        ins.then_inc(self.sem, 1)
        self.eng.wait_ge(self.sem, self.base + self.n)
        if passed is not None:
            self.eng.sem_inc(passed, 1)


def rows(t):
    return P if t < NT - 1 else TAIL


def per_sequence(ap):
    return ap[:, :, None].broadcast_to([P, NSEQ, LSEQ])


def chunk_masks():
    sums = np.zeros((2, LV + 2, P, P), np.float32)
    pairs = np.zeros((2, LV + 1, P, P), np.float32)
    j, i = np.arange(P)[:, None], np.arange(P)[None, :]
    for kind, (n, size) in enumerate([(P, P), (TAIL, LSEQ)]):
        ok = (j < n) & (i < n)
        for l in range(LV):
            half = 1 << l
            if 2 * half > size:
                continue
            mid = i // (2 * half) * (2 * half) + half
            sums[kind, l] = ok & (((i >= mid) & (j >= mid) & (j <= i)) | ((i < mid) & (j > i) & (j < mid)))
            pairs[kind, l] = ok & (i // (2 * half) == j // (2 * half)) & (i >= mid) & (j < mid)
        start = i // size * size
        sums[kind, LV] = ok & (j >= start) & (j <= i)
        sums[kind, LV + 1] = ok & (j > i) & (j < start + size)
        pairs[kind, LV] = ok & (i == j)
    return sums.transpose(2, 0, 1, 3).copy(), pairs.transpose(2, 0, 1, 3).copy()


class Scope:

    def __init__(self, nc, name):
        self.nc, self.name, self.tensors, self.engines, self.sems = nc, name, ExitStack(), ExitStack(), []

    def __enter__(self):
        return self

    def __exit__(self, *a):
        self.engines.close()
        if self.sems:
            self.nc.clear_and_free_semaphores(self.sems)
            self.nc.all_engine_barrier()
        self.tensors.close()

    def sb(self, name, shape, dt=F32):
        return self.tensors.enter_context(self.nc.sbuf_tensor(f"{self.name}_{name}", shape, dt))

    def ps(self, name, shape):
        return self.tensors.enter_context(self.nc.psum_tensor(f"{self.name}_{name}", shape, F32))

    def sem(self, name):
        self.sems.append(self.nc.alloc_semaphore(f"{self.name}_{name}"))
        return self.sems[-1]

    def block(self):
        return self.engines.enter_context(self.nc.Block())


def project3(nc, banks, w_hi, w_lo, rhs_hi, rhs_lo, nk):
    for bank, (t0, n) in zip(banks, TB):
        for k in range(nk):
            hi, lo = rhs_hi[:, k, t0:t0 + n], rhs_lo[:, k, t0:t0 + n]
            nc.tensor.matmul(bank[:, 0:n], w_hi[:, k, :], hi, start=(k == 0), stop=False)
            nc.tensor.matmul(bank[:, 0:n], w_hi[:, k, :], lo, start=False, stop=False)
            last = nc.tensor.matmul(bank[:, 0:n], w_lo[:, k, :], hi, start=False, stop=(k == nk - 1))
        yield last


def split(nc, pool, hi, lo, raw, high, low, count):
    nc.gpsimd.tensor_copy(hi, raw).then_inc(high, 1)
    pool.wait_ge(high, count)
    nc.gpsimd.tensor_tensor(lo, raw, hi.bitcast(F32), ALU.subtract).then_inc(low, 1)


def norm_squares(nc, act, s, src, sq, ready=None):
    for k in range(KD):
        if ready is not None:
            act.wait_ge(ready, k + 1)
        if k >= 2:
            act.wait_ge(s["summed"], k - 1)
        nc.scalar.activation(sq[:, k % 2, :], src[:, k, :], ACT.Square).then_inc(s["squared"], 1)


def norm_sums(nc, pe, s, ones, sq, banks):
    for k in range(KD):
        pe.wait_ge(s["squared"], k + 1)
        for bank, (t0, n) in zip(banks, TB):
            last = nc.tensor.matmul(bank[:, 0:n], ones[:, :], sq[:, k % 2, t0:t0 + n],
                                    start=(k == 0), stop=(k == KD - 1))
        last.then_inc(s["summed"], 1)


def norm_roots(nc, act, s, banks, root, eps, width=D, base=0):
    for bank, (t0, n) in zip(banks, TB):
        nc.scalar.activation(root[:, t0:t0 + n], bank[:, 0:n], ACT.Ln, bias=eps[:, 0:1],
                             scale=1.0 / width).then_inc(s["logged"], 1)
    act.wait_ge(s["logged"], base + len(TB))
    nc.scalar.activation(root[:, :], root[:, :], ACT.Exp, scale=-0.5).then_inc(s["rooted"], 1)


def norm_sems(sc, tag=""):
    return {n: sc.sem(tag + n) for n in ("squared", "summed", "logged", "rooted")}


def modulate(nc, step, out, src, rstd, tmp, gain, shift, done):
    for k in range(KD):
        if k >= 1:
            step.eng.wait_ge(done, k)
        step(nc.vector.tensor_tensor(tmp[:, :], src[:, k, :], rstd[:, :], ALU.mult))
        nc.vector.tensor_scalar(out[:, k, 0:SEQ], tmp[:, 0:SEQ], gain[:, k, 0:1], shift[:, k, 0:1],
                                ALU.mult, ALU.add)
        tail = tmp[:, SEQ:T].rearrange("p (s t) -> p s t", s=NSEQ)
        otail = out[:, k, SEQ:T].rearrange("p (s t) -> p s t", s=NSEQ)
        step(nc.vector.tensor_tensor(tail, tail, per_sequence(gain[:, k, 1:NC]), ALU.mult))
        nc.vector.tensor_tensor(otail, tail, per_sequence(shift[:, k, 1:NC]), ALU.add).then_inc(done, 1)


def residual(nc, step, x, m, rstd, tmp, gain, done):
    for k in range(KD):
        if k >= 1:
            step.eng.wait_ge(done, k)
        step(nc.vector.tensor_tensor(tmp[:, :], m[:, k, :], rstd[:, :], ALU.mult))
        tail = tmp[:, SEQ:T].rearrange("p (s t) -> p s t", s=NSEQ)
        step(nc.vector.tensor_tensor(tail, tail, per_sequence(gain[:, k, 1:NC]), ALU.mult))
        step(nc.vector.scalar_tensor_tensor(out=x[:, k, 0:SEQ], in0=tmp[:, 0:SEQ], scalar=gain[:, k, 0:1],
                                            in1=x[:, k, 0:SEQ], op0=ALU.mult, op1=ALU.add))
        nc.vector.tensor_tensor(x[:, k, SEQ:T], x[:, k, SEQ:T], tmp[:, SEQ:T], ALU.add).then_inc(done, 1)


def condition_phase(nc, A, G):
    with Scope(nc, "cond") as sc:
        WN = 512
        NL = 6 * D // WN
        NBUF = 3
        h_hi, h_lo = G["h_hi"], G["h_lo"]
        x = sc.sb("x", [P, KD, T])
        w = sc.sb("w", [P, NBUF, KD, WN])
        c = sc.sb("c", [P, KD, NC])
        sc_c = sc.sb("silu_c", [P, KD, NC])
        rows_mod = sc.sb("rows_mod", [NC, 2, WN])
        mod = sc.sb("mod", [P, 6 * KD, NC])
        bias = sc.sb("bias", [P, 6 * KD])
        gains = sc.sb("gains", [P, 4, KD])
        sq = sc.sb("sq", [P, 2, T])
        root = sc.sb("root", [P, T])
        tmp = sc.sb("tmp", [P, T])
        small_in, x_in, w_in = sc.sem("small_in"), sc.sem("x_in"), [sc.sem(f"w_in{b}") for b in range(NBUF)]
        sig, silu, w_used, r_out, t_mm, mod_out, own, ready, done, high, low = (sc.sem(n) for n in (
            "sig silu w_used r_out t_mm mod_out own ready done high low").split())
        ns = norm_sems(sc)
        PS = G["PS"]
        block = sc.block()
        NF = WN // P

        @block.sync
        def _(sp):
            for dst, src in ((c, A["cond"]), (bias, A["ada_bias"]), (gains, A["gains"])):
                sp.dma_start(dst[:], src).then_inc(small_in, 16)
            for n in range(NL):
                if n >= NBUF:
                    sp.wait_ge(w_used, n - NBUF + 1)
                sp.dma_start(w[:, n % NBUF], A["w_ada"][n]).then_inc(w_in[n % NBUF], 16)
                if n < KD:
                    sp.dma_start(x[:, n, :], A["x"][n]).then_inc(x_in, 16)

        @block.gpsimd
        def _(pool):
            nc.gpsimd.memset(G["ones"][:, :], 1.0).then_inc(ready, 1)
            nc.gpsimd.memset(G["eps"][:, :], EPS).then_inc(ready, 1)
            nc.gpsimd.memset(G["one"][:, :], 1.0).then_inc(ready, 1)
            nc.gpsimd.memset(G["ident"][:, :], 0.0).then_inc(ready, 1)
            pool.wait_ge(ready, 4)
            nc.gpsimd.affine_select(out=G["ident"][:, :], in_=G["ident"][:, :], compare_op=ALU.not_equal,
                                    fill=1.0, base=0, pattern=[[-1, P]], channel_multiplier=1).then_inc(ready, 1)
            nc.gpsimd.iota(G["iota"][:, :], [[1, P]], base=0, channel_multiplier=0,
                           allow_small_or_imprecise_dtypes=True).then_inc(ready, 1)

        @block.scalar
        def _(act):
            act.wait_ge(small_in, 48)
            nc.scalar.activation(sc_c[:], c[:], ACT.Sigmoid).then_inc(sig, 1)
            for n in range(NL):
                act.wait_ge(w_used, n + 1)
                if n >= 2:
                    act.wait_ge(t_mm, n - 1)
                nc.scalar.activation(rows_mod[:, n % 2, :], PS[0:NC, n % 2, 0:WN], ACT.Copy).then_inc(r_out, 1)
            act.wait_ge(x_in, 16 * KD)
            norm_squares(nc, act, ns, x, sq)
            act.wait_ge(ready, 6)
            act.wait_ge(ns["summed"], KD)
            norm_roots(nc, act, ns, [PS[:, b] for b in (4, 5, 6)], root, G["eps"])
            for k in range(KD):
                act.wait_ge(done, k + 1)
                nc.scalar.activation(h_hi[:, k, :], x[:, k, :], ACT.Copy).then_inc(high, 1)

        @block.tensor
        def _(pe):
            pe.wait_ge(ready, 6)
            pe.wait_ge(silu, 1)

            def transposes(n):
                pe.wait_ge(r_out, n + 1)
                if n >= 2:
                    pe.wait_ge(mod_out, n - 1)
                for f in range(NF):
                    last = nc.tensor.transpose(PS[:, 2 + n % 2, f * NC:(f + 1) * NC],
                                               rows_mod[:, n % 2, f * P:(f + 1) * P], G["ident"][0:NC, 0:NC])
                last.then_inc(t_mm, 1)
            for n in range(NL):
                pe.wait_ge(w_in[n % NBUF], 16 * (n // NBUF) + 16)
                if n >= 2:
                    pe.wait_ge(r_out, n - 1)
                for k in range(KD):
                    last = nc.tensor.matmul(PS[0:NC, n % 2, 0:WN], sc_c[:, k, :], w[:, n % NBUF, k, :],
                                            start=(k == 0), stop=(k == KD - 1))
                last.then_inc(w_used, 1)
                if n:
                    transposes(n - 1)
            transposes(NL - 1)
            norm_sums(nc, pe, ns, G["ones"], sq, [PS[:, b] for b in (4, 5, 6)])

        @block.vector
        def _(dve):
            step = Steps(dve, own)
            dve.wait_ge(sig, 1)
            nc.vector.tensor_tensor(sc_c[:], sc_c[:], c[:], ALU.mult).then_inc(silu, 1)
            dve.wait_ge(small_in, 48)
            for n in range(NL):
                dve.wait_ge(t_mm, n + 1)
                nc.vector.tensor_tensor(mod[:, n * NF:(n + 1) * NF, :],
                                        PS[:, 2 + n % 2, 0:NF * NC].rearrange("p (b c) -> p b c", c=NC),
                                        bias[:, n * NF:(n + 1) * NF][:, :, None].broadcast_to([P, NF, NC]),
                                        ALU.add).then_inc(mod_out, 1)
            dve.wait_ge(mod_out, NL)
            for n, (shift, scale, gate) in enumerate(((0, 1, 2), (3, 4, 5))):
                seg = lambda q: mod[:, q * KD:(q + 1) * KD, :]
                g = lambda q: gains[:, q, :][:, :, None].broadcast_to([P, KD, NC])
                step(nc.vector.scalar_tensor_tensor(out=G["gain"][:, n], in0=seg(scale), scalar=1.0, in1=g(2 * n),
                                                    op0=ALU.add, op1=ALU.mult))
                step(nc.vector.tensor_tensor(G["gate"][:, n], seg(gate), g(2 * n + 1), ALU.mult))
                step(nc.vector.tensor_copy(G["shift"][:, n], seg(shift)))
            dve.wait_ge(ns["rooted"], 1)
            modulate(nc, step, x, x, root, tmp, G["gain"][:, 0], G["shift"][:, 0], done)
            for k in range(KD):
                dve.wait_ge(high, k + 1)
                nc.vector.tensor_tensor(h_lo[:, k, :], x[:, k, :], h_hi[:, k, :].bitcast(F32), ALU.subtract)


def heads_phase(nc, A, G):
    with Scope(nc, "gla") as sc:
        NW = 6
        NSLOT = 4
        SLOT = (0, 1, 2, 3, 0, 1)
        h_hi, h_lo, PS = G["h_hi"], G["h_lo"], G["PS"]
        w = sc.sb("w", [P, 2, KD, P])
        w_hi, w_lo = sc.sb("w_hi", [P, NSLOT, KD, P], F32R), sc.sb("w_lo", [P, NSLOT, KD, P], F32R)
        w_low = sc.sb("w_low", [P, KD, RANK])
        lw_hi, lw_lo = sc.sb("lw_hi", [P, KD, RANK], F32R), sc.sb("lw_lo", [P, KD, RANK], F32R)
        low = sc.sb("low", [RANK + 1, NT * P])
        w_alpha = sc.sb("w_alpha", [RANK + 1, H * DK])
        gnorm = sc.sb("gnorm", [P, 2 * H])
        q, k = sc.sb("q", [P, T]), sc.sb("k", [P, T])
        v = sc.sb("v", [P, NT, DV])
        g = sc.sb("g", [P, NT, DK])
        soft = sc.sb("soft", [P, NT, DK])
        r = sc.sb("r", [P, 2, T])
        o = sc.sb("o", [P, 2, T])
        E = sc.sb("E", [P, 2, LV + 2, P])
        Q, K = sc.sb("Q", [P, LV, P]), sc.sb("K", [P, LV + 1, P])
        Qc = sc.sb("Qc", [P, 2, P])
        sT = sc.sb("sT", [P, P])
        kT = sc.sb("kT", [P, P])
        seq_rows = sc.sb("seq_rows", [TAIL, NSEQ])
        S = sc.sb("S", [P, DV])
        Ss = sc.sb("Ss", [P, NSEQ, DV])
        sums, pairs = sc.sb("sums", [P, LV + 2, P]), sc.sb("pairs", [P, LV + 1, P])
        sums_s, pairs_s = sc.sb("sums_s", [TAIL, LV + 2, TAIL]), sc.sb("pairs_s", [TAIL, LV + 1, TAIL])
        SUMS, PAIRS = (sums, sums_s), (pairs, pairs_s)
        prod = soft[:, 0:LV + 1, :]
        kTs = E[0:TAIL, 1, 0:NSEQ, :]
        sg = v[:].rearrange("p t e -> p (t e)")[:, 0:2 * T].rearrange("p (e t) -> p e t", e=2)
        flat = soft[:].rearrange("p t d -> p (t d)")[:, 0:T]
        names = ("small_in low_ready low_mm q_mm k_mm q_out k_out z_mm z_min z_abs g_ready v_mm v_out r_mm r_out r_sig "
                 "e_mm e_exp qk s_mm s_red t_mm t_out o_mm o_out st_mm st_out kts st_in st_saved st_free "
                 "sq_ready sums own act_own scaled normed o_free ob_saved high low_part passed lw_high lw_low "
                 "logged rooted").split()
        M = {n: sc.sem(n) for n in names}
        w_in = [sc.sem(f"w_in{b}") for b in range(2)]
        block = sc.block()
        bank = lambda b: PS[:, b]
        tiles = [(t, rows(t), 0 if t < NT - 1 else 1) for t in range(NT)]
        assert NT % 2

        @block.sync
        def _(sp):
            sp.sem_inc(M["st_free"], 1)
            sp.sem_inc(M["o_free"], 1)
            for dst, src in ((w_low, A["w_low"]), (w_alpha, A["w_alpha"]), (gnorm, A["gla_norm"]),
                             (seq_rows, A["seq_rows"]), (sums, A["mask_sums"][:, 0]), (pairs, A["mask_pairs"][:, 0]),
                             (sums_s, A["mask_sums"][0:TAIL, 1, :, 0:TAIL]),
                             (pairs_s, A["mask_pairs"][0:TAIL, 1, :, 0:TAIL])):
                sp.dma_start(dst[:], src).then_inc(M["small_in"], 16)

            def bring(i, b):
                sp.dma_start(w[:, b % 2], A["w_heads"][i, b]).then_inc(w_in[b % 2], 16)
            for b in range(2):
                bring(0, b)
            for b in range(2, NW):
                sp.wait_ge(M["low_part"], b - 1)
                bring(0, b)
            sp.dma_start(Ss[:], A["state"][0]).then_inc(M["st_in"], 16)

            def put(i):
                sp.wait_ge(M["st_out"], NST * (i + 1))
                sp.dma_start(A["out_gla_p"][i], S[:]).then_inc(M["st_saved"], 16)
                sp.dma_start(A["out_gla_s"][i], Ss[:]).then_inc(M["st_saved"], 16)
                sp.wait_ge(M["st_saved"], 32 * (i + 1))
                sp.sem_inc(M["st_free"], 1)
                sp.wait_ge(M["normed"], 2 * (i + 1))
                sp.dma_start(A["ob"][i], o[:]).then_inc(M["ob_saved"], 16)
            with sp.Fori(1, H) as i:
                for b in range(2):
                    sp.wait_ge(M["low_part"], NW * i + b - 1)
                    bring(i, b)
                put(i - 1)
                sp.dma_start(Ss[:], A["state"][i]).then_inc(M["st_in"], 16)
                for b in range(2, NW):
                    sp.wait_ge(M["low_part"], NW * i + b - 1)
                    bring(i, b)
                sp.wait_ge(M["ob_saved"], 16 * i)
                sp.sem_inc(M["o_free"], 1)
            put(H - 1)
            sp.wait_ge(M["ob_saved"], 16 * H)

        @block.gpsimd
        def _(pool):
            pool.wait_ge(M["small_in"], 128)
            split(nc, pool, lw_hi[:], lw_lo[:], w_low[:], M["lw_high"], M["lw_low"], 1)
            with pool.Fori(0, H) as i:
                for b in range(NW):
                    pool.wait_ge(w_in[b % 2], 16 * (NW // 2 * i + b // 2) + 16)
                    if b < 2:
                        pool.wait_ge(M["r_mm"], 6 * i + 3 * b + 3)
                    elif b < 4:
                        pool.wait_ge(M["v_mm"], NT * i + NT)
                    else:
                        pool.wait_ge((M["q_mm"], M["k_mm"])[b - 4], 3 * i + 3)
                    pool.sem_inc(M["passed"], 1)
                    split(nc, pool, w_hi[:, SLOT[b]], w_lo[:, SLOT[b]], w[:, b % 2], M["high"], M["low_part"], NW * i + b + 1)

        @block.tensor
        def _(pe):
            pe.sem_inc(M["r_mm"], 6)
            pe.sem_inc(M["v_mm"], NT)
            pe.wait_ge(M["lw_low"], 1)
            for b, (t0, n) in enumerate(TB):
                for kk in range(KD):
                    hi, lo = h_hi[:, kk, t0:t0 + n], h_lo[:, kk, t0:t0 + n]
                    nc.tensor.matmul(PS[0:RANK, b, 0:n], lw_hi[:, kk, :], hi, start=(kk == 0), stop=False)
                    nc.tensor.matmul(PS[0:RANK, b, 0:n], lw_hi[:, kk, :], lo, start=False, stop=False)
                    last = nc.tensor.matmul(PS[0:RANK, b, 0:n], lw_lo[:, kk, :], hi, start=False, stop=(kk == KD - 1))
            last.then_inc(M["low_mm"], 1)
            pe.wait_ge(M["low_ready"], 1)
            with pe.Fori(0, H) as i:
                pe.wait_ge(M["low_part"], NW * i + 1)
                for last in project3(nc, [bank(0), bank(1), bank(2)], w_hi[:, 0], w_lo[:, 0], h_hi, h_lo, KD):
                    last.then_inc(M["q_mm"], 1)
                pe.wait_ge(M["low_part"], NW * i + 2)
                pe.wait_ge(M["rooted"], i + 1)
                for last in project3(nc, [bank(3), bank(4), bank(5)], w_hi[:, 1], w_lo[:, 1], h_hi, h_lo, KD):
                    last.then_inc(M["k_mm"], 1)
                pe.wait_ge(M["q_out"], 3 * i + 3)
                for t, n, _ in tiles:
                    last = nc.tensor.matmul(PS[:, t // 4, t % 4 * DK:(t % 4 + 1) * DK],
                                            low[:, t * P:(t + 1) * P], w_alpha[:, bass.ds(i * DK, DK)],
                                            start=True, stop=True)
                last.then_inc(M["z_mm"], 1)
                pe.wait_ge(M["low_part"], NW * i + 4)
                pe.wait_ge(M["k_out"], 3 * i + 3)
                for t, n, _ in tiles:
                    if t >= 3:
                        pe.wait_ge(M["v_out"], NT * i + t - 2)
                    out = PS[0:n, 3 + t % 3, 0:DV]
                    for kk in range(KD):
                        hi, lo = h_hi[:, kk, t * P:t * P + n], h_lo[:, kk, t * P:t * P + n]
                        nc.tensor.matmul(out, hi, w_hi[:, 2:4, kk, :], start=(kk == 0), stop=False)
                        nc.tensor.matmul(out, hi, w_lo[:, 2:4, kk, :], start=False, stop=False)
                        last = nc.tensor.matmul(out, lo, w_hi[:, 2:4, kk, :], start=False, stop=(kk == KD - 1))
                    last.then_inc(M["v_mm"], 1)
                pe.wait_ge(M["z_abs"], 2 * i + 2)
                for b in range(2):
                    pe.wait_ge(M["low_part"], NW * i + 5 + b)
                    if b:
                        pe.wait_ge(M["v_out"], NT * i + NT)
                    for last in project3(nc, [bank(3 * b), bank(3 * b + 1), bank(3 * b + 2)], w_hi[:, b], w_lo[:, b],
                                         h_hi, h_lo, KD):
                        last.then_inc(M["r_mm"], 1)
                pe.wait_ge(M["r_out"], 6 * i + 6)
                pe.wait_ge(M["g_ready"], 2 * i + 2)

                def exponents(t, n, kind):
                    if t >= 1:
                        pe.wait_ge(M["e_exp"], NT * i + t)
                    for b in range(3):
                        last = nc.tensor.matmul(PS[:, b, 0:384].rearrange("p (l i) -> p l i", l=3)[:, :, 0:n],
                                                g[0:n, t, :], SUMS[kind][0:n, 3 * b:3 * b + 3, 0:n],
                                                start=True, stop=True)
                    last.then_inc(M["e_mm"], 1)

                exponents(*tiles[0])
                for t, n, kind in tiles:
                    if t + 1 < NT:
                        exponents(*tiles[t + 1])
                    pe.wait_ge(M["qk"], 3 * (NT * i + t) + 3)
                    if t >= 1:
                        pe.wait_ge(M["s_red"], NT * i + t)
                        pe.wait_ge(M["t_out"], NT * i + t)
                    nc.tensor.transpose(PS[:, 5, 0:DK], K[:, LV, :], G["ident"][:, :]).then_inc(M["t_mm"], 1)
                    for l in range(LV + 1):
                        lhs = K[:, l, 0:n] if l < LV else k[:, t * P:t * P + n]
                        rhs = Q[:, l, 0:n] if l < LV else q[:, t * P:t * P + n]
                        last = nc.tensor.matmul(PS[0:n, 3 + l // 4, l % 4 * P:l % 4 * P + n], lhs, rhs,
                                                start=True, stop=True)
                    last.then_inc(M["s_mm"], 1)
                    if t < NT - 1:
                        pe.wait_ge(M["t_out"], NT * i + t + 1)
                        if t >= 1:
                            pe.wait_ge(M["st_out"], NST * i + t)
                            pe.wait_ge(M["o_out"], NT * i + t)
                        for e in range(2) if t >= 1 else ():
                            nc.tensor.matmul(PS[:, 6, e * P:e * P + n], S[:, e * P:(e + 1) * P], Qc[:, t % 2, 0:n],
                                             start=(e == 0), stop=False, skip_group_check=True)
                        nc.tensor.matmul(PS[:, 7, 0:DV], kT[0:n, :], v[0:n, t, :],
                                         start=True, stop=True).then_inc(M["st_mm"], 1)
                        pe.wait_ge(M["s_red"], NT * i + t + 1)
                        for e in range(2):
                            last = nc.tensor.matmul(PS[:, 6, e * P:e * P + n], v[0:n, t, e * P:(e + 1) * P],
                                                    sT[0:n, 0:n], start=(t == 0 and e == 0), stop=True,
                                                    skip_group_check=True)
                        last.then_inc(M["o_mm"], 1)
                    else:
                        pe.wait_ge(M["s_red"], NT * i + t + 1)
                        pe.wait_ge(M["o_out"], NT * i + t)
                        pe.wait_ge(M["st_in"], 16 * i + 16)
                        for e in range(2):
                            last = nc.tensor.matmul(PS[:, 6, e * P:e * P + n], v[0:n, t, e * P:(e + 1) * P],
                                                    sT[0:n, 0:n], start=True, stop=False)
                            for s in range(NSEQ):
                                last = nc.tensor.matmul(PS[:, 6, e * P + s * LSEQ:e * P + (s + 1) * LSEQ],
                                                        Ss[:, s, e * P:(e + 1) * P],
                                                        Qc[:, t % 2, s * LSEQ:(s + 1) * LSEQ],
                                                        start=False, stop=(s == NSEQ - 1))
                        last.then_inc(M["o_mm"], 1)
                        pe.wait_ge(M["kts"], i + 1)
                        for s in range(NSEQ):
                            pe.wait_ge(M["st_out"], NST * i + NT - 1 + max(s - 1, 0))
                            nc.tensor.matmul(PS[:, 7 if s % 2 else 4, 0:DV], kTs[:, s, :], v[0:n, t, :],
                                             start=True, stop=True).then_inc(M["st_mm"], 1)
                pe.wait_ge(M["sq_ready"], i + 1)
                pe.wait_ge(M["st_out"], NST * (i + 1))
                for b, (t0, n) in enumerate(TB):
                    for e, src in enumerate((q, k)):
                        last = nc.tensor.matmul(PS[:, 3 + b, 0:n], G["ones"][:, :], src[:, t0:t0 + n],
                                                start=(e == 0), stop=(e == 1))
                last.then_inc(M["sums"], 1)

        @block.scalar
        def _(act):
            act.sem_inc(M["rooted"], 1)
            with act.Fori(0, H) as i:
                for b, (t0, n) in enumerate(TB):
                    act.wait_ge(M["q_mm"], 3 * i + 1 + b)
                    nc.scalar.activation(q[:, t0:t0 + n], PS[:, b, 0:n], ACT.Copy,
                                         scale=float(DK) ** -0.5).then_inc(M["q_out"], 1)
                steps = Steps(act, M["act_own"], 4 * i)
                act.wait_ge(M["z_min"], 2 * i + 2)
                full = PS[:, 0:2, :].rearrange("p b (t d) -> p (b t) d", d=DK)
                nc.scalar.activation(soft[:, 0:NT - 1, :], full, ACT.Abs).then_inc(M["z_abs"], 1)
                nc.scalar.activation(soft[0:TAIL, NT - 1, :], PS[0:TAIL, 2, 0:DK], ACT.Abs).then_inc(M["z_abs"], 1)
                act.wait_ge(M["z_abs"], 2 * i + 2)
                for part in (soft[:, 0:NT - 1, :], soft[0:TAIL, NT - 1, :]):
                    steps(nc.scalar.activation(part, part, ACT.Exp, scale=-1.0))
                for n, part in ((P, soft[:, 0:NT - 1, :]), (TAIL, soft[0:TAIL, NT - 1, :])):
                    steps(nc.scalar.activation(part, part, ACT.Ln, bias=G["one"][0:n, 0:1]))
                for t, n, _ in tiles:
                    act.wait_ge(M["v_mm"], NT * i + t + 1 + NT)
                    nc.scalar.activation(v[0:n, t, :], PS[0:n, 3 + t % 3, 0:DV], ACT.Copy).then_inc(M["v_out"], 1)
                for b in range(6):
                    act.wait_ge(M["r_mm"], 6 * i + b + 1 + 6)
                    t0, n = TB[b % 3]
                    nc.scalar.activation(r[:, b // 3, t0:t0 + n], PS[:, b, 0:n], ACT.Copy).then_inc(M["r_out"], 1)

                def exps(t, n, kind):
                    act.wait_ge(M["e_mm"], NT * i + t + 1)
                    if t >= 2:
                        act.wait_ge(M["st_out"], NST * i + t - 1)
                    src = PS[:, 0:3, 0:384].rearrange("p b (l i) -> p b l i", l=3)[:, :, :, 0:n]
                    dst = E[:, t % 2].rearrange("p (b l) i -> p b l i", l=3)[:, :, :, 0:n]
                    nc.scalar.activation(dst, src, ACT.Exp).then_inc(M["e_exp"], 1)
                exps(*tiles[0])
                for t, n, kind in tiles:
                    if t + 1 < NT:
                        exps(*tiles[t + 1])
                    act.wait_ge(M["t_mm"], NT * i + t + 1)
                    if t >= 1:
                        act.wait_ge(M["st_mm"], NST * i + t)
                    nc.scalar.activation(kT[0:n, :], PS[0:n, 5, 0:DK], ACT.Copy).then_inc(M["t_out"], 1)
                    act.wait_ge(M["o_mm"], NT * i + t + 1)
                    if t == 0:
                        act.wait_ge(M["o_free"], i + 1)
                    nc.scalar.activation(o[:, :, t * P:t * P + n],
                                         PS[:, 6, 0:2 * P].rearrange("p (e i) -> p e i", e=2)[:, :, 0:n],
                                         ACT.Copy).then_inc(M["o_out"], 1)
                act.wait_ge(M["o_out"], NT * i + NT)
                nc.scalar.activation(q[:, :], o[:, 0, :], ACT.Square)
                nc.scalar.activation(k[:, :], o[:, 1, :], ACT.Square).then_inc(M["sq_ready"], 1)
                act.wait_ge(M["sums"], i + 1)
                norm_roots(nc, act, {"logged": M["logged"], "rooted": M["rooted"]}, [bank(3), bank(4), bank(5)], flat,
                           G["eps"], DV, 3 * i)
                act.wait_ge(M["st_mm"], NST * (i + 1))
                nc.scalar.activation(sg, r[:], ACT.Sigmoid).then_inc(M["r_sig"], 1)

        @block.vector
        def _(dve):
            dve.wait_ge(M["small_in"], 128)
            nc.vector.memset(low[:, :], 1.0).then_inc(M["own"], 1)
            dve.wait_ge(M["own"], 1)
            dve.wait_ge(M["low_mm"], 1)
            for b, (t0, n) in enumerate(TB):
                last = nc.vector.tensor_copy(low[0:RANK, t0:t0 + n], PS[0:RANK, b, 0:n])
            last.then_inc(M["low_ready"], 1)
            OWN = NT + 4
            with dve.Fori(0, H) as i:
                step = Steps(dve, M["own"], OWN * i + 1)
                for b, (t0, n) in enumerate(TB):
                    dve.wait_ge(M["k_mm"], 3 * i + 1 + b)
                    nc.vector.tensor_copy(k[:, t0:t0 + n], PS[:, 3 + b, 0:n]).then_inc(M["k_out"], 1)
                dve.wait_ge(M["z_mm"], i + 1)
                full = PS[:, 0:2, :].rearrange("p b (t d) -> p (b t) d", d=DK)
                nc.vector.tensor_scalar(g[:, 0:NT - 1, :], full, 0.0, 1.0 / TAU, ALU.min, ALU.mult).then_inc(M["z_min"], 1)
                nc.vector.tensor_scalar(g[0:TAIL, NT - 1, :], PS[0:TAIL, 2, 0:DK], 0.0, 1.0 / TAU,
                                        ALU.min, ALU.mult).then_inc(M["z_min"], 1)
                dve.wait_ge(M["z_min"], 2 * i + 2)
                dve.wait_ge(M["act_own"], 4 * i + 4)
                for gg, ss in ((g[:, 0:NT - 1, :], soft[:, 0:NT - 1, :]), (g[0:TAIL, NT - 1, :], soft[0:TAIL, NT - 1, :])):
                    nc.vector.scalar_tensor_tensor(out=gg, in0=ss, scalar=-1.0 / TAU, in1=gg, op0=ALU.mult,
                                                   op1=ALU.add).then_inc(M["g_ready"], 1)

                def decay(t, n, kind):
                    tok, Et = slice(t * P, t * P + n), E[:, t % 2]
                    dve.wait_ge(M["e_exp"], NT * i + t + 1)
                    nc.vector.tensor_tensor(Q[:, :, 0:n], Et[:, 0:LV, 0:n],
                                            q[:, None, tok].broadcast_to([P, LV, n]), ALU.mult).then_inc(M["qk"], 1)
                    nc.vector.tensor_tensor(K[:, 0:LV, 0:n], Et[:, 0:LV, 0:n],
                                            k[:, None, tok].broadcast_to([P, LV, n]), ALU.mult).then_inc(M["qk"], 1)
                    nc.vector.tensor_tensor(Qc[:, t % 2, 0:n], Et[:, LV, 0:n], q[:, tok], ALU.mult)
                    nc.vector.tensor_tensor(K[:, LV, 0:n], Et[:, LV + 1, 0:n], k[:, tok], ALU.mult).then_inc(M["qk"], 1)
                decay(*tiles[0])
                for t, n, kind in tiles:
                    Et = E[:, t % 2]
                    dve.wait_ge(M["s_mm"], NT * i + t + 1)
                    if t + 1 < NT:
                        if t >= 1:
                            dve.wait_ge(M["o_mm"], NT * i + t)
                        decay(*tiles[t + 1])
                    step(nc.vector.tensor_tensor(prod[0:n, :, 0:n],
                                                 PS[0:n, 3:5, :].rearrange("p b (l i) -> p (b l) i", i=P)[:, :, 0:n],
                                                 PAIRS[kind][0:n, :, 0:n], ALU.mult))
                    if t >= 1:
                        dve.wait_ge(M["o_mm"], NT * i + t)
                    nc.vector.tensor_reduce(sT[0:n, 0:n], prod[0:n, :, 0:n].rearrange("p l i -> p i l"), AX.X,
                                            ALU.add).then_inc(M["s_red"], 1)
                    if t < NT - 1:
                        dve.wait_ge(M["st_mm"], NST * i + t + 1)
                        if t == 0:
                            dve.wait_ge(M["st_free"], i + 1)
                            nc.vector.tensor_copy(S[:, :], PS[:, 7, 0:DV]).then_inc(M["st_out"], 1)
                        else:
                            dve.wait_ge(M["st_out"], NST * i + t)
                            nc.vector.scalar_tensor_tensor(out=S[:, :], in0=S[:, :], scalar=Et[:, LV, n - 1:n],
                                                           in1=PS[:, 7, 0:DV], op0=ALU.mult,
                                                           op1=ALU.add).then_inc(M["st_out"], 1)
                    else:
                        dve.wait_ge(M["t_out"], NT * i + NT)
                        dve.wait_ge(M["st_out"], NST * i + NT - 1)
                        nc.vector.tensor_tensor(kTs, kT[0:n, None, :].broadcast_to([n, NSEQ, DK]),
                                                seq_rows[:, :, None].broadcast_to([n, NSEQ, DK]),
                                                ALU.mult).then_inc(M["kts"], 1)
                        for s in range(NSEQ):
                            dve.wait_ge(M["st_mm"], NST * i + NT + s)
                            nc.vector.scalar_tensor_tensor(out=Ss[:, s, :], in0=Ss[:, s, :],
                                                           scalar=Et[:, LV, (s + 1) * LSEQ - 1:(s + 1) * LSEQ],
                                                           in1=PS[:, 7 if s % 2 else 4, 0:DV], op0=ALU.mult,
                                                           op1=ALU.add).then_inc(M["st_out"], 1)
                dve.wait_ge(M["rooted"], i + 2)
                for e in range(2):
                    step(nc.vector.tensor_tensor(o[:, e, :], o[:, e, :], flat, ALU.mult))
                dve.wait_ge(M["r_sig"], i + 1)
                for e in range(2):
                    step(nc.vector.tensor_tensor(r[:, e, :], r[:, e, :], sg[:, e, :], ALU.mult))
                    nc.vector.scalar_tensor_tensor(out=o[:, e, :], in0=o[:, e, :], scalar=gnorm[:, bass.ds(2 * i + e, 1)],
                                                   in1=r[:, e, :], op0=ALU.mult, op1=ALU.mult).then_inc(M["normed"], 1)
                assert step.n == OWN


class Weights:

    def __init__(self, sc, blocks, used, sources):
        self.n, self.used, self.sources = blocks, used, sources
        self.raw = sc.sb("w", [P, blocks, KD, P])
        self.hi, self.lo = sc.sb("w_hi", [P, blocks, KD, P], F32R), sc.sb("w_lo", [P, blocks, KD, P], F32R)
        self.high, self.low, self.passed = sc.sem("w_high"), sc.sem("w_low"), sc.sem("w_passed")
        self.landed = [sc.sem(f"w_in{b}") for b in range(blocks)]

    def bring(self, sp, steps):
        def step(i, later=True):
            for b, src in enumerate(self.sources):
                if later:
                    sp.wait_ge(self.low, self.n * (i - 1) + b + 1)
                nk = src(0).shape[1]
                sp.dma_start(self.raw[:, b, 0:nk], src(i)).then_inc(self.landed[b], 16)
        step(0, later=False)
        with sp.Fori(1, steps) as i:
            step(i)

    def split(self, nc, pool, steps):
        def step(i, later=True):
            for b, src in enumerate(self.sources):
                nk = src(0).shape[1]
                pool.wait_ge(self.landed[b], 16 * i + 16)
                if later:
                    sem, first, more = self.used(b)
                    pool.wait_ge(sem, more * (i - 1) + first)
                pool.sem_inc(self.passed, 1)
                split(nc, pool, self.hi[:, b, 0:nk], self.lo[:, b, 0:nk], self.raw[:, b, 0:nk], self.high, self.low,
                      self.n * i + b + 1)
        step(0, later=False)
        with pool.Fori(1, steps) as i:
            step(i)

    def project(self, nc, pe, i, b, banks, rhs_hi, rhs_lo, nk=KD):
        pe.wait_ge(self.low, self.n * i + b + 1)
        return project3(nc, banks, self.hi[:, b], self.lo[:, b], rhs_hi, rhs_lo, nk)


def split_inputs(nc, sc, tag, hi, lo, raw, source, chunks):
    landed = [sc.sem(f"{tag}_in{b}") for b in range(2)]
    high, low = sc.sem(f"{tag}_high"), sc.sem(f"{tag}_low")

    def fetch(sp):
        for k in range(chunks):
            if k >= 2:
                sp.wait_ge(low, k - 1)
            sp.dma_start(raw[:, k % 2, :], source(k)).then_inc(landed[k % 2], 16)

    def highs(act):
        for k in range(chunks):
            act.wait_ge(landed[k % 2], 16 * (k // 2) + 16)
            nc.scalar.activation(hi[:, k, :], raw[:, k % 2, :], ACT.Copy).then_inc(high, 1)

    def lows(dve):
        for k in range(chunks):
            dve.wait_ge(high, k + 1)
            nc.vector.tensor_tensor(lo[:, k, :], raw[:, k % 2, :], hi[:, k, :].bitcast(F32), ALU.subtract).then_inc(low, 1)
    return fetch, highs, lows, low


def conv_phase(nc, A, G):
    with Scope(nc, "conv") as sc:
        NB = 6
        PS = G["PS"]
        cg, bg, y = (sc.sb(n, [P, T]) for n in ("cg", "bg", "y"))
        a_in = sc.sb("a_in", [P, CC, T])
        up = sc.sb("up", [P, CW - 1 + SEQ])
        us = sc.sb("us", [P, NSEQ, CW - 1 + LSEQ])
        taps, cbias = sc.sb("taps", [P, CW, CC]), sc.sb("cbias", [P, CC])
        past = sc.sb("past", [P, CC, NSEQ, CW - 1])
        last_p, last_s = sc.sb("last_p", [P, CC, CW - 1]), sc.sb("last_s", [P, CC, NSEQ, CW - 1])
        small_in, c_mm, h_mm, b_mm, c_out, u_out, b_out, conv_out, own, saved = (sc.sem(n) for n in (
            "small_in c_mm h_mm b_mm c_out u_out b_out conv_out own saved").split())
        w = Weights(sc, 3, lambda b: ((c_mm, h_mm, b_mm)[b], 3, 3), [lambda i, b=b: A["w_conv"][i, b] for b in range(3)])
        block = sc.block()
        sets = lambda n: [PS[:, 3 * (n % 2) + b] for b in range(3)]
        OPS = 3 + 2 * CW

        @block.sync
        def _(sp):
            for dst, src in ((taps, A["conv_w"]), (cbias, A["conv_b"]), (past, A["conv_state"])):
                sp.dma_start(dst[:], src).then_inc(small_in, 16)
            w.bring(sp, CC)
            sp.wait_ge(conv_out, CC + 1)
            sp.dma_start(A["out_conv_p"], last_p[:]).then_inc(saved, 16)
            sp.dma_start(A["out_conv_s"], last_s[:]).then_inc(saved, 16)
            sp.dma_start(A["a_in"], a_in[:]).then_inc(saved, 16)
            sp.wait_ge(saved, 48)

        @block.gpsimd
        def _(pool):
            w.split(nc, pool, CC)

        @block.tensor
        def _(pe):
            with pe.Fori(0, CC // 2) as i:
                for n in range(NB):
                    c, kind = n // 3, n % 3
                    if kind == 0:
                        pe.wait_ge(u_out, 6 * i + 3 * c + 3)
                    elif kind == 1:
                        pe.wait_ge(b_out, 6 * i + 3 * c + 3)
                    else:
                        pe.wait_ge(c_out, 6 * i + 3 * c + 3)
                    for last in w.project(nc, pe, 2 * i + c, kind, sets(n), G["h_hi"], G["h_lo"]):
                        last.then_inc((c_mm, h_mm, b_mm)[kind], 1)

        @block.scalar
        def _(act):
            act.sem_inc(b_out, 3)
            with act.Fori(0, CC // 2) as i:
                for n in (0, 2, 3, 5):
                    c = n // 3
                    mm, out, dst = (c_mm, c_out, cg) if n % 3 == 0 else (b_mm, b_out, bg)
                    if n % 3 == 0:
                        act.wait_ge(u_out, 6 * i + 3 * c + 3)
                    else:
                        act.wait_ge(conv_out, 2 * i + c + 1)
                    for b, (t0, m) in enumerate(TB):
                        act.wait_ge(mm, 6 * i + 3 * c + b + 1)
                        nc.scalar.activation(dst[:, t0:t0 + m], sets(n)[b][:, 0:m], ACT.Copy).then_inc(out, 1)

        @block.vector
        def _(dve):
            dve.sem_inc(u_out, 3)
            dve.sem_inc(conv_out, 1)
            dve.wait_ge(small_in, 48)
            step = Steps(dve, own)
            step(nc.vector.memset(up[:, 0:CW - 1], 0.0))
            with dve.Fori(0, CC // 2) as i:
                step = Steps(dve, own, 2 * OPS * i + 1)
                for c in range(2):
                    ch = bass.ds(2 * i + c, 1)
                    step(nc.vector.tensor_copy(us[:, :, 0:CW - 1], past[:, ch].rearrange("p a s w -> p (a s) w")))
                    for b, (t0, m) in enumerate(TB):
                        dve.wait_ge(h_mm, 6 * i + 3 * c + b + 1)
                        dve.wait_ge(c_out, 6 * i + 3 * c + b + 1)
                        src = sets(3 * c + 1)[b]
                        n = min(m, SEQ - t0)
                        ins = nc.vector.tensor_tensor(up[:, CW - 1 + t0:CW - 1 + t0 + n], src[:, 0:n],
                                                      cg[:, t0:t0 + n], ALU.mult)
                        if n < m:
                            ins = nc.vector.tensor_tensor(us[:, :, CW - 1:], src[:, n:m].rearrange("p (s t) -> p s t", s=NSEQ),
                                                          cg[:, SEQ:T].rearrange("p (s t) -> p s t", s=NSEQ), ALU.mult)
                        ins.then_inc(u_out, 1)
                    dve.wait_ge(u_out, 6 * i + 3 * c + 6)
                    ys = y[:, SEQ:T].rearrange("p (s t) -> p s t", s=NSEQ)
                    tap = lambda n: taps[:, n, ch]
                    step(nc.vector.tensor_copy(last_p[:, ch].rearrange("p a w -> p (a w)"), up[:, SEQ:]))
                    step(nc.vector.tensor_copy(last_s[:, ch].rearrange("p a s w -> p (a s) w"), us[:, :, LSEQ:]))
                    for full, out, n in ((up, y[:, 0:SEQ], SEQ), (us, ys, LSEQ)):
                        at = lambda q: full[:, q:q + n] if full is up else full[:, :, q:q + n]
                        step(nc.vector.tensor_scalar(out, at(CW - 1), tap(CW - 1), cbias[:, ch], ALU.mult, ALU.add))
                        for q in range(CW - 1):
                            step(nc.vector.scalar_tensor_tensor(out=out, in0=at(q), scalar=tap(q), in1=out,
                                                                op0=ALU.mult, op1=ALU.add))
                    dve.wait_ge(b_out, 6 * i + 3 * c + 6)
                    nc.vector.tensor_tensor(a_in[:, ch].rearrange("p a t -> p (a t)"), y[:, :], bg[:, :],
                                            ALU.mult).then_inc(conv_out, 1)
                    dve.wait_ge(conv_out, 2 * i + c + 2)
                    assert step.n == OPS * (c + 1)


def gate_phase(nc, A, G):
    with Scope(nc, "side") as sc:
        PS = G["PS"]
        sig = sc.sb("sig", [P, 2, 2, T])
        mm, out, free = (sc.sem(n) for n in "mm out free".split())
        saved = [sc.sem(f"saved{b}") for b in range(2)]
        w = Weights(sc, 2, lambda b: (mm, 3 * b + 3, 6), [lambda i, b=b: A["w_gate_ab"][i, b] for b in range(2)])
        block = sc.block()
        sets = lambda n: [PS[:, 3 * n + b] for b in range(3)]

        @block.sync
        def _(sp):
            w.bring(sp, KD)

        @block.gpsimd
        def _(pool):
            w.split(nc, pool, KD)

        @block.tensor
        def _(pe):
            with pe.Fori(0, KD) as i:
                for n in range(2):
                    pe.wait_ge(out, 6 * i + 3 * n + 3)
                    for last in w.project(nc, pe, i, n, sets(n), G["h_hi"], G["h_lo"]):
                        last.then_inc(mm, 1)

        @block.scalar
        def _(act):
            act.sem_inc(out, 6)
            with act.Fori(0, KD // 2) as i:
                for par in range(2):
                    for n in range(2):
                        for b, (t0, m) in enumerate(TB):
                            act.wait_ge(mm, 12 * i + 6 * par + 3 * n + b + 1)
                            if n == 0 and b == 0:
                                act.wait_ge(free, 2 * i + par + 1)
                            nc.scalar.activation(sig[:, par, n, t0:t0 + m], sets(n)[b][:, 0:m], ACT.Sigmoid).then_inc(out, 1)
                    act.wait_ge(out, 12 * i + 6 * par + 12)
                    act.dma_start(A["sig"][2 * i + par], sig[:, par]).then_inc(saved[par], 16)

        @block.vector
        def _(dve):
            dve.sem_inc(free, 2)
            with dve.Fori(0, KD // 2) as i:
                for par in range(2):
                    dve.wait_ge(saved[par], 16 * i + 16)
                    dve.sem_inc(free, 1)


def merge_phase(nc, A, G):
    with Scope(nc, "merge") as sc:
        PS, merged = G["PS"], G["merged"]
        raw = sc.sb("raw", [P, 2, T])
        a_hi, a_lo = sc.sb("a_hi", [P, CC, T], F32R), sc.sb("a_lo", [P, CC, T], F32R)
        b_hi, b_lo = sc.sb("b_hi", [P, KD, T], F32R), sc.sb("b_lo", [P, KD, T], F32R)
        sig = sc.sb("sig", [P, 2, T])
        parts = sc.sb("parts", [P, 2, T])
        mm, part, done = (sc.sem(n) for n in "mm part done".split())
        sig_in = sc.sem("sig_in")
        w = Weights(sc, 2, lambda b: (mm, 3 * b + 3, 6), [lambda i: A["w_proj_a"][i], lambda i: A["w_proj_b"][i]])
        fetch, highs, lows, low = split_inputs(
            nc, sc, "x", _Joined(a_hi, b_hi, CC), _Joined(a_lo, b_lo, CC), raw,
            lambda k: A["a_in"][:, k, :] if k < CC else A["ob"][(k - CC) // 2, :, (k - CC) % 2, :], CC + KD)
        block = sc.block()
        sets = lambda n: [PS[:, 3 * n + b] for b in range(3)]

        @block.sync
        def _(sp):
            fetch(sp)
            w.bring(sp, KD)

        @block.gpsimd
        def _(pool):
            w.split(nc, pool, KD)

        @block.tensor
        def _(pe):
            pe.wait_ge(low, CC + KD)
            with pe.Fori(0, KD) as i:
                for n, (x_hi, x_lo, nk) in enumerate(((a_hi, a_lo, CC), (b_hi, b_lo, KD))):
                    pe.wait_ge(part, 6 * i + 3 * n + 3)
                    for last in w.project(nc, pe, i, n, sets(n), x_hi, x_lo, nk):
                        last.then_inc(mm, 1)

        @block.scalar
        def _(act):
            highs(act)
            with act.Fori(0, KD) as i:
                act.wait_ge(part, 6 * i + 6)
                act.dma_start(sig[:], A["sig"][i]).then_inc(sig_in, 16)

        @block.vector
        def _(dve):
            dve.sem_inc(part, 6)
            lows(dve)
            with dve.Fori(0, KD) as i:
                dve.wait_ge(sig_in, 16 * i + 16)
                for n in range(2):
                    for b, (t0, m) in enumerate(TB):
                        dve.wait_ge(mm, 6 * i + 3 * n + b + 1)
                        nc.vector.tensor_tensor(parts[:, n, t0:t0 + m], sets(n)[b][:, 0:m], sig[:, n, t0:t0 + m],
                                                ALU.mult).then_inc(part, 1)
                dve.wait_ge(part, 6 * i + 12)
                nc.vector.tensor_tensor(merged[:, bass.ds(i, 1)].rearrange("p a t -> p (a t)"), parts[:, 0, :], parts[:, 1, :],
                                        ALU.add).then_inc(done, 1)
                dve.wait_ge(done, i + 1)


class _Joined:

    def __init__(self, first, second, n):
        self.first, self.second, self.n = first, second, n

    def __getitem__(self, at):
        p, k, t = at
        return self.first[p, k, t] if k < self.n else self.second[p, k - self.n, t]


def out_phase(nc, A, G):
    with Scope(nc, "out") as sc:
        NB = 2
        PS, merged = G["PS"], G["merged"]
        x = merged
        m = sc.sb("m", [P, KD, T])
        m_hi, m_lo = sc.sb("m_hi", [P, KD, T], F32R), sc.sb("m_lo", [P, KD, T], F32R)
        sq = sc.sb("sq", [P, 2, T])
        root, tmp = sc.sb("root", [P, T]), sc.sb("tmp", [P, T])
        x_in, mm, m_out, own, saved, high, low = (sc.sem(n) for n in "x_in mm m_out own saved high low".split())
        x2_done, h2_done = sc.sem("x2_done"), sc.sem("h2_done")
        n1, n2 = norm_sems(sc, "post_"), norm_sems(sc, "pre_")
        w = Weights(sc, NB, lambda b: (mm, 3 * b + 3, 3 * NB), [lambda i, b=b: A["w_out"][2 * i + b] for b in range(NB)])
        block = sc.block()
        sets = lambda n: [PS[:, 3 * (n % 2) + b] for b in range(3)]

        @block.sync
        def _(sp):
            w.bring(sp, KD // NB)
            for k in range(KD):
                sp.wait_ge(low, k + 1)
                sp.dma_start(x[:, k, :], A["x"][k]).then_inc(x_in, 16)
            for k in range(KD):
                sp.wait_ge(x2_done, k + 1)
                sp.dma_start(A["x2"][:, k, :], x[:, k, :]).then_inc(saved, 16)
            for k in range(KD):
                sp.wait_ge(h2_done, k + 1)
                sp.dma_start(A["h2"][:, k, :], m[:, k, :]).then_inc(saved, 16)
            sp.wait_ge(saved, 32 * KD)

        @block.gpsimd
        def _(pool):
            w.split(nc, pool, KD // NB)

        @block.tensor
        def _(pe):
            pe.wait_ge(low, KD)
            with pe.Fori(0, KD // NB) as i:
                for n in range(NB):
                    pe.wait_ge(m_out, 6 * i + 3 * n + 3)
                    for last in w.project(nc, pe, i, n, sets(n), m_hi, m_lo):
                        last.then_inc(mm, 1)
            pe.wait_ge(m_out, 6 + 3 * KD)
            norm_sums(nc, pe, n1, G["ones"], sq, sets(0))
            norm_sums(nc, pe, n2, G["ones"], sq, sets(1))

        @block.scalar
        def _(act):
            act.sem_inc(m_out, 6)
            for k in range(KD):
                nc.scalar.activation(m_hi[:, k, :], merged[:, k, :], ACT.Copy).then_inc(high, 1)
            with act.Fori(0, KD // NB) as i:
                for n in range(NB):
                    for b, (t0, q) in enumerate(TB):
                        act.wait_ge(mm, 6 * i + 3 * n + b + 1)
                        nc.scalar.activation(m[:, bass.ds(2 * i + n, 1), t0:t0 + q].rearrange("p a t -> p (a t)"),
                                             sets(n)[b][:, 0:q], ACT.Copy).then_inc(m_out, 1)
            act.wait_ge(m_out, 6 + 3 * KD)
            norm_squares(nc, act, n1, m, sq)
            act.wait_ge(n1["summed"], KD)
            norm_roots(nc, act, n1, sets(0), root, G["eps"])
            norm_squares(nc, act, n2, x, sq, x2_done)
            act.wait_ge(n2["summed"], KD)
            norm_roots(nc, act, n2, sets(1), root, G["eps"])

        @block.vector
        def _(dve):
            step = Steps(dve, own)
            for k in range(KD):
                dve.wait_ge(high, k + 1)
                nc.vector.tensor_tensor(m_lo[:, k, :], merged[:, k, :], m_hi[:, k, :].bitcast(F32),
                                        ALU.subtract).then_inc(low, 1)
            dve.wait_ge(x_in, 16 * KD)
            dve.wait_ge(n1["rooted"], 1)
            residual(nc, step, x, m, root, tmp, G["gate"][:, 0], x2_done)
            dve.wait_ge(n2["rooted"], 1)
            modulate(nc, step, m, x, root, tmp, G["gain"][:, 1], G["shift"][:, 1], h2_done)


def stream_weights(sp, steps, w, w_in, used, sources):
    for b, src in enumerate(sources):
        sp.dma_start(w[:, b, 0:src(0).shape[1]], src(0)).then_inc(w_in[b], 16)
    with sp.Fori(1, steps) as i:
        for b, src in enumerate(sources):
            mm, first, more = used(b)
            sp.wait_ge(mm, more * (i - 1) + first)
            sp.dma_start(w[:, b, 0:src(0).shape[1]], src(i)).then_inc(w_in[b], 16)


def keys_phase(nc, A, G):
    with Scope(nc, "keys") as sc:
        NB = 2
        PS = G["PS"]
        h_hi, h_lo = G["h_hi"], G["h_lo"]
        h2 = sc.sb("h2", [P, KD, T])
        w = sc.sb("w", [P, NB, KD, P])
        w_hi, w_lo = sc.sb("w_hi", [P, NB, KD, P], F32R), sc.sb("w_lo", [P, NB, KD, P], F32R)
        sub = sc.sb("sub", [P, 2 * PH, NK])
        qT = sc.sb("qT", [P, NB, T])
        s1 = sc.sb("s1", [P, NB, NT, NK])
        s2 = sc.sb("s2", [P, NT, NK])
        best, place = sc.sb("best", [P, NT, TOPK]), sc.sb("place", [P, NT, TOPK], U32)
        w_in = [sc.sem(f"w_in{b}") for b in range(NB)]
        h_in = [sc.sem(f"h_in{k}") for k in range(KD)]
        sub_in, q_mm, q_out, s_mm, s_out, own, listed, passed, high, low, h_high, h_low, q_free, passed_pool = (sc.sem(n) for n in (
            "sub_in q_mm q_out s_mm s_out own listed passed high low h_high h_low q_free passed_pool").split())
        block = sc.block()
        sets = lambda n: [PS[:, 3 * (n % 2) + b] for b in range(3)]
        SB = ((6, 0), (1, 3))
        pairbank = lambda n: (PS[:, 6:8, :], PS[:, 1:3, :])[n].rearrange("p b (t d) -> p (b t) d", d=NK)
        lone = lambda n: PS[0:TAIL, (0, 3)[n], 0:NK]
        OPS = 5

        @block.sync
        def _(sp):
            for k in range(KD):
                sp.dma_start(h2[:, k, :], A["h2"][:, k, :]).then_inc(h_in[k], 16)
            sp.dma_start(sub[:], A["subkeys"]).then_inc(sub_in, 16)
            stream_weights(sp, PH, w, w_in, lambda b: (low, b + 1, NB), [lambda i, b=b: A["w_query"][2 * i + b] for b in range(NB)])

        @block.tensor
        def _(pe):
            pe.wait_ge(h_low, KD)
            pe.wait_ge(sub_in, 16)
            with pe.Fori(0, PH) as i:
                for n in range(NB):
                    pe.wait_ge(low, NB * i + n + 1)
                    pe.wait_ge(s_out, 4 * i + 4)
                    for last in project3(nc, sets(n), w_hi[:, n], w_lo[:, n], h_hi, h_lo, KD):
                        last.then_inc(q_mm, 1)
                for n in range(NB):
                    pe.wait_ge(q_out, 6 * i + (3, 6)[n])
                    for t in range(NT):
                        out = pairbank(n)[:, t, :] if t < NT - 1 else lone(n)
                        last = nc.tensor.matmul(out, qT[:, n, t * P:t * P + rows(t)],
                                                sub[:, bass.ds(2 * i + n, 1), :].rearrange("p a k -> p (a k)"),
                                                start=True, stop=True)
                    last.then_inc(s_mm, 1)

        @block.gpsimd
        def _(pool):
            with pool.Fori(0, PH) as i:
                for n in range(NB):
                    pool.wait_ge(w_in[n], 16 * i + 16)
                    pool.wait_ge(q_free, NB * i + n + 1)
                    pool.sem_inc(passed_pool, 1)
                    split(nc, pool, w_hi[:, n], w_lo[:, n], w[:, n], high, low, NB * i + n + 1)

        @block.scalar
        def _(act):
            act.sem_inc(s_out, 4)
            act.sem_inc(q_free, 2)
            for k in range(KD):
                act.wait_ge(h_in[k], 16)
                nc.scalar.activation(h_hi[:, k, :], h2[:, k, :], ACT.Copy).then_inc(h_high, 1)
            with act.Fori(0, PH) as i:
                for n in range(NB):
                    for b, (t0, m) in enumerate(TB):
                        act.wait_ge(q_mm, 6 * i + 3 * n + b + 1)
                        nc.scalar.activation(qT[:, n, t0:t0 + m], sets(n)[b][:, 0:m], ACT.Copy).then_inc(q_out, 1)
                    act.sem_inc(q_free, 1)
                for n in range(NB):
                    act.wait_ge(s_mm, 2 * i + n + 1)
                    act.wait_ge(listed, 2 * i + n + 1)
                    nc.scalar.activation(s1[:, n, 0:NT - 1, :], pairbank(n), ACT.Copy).then_inc(s_out, 1)
                    nc.scalar.activation(s1[0:TAIL, n, NT - 1, :], lone(n), ACT.Copy).then_inc(s_out, 1)

        @block.vector
        def _(dve):
            dve.sem_inc(listed, 2)
            step = Steps(dve, own)
            step(nc.vector.memset(G["best"][:], 0.0))
            step(nc.vector.memset(G["place"][:], 0.0))
            for k in range(KD):
                dve.wait_ge(h_high, k + 1)
                nc.vector.tensor_tensor(h_lo[:, k, :], h2[:, k, :], h_hi[:, k, :].bitcast(F32),
                                        ALU.subtract).then_inc(h_low, 1)
            with dve.Fori(0, PH) as i:
                for n in range(NB):
                    step = Steps(dve, own, OPS * (NB * i + n) + 2)
                    dve.wait_ge(s_out, 4 * i + 2 * n + 6)
                    dve.sem_inc(passed, 1)
                    for t in range(NT):
                        last = nc.vector.max(best[0:rows(t), t, 0:8], s1[0:rows(t), n, t, :])
                    step(last, passed)
                    for t in range(NT):
                        nc.vector.max_index(place[0:rows(t), t, 0:8], best[0:rows(t), t, 0:8], s1[0:rows(t), n, t, :])
                        last = nc.vector.match_replace(s2[0:rows(t), t, :], best[0:rows(t), t, 0:8],
                                                       s1[0:rows(t), n, t, :], LOWEST)
                    step(last, passed)
                    for t in range(NT):
                        last = nc.vector.max(best[0:rows(t), t, 8:16], s2[0:rows(t), t, :])
                    step(last, passed)
                    for t in range(NT):
                        last = nc.vector.max_index(place[0:rows(t), t, 8:16], best[0:rows(t), t, 8:16], s2[0:rows(t), t, :])
                    step(last)
                    side = bass.ds(2 * i + n, 1)
                    for dst, src in ((G["best"], best), (G["place"], place)):
                        last = nc.vector.tensor_copy(dst[:, 0:NT - 1, side, :].rearrange("p t a k -> p t (a k)"), src[:, 0:NT - 1, :])
                        last = nc.vector.tensor_copy(dst[0:TAIL, NT - 1, side, :].rearrange("p a k -> p (a k)"), src[0:TAIL, NT - 1, :])
                    step(last)
                    dve.sem_inc(listed, 1)


class Hidden:

    def __init__(self, sc, A, G, slots, banks, first):
        self.A, self.G, self.slots, self.banks, self.first, self.PS = A, G, slots, banks, first, G["PS"]
        self.u = sc.sb("u", [P, slots, KD, P])
        self.hi, self.lo = sc.sb("u_hi", [P, slots, KD, P], F32R), sc.sb("u_lo", [P, slots, KD, P], F32R)
        self.ge = sc.sb("ge", [P, slots, T])
        names = "u_in u_high u_low u_mm ge_out u_passed ge_free hid_saved".split()
        (_, self.high, self.low, self.mm, self.out, self.passed, self.free, _) = (sc.sem(n) for n in names)
        self.u_in = [sc.sem(f"u_in_{b}") for b in range(slots)]
        self.saved = [sc.sem(f"saved_{b}") for b in range(slots)]

    def bring(self, sp, n, slot, turn, reuse=True):
        if reuse:
            sp.wait_ge(self.low, n - self.slots + 1)
        sp.dma_start(self.u[:, slot], self.A["u"][self.first + n]).then_inc(self.u_in[slot], 16)

    def split(self, nc, pool, n, slot, turn):
        pool.wait_ge(self.u_in[slot], 16 * turn + 16)
        pool.wait_ge(self.out, 3 * n + 3)
        pool.sem_inc(self.passed, 1)
        split(nc, pool, self.hi[:, slot], self.lo[:, slot], self.u[:, slot], self.high, self.low, n + 1)

    def multiply(self, nc, pe, n, slot, b):
        t0, m = TB[b]
        if b == 0:
            pe.wait_ge(self.low, n + 1)
        pe.wait_ge(self.out, 3 * n + b + 3 * self.slots - len(self.banks) + 1)
        out, h_hi, h_lo = self.PS[:, self.banks[b], 0:m], self.G["h_hi"], self.G["h_lo"]
        for k in range(KD):
            hi, lo = h_hi[:, k, t0:t0 + m], h_lo[:, k, t0:t0 + m]
            nc.tensor.matmul(out, self.hi[:, slot, k, :], hi, start=(k == 0), stop=False)
            nc.tensor.matmul(out, self.hi[:, slot, k, :], lo, start=False, stop=False)
            last = nc.tensor.matmul(out, self.lo[:, slot, k, :], hi, start=False, stop=(k == KD - 1))
        last.then_inc(self.mm, 1)

    def gelu(self, nc, act, n, slot, b):
        t0, m = TB[b]
        if b == 0:
            act.wait_ge(self.free, n + 1)
        act.wait_ge(self.mm, 3 * n + b + 1)
        nc.scalar.activation(self.ge[:, slot, t0:t0 + m], self.PS[:, self.banks[b], 0:m],
                             ACT.Gelu_apprx_tanh).then_inc(self.out, 1)

    def credits(self, act, sp):
        if act is not None:
            act.sem_inc(self.out, 3 * self.slots)
        if sp is not None:
            sp.sem_inc(self.free, self.slots)

    def put(self, sp, n, slot):
        sp.wait_ge(self.out, 3 * n + 3 + 3 * self.slots)
        sp.dma_start(self.A["hid"][self.first + n], self.ge[:, slot]).then_inc(self.saved[slot], 16)

    def landed(self, sp, slot, turn):
        sp.wait_ge(self.saved[slot], 16 * turn + 16)
        sp.sem_inc(self.free, 1)


def pick_phase(nc, A, G):
    with Scope(nc, "pick") as sc:
        PS = G["PS"]
        sums = sc.sb("sums", [P, PH, TOPK * TOPK])
        sums2 = sc.sb("sums2", [P, PH, TOPK * TOPK])
        top, at = sc.sb("top", [P, PH, TOPK]), sc.sb("at", [P, PH, TOPK], U32)
        half = [sc.sb(f"half{s}", [P, HK], U32) for s in range(2)]
        halff = [sc.sb(f"halff{s}", [P, HK]) for s in range(2)]
        eq = [sc.sb(f"eq{s}", [P, HK, TOPK]) for s in range(2)]
        route = sc.sb("route", [P, 3, HK])
        diff, total = sc.sb("diff", [P, PH, TOPK]), sc.sb("total", [P, PH])
        own, t_mm, t_out, d_out, e_out, passed = (sc.sem(n) for n in "own t_mm t_out d_out e_out passed".split())
        NS = PICK_CHUNKS
        hid = Hidden(sc, A, G, NS, (1, 2, 3), 0)
        block = sc.block()
        OPS = 18

        def tiles(eng, body):
            with eng.Fori(0, NT - 1) as i:
                body(i, NS)
            body(NT - 1, NS - 1)

        @block.sync
        def _(sp):
            hid.credits(None, sp)
            for c in range(NS):
                hid.bring(sp, c, c, 0, reuse=False)

            def move(i, chunks):
                if chunks == NS:
                    for c in range(NS - 1):
                        hid.bring(sp, NS * (i + 1) + c, c, None)
                for c in range(chunks):
                    hid.put(sp, NS * i + c, c)
                    if c == 0 and chunks == NS:
                        pass
                if chunks == NS:
                    hid.bring(sp, NS * (i + 1) + NS - 1, NS - 1, None)
                for c in range(chunks):
                    hid.landed(sp, c, i)
            tiles(sp, move)

        @block.gpsimd
        def _(pool):
            def parts(i, chunks):
                for c in range(chunks):
                    hid.split(nc, pool, NS * i + c, c, i)
            tiles(pool, parts)

        @block.tensor
        def _(pe):
            def work(i, chunks):
                for c in range(chunks):
                    for b in range(len(TB)):
                        hid.multiply(nc, pe, NS * i + c, c, b)
                pe.wait_ge(own, OPS * i + OPS)
                pe.wait_ge(t_out, i + 1)
                for n in range(3):
                    last = nc.tensor.transpose(PS[:, 0, n * P:(n + 1) * P], route[:, n, :], G["ident"][:, :])
                last.then_inc(t_mm, 1)
            tiles(pe, work)

        @block.scalar
        def _(act):
            act.sem_inc(t_out, 1)
            hid.credits(act, None)

            def work(i, chunks):
                for c in range(chunks):
                    for b in range(len(TB)):
                        hid.gelu(nc, act, NS * i + c, c, b)
                    if c == 1:
                        act.wait_ge(d_out, i + 1)
                        nc.scalar.activation(diff[:], diff[:], ACT.Exp).then_inc(e_out, 1)
                act.wait_ge(t_mm, i + 1)
                nc.scalar.activation(G["routeT"][:, :, bass.ds(i * P, P)],
                                     PS[:, 0, 0:3 * P].rearrange("p (n t) -> p n t", n=3), ACT.Copy).then_inc(t_out, 1)
            tiles(act, work)

        @block.vector
        def _(dve):
            with dve.Fori(0, NT) as i:
                step = Steps(dve, own, OPS * i)
                sv = G["best"][:, bass.ds(i, 1)].rearrange("p a (h s) k -> p (a h) s k", s=2)
                si = G["place"][:, bass.ds(i, 1)].rearrange("p a (h s) k -> p (a h) s k", s=2)
                step(nc.vector.tensor_tensor(sums[:].rearrange("p h (a b) -> p h a b", a=TOPK),
                                             sv[:, :, 0, :, None].broadcast_to([P, PH, TOPK, TOPK]),
                                             sv[:, :, 1, None, :].broadcast_to([P, PH, TOPK, TOPK]), ALU.add), passed)
                for hh in range(PH):
                    last = nc.vector.max(top[:, hh, 0:8], sums[:, hh, :])
                step(last, passed)
                for hh in range(PH):
                    nc.vector.max_index(at[:, hh, 0:8], top[:, hh, 0:8], sums[:, hh, :])
                    last = nc.vector.match_replace(sums2[:, hh, :], top[:, hh, 0:8], sums[:, hh, :], LOWEST)
                step(last, passed)
                for hh in range(PH):
                    last = nc.vector.max(top[:, hh, 8:16], sums2[:, hh, :])
                step(last, passed)
                for hh in range(PH):
                    last = nc.vector.max_index(at[:, hh, 8:16], top[:, hh, 8:16], sums2[:, hh, :])
                step(last)
                nc.vector.tensor_tensor(diff[:], top[:], top[:, :, 0:1].broadcast_to([P, PH, TOPK]),
                                        ALU.subtract).then_inc(d_out, 1)
                atf = at[:].rearrange("p h k -> p (h k)")
                step(nc.vector.tensor_scalar(half[0][:, :], atf, 4, None, ALU.logical_shift_right))
                step(nc.vector.tensor_scalar(half[1][:, :], atf, TOPK - 1, None, ALU.bitwise_and))
                for n in range(2):
                    step(nc.vector.tensor_copy(halff[n][:, :], half[n][:, :]))
                for n in range(2):
                    step(nc.vector.tensor_tensor(eq[n][:], halff[n][:, :, None].broadcast_to([P, HK, TOPK]),
                                                 G["iota"][:, None, 0:TOPK].broadcast_to([P, HK, TOPK]), ALU.is_equal))
                    e4 = eq[n][:].rearrange("p (h k) a -> p h k a", h=PH)
                    step(nc.vector.tensor_tensor(e4, e4, si[:, :, n, None, :].broadcast_to([P, PH, TOPK, TOPK]), ALU.mult))
                dve.wait_ge(t_out, i + 1)
                for n in range(2):
                    step(nc.vector.tensor_reduce(route[:, n, :], eq[n][:], AX.X, ALU.add))
                dve.wait_ge(e_out, i + 1)
                step(nc.vector.tensor_reduce(total[:, :], diff[:], AX.X, ALU.add))
                step(nc.vector.reciprocal(total[:, :], total[:, :]))
                step(nc.vector.tensor_tensor(route[:, 2, :].rearrange("p (h k) -> p h k", h=PH), diff[:],
                                             total[:, :, None].broadcast_to([P, PH, TOPK]), ALU.mult))
                assert step.n == OPS


def gates_phase(nc, A, G):
    with Scope(nc, "gates") as sc:
        PS, routeT = G["PS"], G["routeT"]
        NG, TG = 4, 4
        hot_i, hot_j = sc.sb("hot_i", [P, NG, TG, NK]), sc.sb("hot_j", [P, NG, TG, NK])
        part = sc.sb("part", [P, 2, 3, GB])
        gm = sc.sb("gm", [P, 2, NK, GB])
        hot, mm, out, saved, gm_free, own = (sc.sem(n) for n in "hot mm out saved gm_free own".split())
        NB = 4
        hid = Hidden(sc, A, G, 2, (4, 5, 6), PICK_CHUNKS * NT - 1)
        block = sc.block()
        PER = GB // TG
        units = [(c, b) for c in range(GATE_CHUNKS) for b in range(len(TB))]
        after = [units[len(units) * g // PER:len(units) * (g + 1) // PER] for g in range(PER)]
        assert PICK_CHUNKS * NT - 1 + GATE_CHUNKS * NGB == NK

        def blocks(eng, body):
            with eng.Fori(0, NGB // 2) as i:
                for b in range(2):
                    body(2 * i + b, b)
            assert NGB % 2
            body(NGB - 1, 0, True)

        @block.sync
        def _(sp):
            sp.sem_inc(gm_free, 2)
            hid.credits(None, sp)
            for c in range(2):
                hid.bring(sp, c, c, None, reuse=False)

            def move(blk, b, last=False):
                for c in range(GATE_CHUNKS):
                    n = GATE_CHUNKS * blk + c
                    if not (last and c >= GATE_CHUNKS - 2):
                        hid.bring(sp, n + 2, c % 2, None)
                    hid.put(sp, n, c % 2)
                    hid.landed(sp, c % 2, GATE_CHUNKS // 2 * blk + c // 2)
                sp.wait_ge(out, PER * blk + PER + NB)
                sp.dma_start(A["gm"][blk], gm[:, b]).then_inc(saved, 16)
                sp.wait_ge(saved, 16 * blk + 16)
                sp.sem_inc(gm_free, 1)
            blocks(sp, move)

        @block.gpsimd
        def _(pool):
            def parts(blk, b, last=False):
                for c in range(GATE_CHUNKS):
                    hid.split(nc, pool, GATE_CHUNKS * blk + c, c % 2, GATE_CHUNKS // 2 * blk + c // 2)
            blocks(pool, parts)

        @block.vector
        def _(dve):
            def build(blk, b, last=False):
                nc.vector.tensor_copy(part[:, b], routeT[:, :, bass.ds(blk * GB, GB)]).then_inc(own, 1)
                dve.wait_ge(own, blk + 1)
                for g in range(PER):
                    dve.wait_ge(mm, PER * blk + g + 1)
                    for t in range(TG):
                        at = g * TG + t
                        nc.vector.tensor_scalar(hot_i[:, g % NG, t, :], G["iota"][:, :], part[:, b, 0, at:at + 1],
                                                None, ALU.is_equal)
                        last = nc.vector.tensor_scalar(hot_j[:, g % NG, t, :], G["iota"][:, :],
                                                       part[:, b, 1, at:at + 1], part[:, b, 2, at:at + 1],
                                                       ALU.is_equal, ALU.mult)
                    last.then_inc(hot, 1)
            blocks(dve, build)

        @block.tensor
        def _(pe):
            pe.sem_inc(mm, NG)
            def multiply(blk, b, last=False):
                for g in range(PER):
                    pe.wait_ge(hot, PER * blk + g + 1)
                    pe.wait_ge(out, PER * blk + g + 1)
                    for t in range(TG):
                        last = nc.tensor.matmul(PS[:, g % NB, t * NK:(t + 1) * NK], hot_i[:, g % NG, t, :],
                                                hot_j[:, g % NG, t, :], start=True, stop=True)
                    last.then_inc(mm, 1)
                    for c, q in after[g]:
                        hid.multiply(nc, pe, GATE_CHUNKS * blk + c, c % 2, q)
            blocks(pe, multiply)

        @block.scalar
        def _(act):
            act.sem_inc(out, NB)
            hid.credits(act, None)

            def empty(blk, b, last=False):
                act.wait_ge(gm_free, blk + 1)
                for g in range(PER):
                    act.wait_ge(mm, PER * blk + g + 1 + NG)
                    nc.scalar.activation(gm[:, b, :, g * TG:(g + 1) * TG].rearrange("p j t -> p t j"),
                                         PS[:, g % NB, :].rearrange("p (t j) -> p t j", t=TG), ACT.Copy).then_inc(out, 1)
                    for c, q in after[g]:
                        hid.gelu(nc, act, GATE_CHUNKS * blk + c, c % 2, q)
            blocks(act, empty)


def experts_phase(nc, A, G):
    with Scope(nc, "exp") as sc:
        PS, acc = G["PS"], G["acc"]
        v, v_hi, v_lo = sc.sb("v", [P, CP, D]), sc.sb("v_hi", [P, CP, D], F32R), sc.sb("v_lo", [P, CP, D], F32R)
        hid, gm = sc.sb("hid", [P, CP, T]), sc.sb("gm", [P, CP, NGB, GB])
        pr = sc.sb("pr", [P, 3, 384])
        w_hi, w_lo = sc.sb("w_hi", [P, 2, CP, T], F32R), sc.sb("w_lo", [P, 2, CP, T], F32R)
        v_in, v_high, v_low, pr_out, w_high, w_low, v_mm, acc_out = (sc.sem(n) for n in (
            "v_in v_high v_low pr_out w_high w_low v_mm acc_out").split())
        c_in = [sc.sem(f"c_in{c}") for c in range(CP)]
        block = sc.block()
        NW, NV, NBANK = CP * len(TB), KD * len(TB), 8
        w_tiles = [(c, t0, n) for c in range(CP) for t0, n in TB]
        v_tiles = [(d, t0, n) for d in range(KD) for t0, n in TB]
        slices = [slice(d * P, (d + 1) * P) for d in range(KD)]

        def steps(eng, body):
            with eng.Fori(0, NSTEP // 2 - 1) as i:
                for par in range(2):
                    body(2 * i + par, par, False)
            body(NSTEP - 2, 0, False)
            body(NSTEP - 1, 1, True)

        @block.sync
        def _(sp):
            def chunk(i, c):
                sp.dma_start(hid[:, c], A["hid"][CP * i + c]).then_inc(c_in[c], 16)
                sp.dma_start(gm[:, c], A["gm"][:, :, bass.ds(CP * i + c, 1), :].rearrange("b p a t -> p b (a t)")
                             ).then_inc(c_in[c], 16)
            for c in range(CP):
                chunk(0, c)
            sp.dma_start(v[:], A["v"][0]).then_inc(v_in, 16)

            def ahead(i):
                for c in range(CP):
                    sp.wait_ge(pr_out, NW * (i - 1) + len(TB) * (c + 1) + 3)
                    chunk(i, c)
                sp.wait_ge(v_low, KD * (i - 1) + KD)
                sp.dma_start(v[:], A["v"][i]).then_inc(v_in, 16)
            with sp.Fori(1, NSTEP) as i:
                ahead(i)

        @block.tensor
        def _(pe):
            def step(i, par, last_step):
                pe.wait_ge(w_low, NW * i + NW + 3)
                for m, (d, t0, n) in enumerate(v_tiles):
                    if m % len(TB) == 0:
                        pe.wait_ge(v_low, KD * i + d + 1)
                    pe.wait_ge(acc_out, NV * i + m + 1)
                    out = PS[:, m % NBANK, 0:n]
                    for c in range(CP):
                        hi, lo = w_hi[:, par, c, t0:t0 + n], w_lo[:, par, c, t0:t0 + n]
                        nc.tensor.matmul(out, v_hi[:, c, slices[d]], hi, start=(c == 0), stop=False)
                        nc.tensor.matmul(out, v_hi[:, c, slices[d]], lo, start=False, stop=False)
                        last = nc.tensor.matmul(out, v_lo[:, c, slices[d]], hi, start=False, stop=(c == CP - 1))
                    last.then_inc(v_mm, 1)
            steps(pe, step)

        @block.scalar
        def _(act):
            def high_w(i, m, par):
                c, t0, n = w_tiles[m]
                act.wait_ge(pr_out, NW * i + m + 1 + 3)
                nc.scalar.activation(w_hi[:, par, c, t0:t0 + n], pr[:, m % 3, 0:n], ACT.Copy).then_inc(w_high, 1)

            def high_v(d):
                nc.scalar.activation(v_hi[:, :, slices[d]], v[:, :, slices[d]], ACT.Copy).then_inc(v_high, 1)
            act.wait_ge(v_in, 16)
            for d in range(KD):
                high_v(d)
            for m in range(NW):
                high_w(0, m, 0)

            def step(i, par, last_step):
                if last_step:
                    return
                for d in range(KD):
                    for m in range(NW * d // KD, NW * (d + 1) // KD):
                        high_w(i + 1, m, 1 - par)
                    act.wait_ge(v_in, 16 * i + 32)
                    act.wait_ge(v_mm, NV * i + len(TB) * (d + 1))
                    high_v(d)
            steps(act, step)

        @block.gpsimd
        def _(pool):
            def low_v(d):
                nc.gpsimd.tensor_tensor(v_lo[:, :, slices[d]], v[:, :, slices[d]], v_hi[:, :, slices[d]].bitcast(F32),
                                        ALU.subtract).then_inc(v_low, 1)
            for d in range(KD):
                pool.wait_ge(v_high, d + 1)
                low_v(d)
            with pool.Fori(1, NSTEP) as i:
                for d in range(KD):
                    pool.wait_ge(v_high, KD * i + d + 1)
                    low_v(d)

        @block.vector
        def _(dve):
            dve.sem_inc(pr_out, 3)
            dve.sem_inc(w_low, 3)
            nc.vector.memset(acc[:], 0.0).then_inc(acc_out, NBANK)

            def product(i, m):
                c, t0, n = w_tiles[m]
                if m % len(TB) == 0:
                    dve.wait_ge(c_in[c], 32 * i + 32)
                dve.wait_ge(w_low, NW * i + m + 1)
                nc.vector.tensor_tensor(pr[:, m % 3, 0:n], hid[:, c, t0:t0 + n],
                                        gm[:, c].rearrange("p b t -> p (b t)")[:, t0:t0 + n], ALU.mult).then_inc(pr_out, 1)

            def low_w(i, m, par):
                c, t0, n = w_tiles[m]
                dve.wait_ge(w_high, NW * i + m + 1)
                nc.vector.tensor_tensor(w_lo[:, par, c, t0:t0 + n], pr[:, m % 3, 0:n],
                                        w_hi[:, par, c, t0:t0 + n].bitcast(F32), ALU.subtract).then_inc(w_low, 1)
            for m in range(NW):
                product(0, m)
                if m:
                    low_w(0, m - 1, 0)
            low_w(0, NW - 1, 0)

            def step(i, par, last_step):
                dve.wait_ge(acc_out, NV * i + NBANK)
                for m, (d, t0, n) in enumerate(v_tiles):
                    if m % 2 == 0 and not last_step:
                        product(i + 1, m // 2)
                        if m:
                            low_w(i + 1, m // 2 - 1, 1 - par)
                    dve.wait_ge(v_mm, NV * i + m + 1)
                    nc.vector.tensor_tensor(acc[:, d, t0:t0 + n], acc[:, d, t0:t0 + n], PS[:, m % NBANK, 0:n],
                                            ALU.add).then_inc(acc_out, 1)
                if not last_step:
                    low_w(i + 1, NW - 1, 1 - par)
            steps(dve, step)


def final_phase(nc, A, G):
    with Scope(nc, "fin") as sc:
        PS, acc = G["PS"], G["acc"]
        x = sc.sb("x", [P, KD, T])
        sq = sc.sb("sq", [P, 2, T])
        root, tmp = sc.sb("root", [P, T]), sc.sb("tmp", [P, T])
        x_in, own, done, saved = (sc.sem(n) for n in "x_in own done saved".split())
        ns = norm_sems(sc)
        block = sc.block()
        banks = [PS[:, b] for b in range(3)]

        @block.sync
        def _(sp):
            sp.dma_start(x[:], A["x2"]).then_inc(x_in, 16)
            for k in range(KD):
                sp.wait_ge(done, k + 1)
                sp.dma_start(A["out_y"][:, k, :], x[:, k, :]).then_inc(saved, 16)
            sp.wait_ge(saved, 16 * KD)

        @block.scalar
        def _(act):
            norm_squares(nc, act, ns, acc, sq)
            act.wait_ge(ns["summed"], KD)
            norm_roots(nc, act, ns, banks, root, G["eps"])

        @block.tensor
        def _(pe):
            norm_sums(nc, pe, ns, G["ones"], sq, banks)

        @block.vector
        def _(dve):
            step = Steps(dve, own)
            dve.wait_ge(x_in, 16)
            dve.wait_ge(ns["rooted"], 1)
            residual(nc, step, x, acc, root, tmp, G["gate"][:, 1], done)


def hybrid_decoder(nc, A):
    with Scope(nc, "all") as top:
        G = {"PS": top.ps("PS", [P, 8, 512])}
        for name, shape in (("ones", [P, P]), ("ident", [P, P]), ("iota", [P, NK]), ("eps", [P, 1]), ("one", [P, 1]),
                            ("gain", [P, 2, KD, NC]), ("shift", [P, 2, KD, NC]), ("gate", [P, 2, KD, NC])):
            G[name] = top.sb(name, shape)
        with Scope(nc, "mix") as mix:
            G["h_hi"], G["h_lo"] = mix.sb("h_hi", [P, KD, T], F32R), mix.sb("h_lo", [P, KD, T], F32R)
            condition_phase(nc, A, G)
            heads_phase(nc, A, G)
            conv_phase(nc, A, G)
            gate_phase(nc, A, G)
        with Scope(nc, "join") as join:
            G["merged"] = join.sb("merged", [P, KD, T])
            merge_phase(nc, A, G)
            out_phase(nc, A, G)
        with Scope(nc, "route") as route:
            G["h_hi"], G["h_lo"] = route.sb("h_hi", [P, KD, T], F32R), route.sb("h_lo", [P, KD, T], F32R)
            G["routeT"] = route.sb("routeT", [P, 3, NT * P])
            with Scope(nc, "lists") as lists:
                G["best"] = lists.sb("best", [P, NT, 2 * PH, TOPK])
                G["place"] = lists.sb("place", [P, NT, 2 * PH, TOPK])
                keys_phase(nc, A, G)
                pick_phase(nc, A, G)
            gates_phase(nc, A, G)
        G["acc"] = top.sb("acc", [P, KD, T])
        experts_phase(nc, A, G)
        final_phase(nc, A, G)


def chunked(a):
    a = np.asarray(a)
    a = a.reshape(a.shape[:-1] + (-1, P))
    return np.ascontiguousarray(np.moveaxis(a, -1, 0))


def blocks_of(w):
    k, n = w.shape
    return np.ascontiguousarray(w.reshape(k // P, P, n // P, P).transpose(2, 1, 0, 3))


def arrange(i):
    i = {k: np.asarray(v) for k, v in i.items()}
    sizes = (D // 2, D // 2, D // 2, H * DK, H * DK, H * DV, H * DV, D, D, RANK)
    cuts = np.cumsum((0,) + sizes)
    part = [i["w_in"][0][:, a:b] for a, b in zip(cuts[:-1], cuts[1:])]
    bg, cg, hin, q, k, v, r, ga, gb = (blocks_of(p) for p in part[:9])
    x = np.concatenate([i["x_prompt"].reshape(SEQ, D), i["x_sample"].reshape(NSEQ * LSEQ, D)]).T
    sums, pairs = chunk_masks()
    seq_rows = (np.arange(TAIL)[:, None] // LSEQ == np.arange(NSEQ)[None, :]).astype(np.float32)
    u = i["peer_u"][0].reshape(NK, NK, KD, P)
    a = {
        "x": x.reshape(KD, P, T),
        "cond": chunked(np.concatenate([i["c_prompt"], i["c_sample"]])).transpose(0, 2, 1),
        "ada_bias": chunked(i["b_ada"][0]),
        "gains": chunked(np.concatenate([i["norm_mix_pre"], i["norm_mix_post"], i["norm_ffn_pre"], i["norm_ffn_post"]])),
        "w_ada": i["w_ada"][0].reshape(KD, P, 12, 512).transpose(2, 1, 0, 3),
        "w_low": part[9].reshape(KD, P, RANK).transpose(1, 0, 2),
        "w_alpha": np.concatenate([i["w_alpha"][0], i["b_alpha"]]),
        "gla_norm": chunked(i["gla_norm_w"][0]),
        "seq_rows": seq_rows, "mask_sums": sums, "mask_pairs": pairs,
        "w_heads": np.stack([q, k, v[0::2], v[1::2], r[0::2], r[1::2]], 1),
        "state": i["state_gla"][0].transpose(1, 2, 0, 3),
        "conv_w": chunked(i["conv_w"][0]), "conv_b": chunked(i["conv_b"][0]),
        "conv_state": chunked(i["state_conv"][0]).transpose(0, 3, 1, 2),
        "w_conv": np.stack([cg, hin, bg], 1),
        "w_gate_ab": np.stack([ga, gb], 1),
        "w_proj_a": blocks_of(i["w_proj_a"][0]), "w_proj_b": blocks_of(i["w_proj_b"][0]),
        "w_out": blocks_of(i["w_out"][0]), "w_query": blocks_of(i["peer_wq"][0]),
        "subkeys": i["peer_subkeys"][0].reshape(2 * PH, NK, P).transpose(2, 0, 1),
        "u": u.transpose(1, 3, 2, 0),
        "v": i["peer_v"][0].reshape(NK, NSTEP, CP, D).transpose(1, 0, 2, 3),
    }
    return {n: np.ascontiguousarray(v) for n, v in a.items()}


_OUTS = {"out_y": (P, KD, T), "out_conv_p": (P, CC, CW - 1), "out_conv_s": (P, CC, NSEQ, CW - 1),
         "out_gla_p": (H, DK, DV), "out_gla_s": (H, DK, NSEQ, DV)}
_SCRATCH = {"ob": (H, P, 2, T), "a_in": (P, CC, T), "sig": (KD, P, 2, T), "x2": (P, KD, T), "h2": (P, KD, T), "gm": (NGB, P, NK, GB), "hid": (NK, P, T)}


def kernel(**inputs):
    import concourse.bacc as bacc
    from concourse.bass_utils import run_bass_kernel_spmd

    nc = bacc.Bacc("TRN2", target_bir_lowering=False, num_devices=1)
    arrays, A = {}, {}
    for name, a in arrange(inputs).items():
        arrays[f"in_{name}"] = a
        A[name] = nc.dram_tensor(f"in_{name}", a.shape, F32, kind="ExternalInput").ap()
    for name, shape in _OUTS.items():
        A[name] = nc.dram_tensor(name, shape, F32, kind="ExternalOutput").ap()
    for name, shape in _SCRATCH.items():
        A[name] = nc.dram_tensor(f"scratch_{name}", shape, F32, kind="Internal").ap()
    hybrid_decoder(nc, A)
    got = run_bass_kernel_spmd(nc, [arrays], core_ids=[0]).results[0]
    y = got["out_y"].transpose(2, 1, 0).reshape(T, D)
    conv_p = got["out_conv_p"].transpose(2, 1, 0).reshape(1, 1, CW - 1, D // 2)
    conv_s = got["out_conv_s"].transpose(2, 3, 1, 0).reshape(1, NSEQ, CW - 1, D // 2)
    gla_p = got["out_gla_p"].reshape(1, 1, H, DK, DV)
    gla_s = got["out_gla_s"].transpose(2, 0, 1, 3).reshape(1, NSEQ, H, DK, DV)
    return (y[:SEQ].reshape(1, SEQ, D), y[SEQ:].reshape(NSEQ, LSEQ, D), conv_p, gla_p, conv_s, gla_s)
```

```python
import numpy as np
import concourse.bass as bass
from concourse import mybir
from concourse.alu_op_type import AluOpType as ALU
from contextlib import ExitStack

F32 = mybir.dt.float32
F32R = mybir.dt.float32r
BF16 = mybir.dt.bfloat16
U32 = mybir.dt.uint32
ACT = mybir.ActivationFunctionType
AX = mybir.AxisListType

P = 128
D = 1024
KD = D // P
SEQ = 1024
NSEQ, LSEQ = 8, 8
T = SEQ + NSEQ * LSEQ
NC = 1 + NSEQ
NT = -(-T // P)
TAIL = T - (NT - 1) * P
NST = NT - 1 + NSEQ
TB = [(0, 384), (384, 384), (768, 320)]
CC = D // 2 // P
CW = 3
H, DK, DV = 4, 128, 256
RANK = 16
TAU = 16.0
LV = 7
PH, NK, TOPK = 8, 128, 16
HK = PH * TOPK
GB = 64
NGB = T // GB
CP = 4
NSTEP = NK // CP
PICK_CHUNKS = 3
GATE_CHUNKS = 6
EPS = 1e-6
LOWEST = -3.0e38


class Steps:

    def __init__(self, eng, sem, base=0):
        self.eng, self.sem, self.base, self.n = eng, sem, base, 0

    def __call__(self, ins, passed=None):
        self.n += 1
        ins.then_inc(self.sem, 1)
        self.eng.wait_ge(self.sem, self.base + self.n)
        if passed is not None:
            self.eng.sem_inc(passed, 1)


def rows(t):
    return P if t < NT - 1 else TAIL


def per_sequence(ap):
    return ap[:, :, None].broadcast_to([P, NSEQ, LSEQ])


def chunk_masks():
    sums = np.zeros((2, LV + 2, P, P), np.float32)
    pairs = np.zeros((2, LV + 1, P, P), np.float32)
    j, i = np.arange(P)[:, None], np.arange(P)[None, :]
    for kind, (n, size) in enumerate([(P, P), (TAIL, LSEQ)]):
        ok = (j < n) & (i < n)
        for l in range(LV):
            half = 1 << l
            if 2 * half > size:
                continue
            mid = i // (2 * half) * (2 * half) + half
            sums[kind, l] = ok & (((i >= mid) & (j >= mid) & (j <= i)) | ((i < mid) & (j > i) & (j < mid)))
            pairs[kind, l] = ok & (i // (2 * half) == j // (2 * half)) & (i >= mid) & (j < mid)
        start = i // size * size
        sums[kind, LV] = ok & (j >= start) & (j <= i)
        sums[kind, LV + 1] = ok & (j > i) & (j < start + size)
        pairs[kind, LV] = ok & (i == j)
    return sums.transpose(2, 0, 1, 3).copy(), pairs.transpose(2, 0, 1, 3).copy()


class Scope:

    def __init__(self, nc, name):
        self.nc, self.name, self.tensors, self.engines, self.sems = nc, name, ExitStack(), ExitStack(), []

    def __enter__(self):
        return self

    def __exit__(self, *a):
        self.engines.close()
        if self.sems:
            self.nc.clear_and_free_semaphores(self.sems)
            self.nc.all_engine_barrier()
        self.tensors.close()

    def sb(self, name, shape, dt=F32):
        return self.tensors.enter_context(self.nc.sbuf_tensor(f"{self.name}_{name}", shape, dt))

    def ps(self, name, shape):
        return self.tensors.enter_context(self.nc.psum_tensor(f"{self.name}_{name}", shape, F32))

    def sem(self, name):
        self.sems.append(self.nc.alloc_semaphore(f"{self.name}_{name}"))
        return self.sems[-1]

    def block(self):
        return self.engines.enter_context(self.nc.Block())


def project3(nc, banks, w_hi, w_lo, rhs_hi, rhs_lo, nk):
    for bank, (t0, n) in zip(banks, TB):
        for k in range(nk):
            hi, lo = rhs_hi[:, k, t0:t0 + n], rhs_lo[:, k, t0:t0 + n]
            nc.tensor.matmul(bank[:, 0:n], w_hi[:, k, :], hi, start=(k == 0), stop=False)
            nc.tensor.matmul(bank[:, 0:n], w_hi[:, k, :], lo, start=False, stop=False)
            last = nc.tensor.matmul(bank[:, 0:n], w_lo[:, k, :], hi, start=False, stop=(k == nk - 1))
        yield last


def split(nc, pool, hi, lo, raw, high, low, count):
    nc.gpsimd.tensor_copy(hi, raw).then_inc(high, 1)
    pool.wait_ge(high, count)
    nc.gpsimd.tensor_tensor(lo, raw, hi.bitcast(F32), ALU.subtract).then_inc(low, 1)


def norm_squares(nc, act, s, src, sq, ready=None, chunks=range(KD)):
    for k in chunks:
        if ready is not None:
            act.wait_ge(ready, k + 1)
        if k >= 2:
            act.wait_ge(s["summed"], k - 1)
        nc.scalar.activation(sq[:, k % 2, :], src[:, k, :], ACT.Square).then_inc(s["squared"], 1)


def norm_sums(nc, pe, s, ones, sq, banks, chunks=range(KD)):
    for k in chunks:
        pe.wait_ge(s["squared"], k + 1)
        for bank, (t0, n) in zip(banks, TB):
            last = nc.tensor.matmul(bank[:, 0:n], ones[:, :], sq[:, k % 2, t0:t0 + n],
                                    start=(k == 0), stop=(k == KD - 1))
        last.then_inc(s["summed"], 1)


def norm_roots(nc, act, s, banks, root, eps, width=D, base=0):
    for bank, (t0, n) in zip(banks, TB):
        nc.scalar.activation(root[:, t0:t0 + n], bank[:, 0:n], ACT.Ln, bias=eps[:, 0:1],
                             scale=1.0 / width).then_inc(s["logged"], 1)
    act.wait_ge(s["logged"], base + len(TB))
    nc.scalar.activation(root[:, :], root[:, :], ACT.Exp, scale=-0.5).then_inc(s["rooted"], 1)


def norm_sems(sc, tag=""):
    return {n: sc.sem(tag + n) for n in ("squared", "summed", "logged", "rooted")}


def modulate(nc, step, out, src, rstd, tmp, gain, shift, done):
    for k in range(KD):
        if k >= 1:
            step.eng.wait_ge(done, k)
        step(nc.vector.tensor_tensor(tmp[:, :], src[:, k, :], rstd[:, :], ALU.mult))
        nc.vector.tensor_scalar(out[:, k, 0:SEQ], tmp[:, 0:SEQ], gain[:, k, 0:1], shift[:, k, 0:1],
                                ALU.mult, ALU.add)
        tail = tmp[:, SEQ:T].rearrange("p (s t) -> p s t", s=NSEQ)
        otail = out[:, k, SEQ:T].rearrange("p (s t) -> p s t", s=NSEQ)
        step(nc.vector.tensor_tensor(tail, tail, per_sequence(gain[:, k, 1:NC]), ALU.mult))
        nc.vector.tensor_tensor(otail, tail, per_sequence(shift[:, k, 1:NC]), ALU.add).then_inc(done, 1)


def residual(nc, step, x, m, rstd, tmp, gain, done):
    for k in range(KD):
        if k >= 1:
            step.eng.wait_ge(done, k)
        step(nc.vector.tensor_tensor(tmp[:, :], m[:, k, :], rstd[:, :], ALU.mult))
        tail = tmp[:, SEQ:T].rearrange("p (s t) -> p s t", s=NSEQ)
        step(nc.vector.tensor_tensor(tail, tail, per_sequence(gain[:, k, 1:NC]), ALU.mult))
        step(nc.vector.scalar_tensor_tensor(out=x[:, k, 0:SEQ], in0=tmp[:, 0:SEQ], scalar=gain[:, k, 0:1],
                                            in1=x[:, k, 0:SEQ], op0=ALU.mult, op1=ALU.add))
        nc.vector.tensor_tensor(x[:, k, SEQ:T], x[:, k, SEQ:T], tmp[:, SEQ:T], ALU.add).then_inc(done, 1)


def condition_phase(nc, A, G):
    with Scope(nc, "cond") as sc:
        WN = 512
        NL = 6 * D // WN
        NBUF = 3
        h_hi, h_lo = G["h_hi"], G["h_lo"]
        x = sc.sb("x", [P, KD, T])
        w = sc.sb("w", [P, NBUF, KD, WN])
        c = sc.sb("c", [P, KD, NC])
        sc_c = sc.sb("silu_c", [P, KD, NC])
        rows_mod = sc.sb("rows_mod", [NC, 2, WN])
        mod = sc.sb("mod", [P, 6 * KD, NC])
        bias = sc.sb("bias", [P, 6 * KD])
        gains = sc.sb("gains", [P, 4, KD])
        sq = sc.sb("sq", [P, 2, T])
        root = sc.sb("root", [P, T])
        tmp = sc.sb("tmp", [P, T])
        small_in, w_in = sc.sem("small_in"), [sc.sem(f"w_in{b}") for b in range(NBUF)]
        sig, silu, w_used, r_out, t_mm, mod_out, own, ready, done, high, low = (sc.sem(n) for n in (
            "sig silu w_used r_out t_mm mod_out own ready done high low").split())
        ns = norm_sems(sc)
        PS = G["PS"]
        x_in = [sc.sem(f"x_in{k}") for k in range(KD)]
        block = sc.block()
        NF = WN // P

        @block.sync
        def _(sp):
            for dst, src in ((c, A["cond"]), (bias, A["ada_bias"]), (gains, A["gains"])):
                sp.dma_start(dst[:], src).then_inc(small_in, 16)
            for n in range(NL):
                if n >= NBUF:
                    sp.wait_ge(w_used, n - NBUF + 1)
                sp.dma_start(w[:, n % NBUF], A["w_ada"][n]).then_inc(w_in[n % NBUF], 16)
                if n < KD:
                    sp.dma_start(x[:, n, :], A["x"][n]).then_inc(x_in[n], 16)

        @block.gpsimd
        def _(pool):
            nc.gpsimd.memset(G["ones"][:, :], 1.0).then_inc(ready, 1)
            nc.gpsimd.memset(G["eps"][:, :], EPS).then_inc(ready, 1)
            nc.gpsimd.memset(G["one"][:, :], 1.0).then_inc(ready, 1)
            nc.gpsimd.memset(G["ident"][:, :], 0.0).then_inc(ready, 1)
            pool.wait_ge(ready, 4)
            nc.gpsimd.affine_select(out=G["ident"][:, :], in_=G["ident"][:, :], compare_op=ALU.not_equal,
                                    fill=1.0, base=0, pattern=[[-1, P]], channel_multiplier=1).then_inc(ready, 1)
            nc.gpsimd.iota(G["iota"][:, :], [[1, P]], base=0, channel_multiplier=0,
                           allow_small_or_imprecise_dtypes=True).then_inc(ready, 1)
            for k in range(KD):
                pool.wait_ge(high, k + 1)
                nc.gpsimd.tensor_tensor(h_lo[:, k, :], x[:, k, :], h_hi[:, k, :].bitcast(F32), ALU.subtract)

        @block.scalar
        def _(act):
            act.wait_ge(small_in, 48)
            nc.scalar.activation(sc_c[:], c[:], ACT.Sigmoid).then_inc(sig, 1)
            for n in range(NL):
                act.wait_ge(w_used, n + 1)
                if n >= 2:
                    act.wait_ge(t_mm, n - 1)
                nc.scalar.activation(rows_mod[:, n % 2, :], PS[0:NC, n % 2, 0:WN], ACT.Copy).then_inc(r_out, 1)
                if 2 <= n < KD + 2:
                    act.wait_ge(x_in[n - 2], 16)
                    norm_squares(nc, act, ns, x, sq, chunks=(n - 2,))
            act.wait_ge(ready, 6)
            act.wait_ge(ns["summed"], KD)
            norm_roots(nc, act, ns, [PS[:, b] for b in (4, 5, 6)], root, G["eps"])
            for k in range(KD):
                act.wait_ge(done, k + 1)
                nc.scalar.activation(h_hi[:, k, :], x[:, k, :], ACT.Copy).then_inc(high, 1)

        @block.tensor
        def _(pe):
            pe.wait_ge(ready, 6)
            pe.wait_ge(silu, 1)

            def transposes(n):
                pe.wait_ge(r_out, n + 1)
                if n >= 2:
                    pe.wait_ge(mod_out, n - 1)
                for f in range(NF):
                    last = nc.tensor.transpose(PS[:, 2 + n % 2, f * NC:(f + 1) * NC],
                                               rows_mod[:, n % 2, f * P:(f + 1) * P], G["ident"][0:NC, 0:NC])
                last.then_inc(t_mm, 1)
            for n in range(NL):
                pe.wait_ge(w_in[n % NBUF], 16 * (n // NBUF) + 16)
                if n >= 2:
                    pe.wait_ge(r_out, n - 1)
                for k in range(KD):
                    last = nc.tensor.matmul(PS[0:NC, n % 2, 0:WN], sc_c[:, k, :], w[:, n % NBUF, k, :],
                                            start=(k == 0), stop=(k == KD - 1))
                last.then_inc(w_used, 1)
                if n:
                    transposes(n - 1)
                if 3 <= n < KD + 3:
                    norm_sums(nc, pe, ns, G["ones"], sq, [PS[:, b] for b in (4, 5, 6)], chunks=(n - 3,))
            transposes(NL - 1)

        @block.vector
        def _(dve):
            step = Steps(dve, own)
            dve.wait_ge(sig, 1)
            nc.vector.tensor_tensor(sc_c[:], sc_c[:], c[:], ALU.mult).then_inc(silu, 1)
            dve.wait_ge(small_in, 48)
            for n in range(NL):
                dve.wait_ge(t_mm, n + 1)
                nc.vector.tensor_tensor(mod[:, n * NF:(n + 1) * NF, :],
                                        PS[:, 2 + n % 2, 0:NF * NC].rearrange("p (b c) -> p b c", c=NC),
                                        bias[:, n * NF:(n + 1) * NF][:, :, None].broadcast_to([P, NF, NC]),
                                        ALU.add).then_inc(mod_out, 1)
            dve.wait_ge(mod_out, NL)
            for n, (shift, scale, gate) in enumerate(((0, 1, 2), (3, 4, 5))):
                seg = lambda q: mod[:, q * KD:(q + 1) * KD, :]
                g = lambda q: gains[:, q, :][:, :, None].broadcast_to([P, KD, NC])
                step(nc.vector.scalar_tensor_tensor(out=G["gain"][:, n], in0=seg(scale), scalar=1.0, in1=g(2 * n),
                                                    op0=ALU.add, op1=ALU.mult))
                step(nc.vector.tensor_tensor(G["gate"][:, n], seg(gate), g(2 * n + 1), ALU.mult))
                step(nc.vector.tensor_copy(G["shift"][:, n], seg(shift)))
            dve.wait_ge(ns["rooted"], 1)
            modulate(nc, step, x, x, root, tmp, G["gain"][:, 0], G["shift"][:, 0], done)


def heads_phase(nc, A, G):
    with Scope(nc, "gla") as sc:
        NW = 6
        NSLOT = 4
        SLOT = (0, 1, 2, 3, 0, 1)
        h_hi, h_lo, PS = G["h_hi"], G["h_lo"], G["PS"]
        w = sc.sb("w", [P, 2, KD, P])
        w_hi, w_lo = sc.sb("w_hi", [P, NSLOT, KD, P], F32R), sc.sb("w_lo", [P, NSLOT, KD, P], F32R)
        lw_hi, lw_lo = sc.sb("lw_hi", [P, KD, RANK], F32R), sc.sb("lw_lo", [P, KD, RANK], F32R)
        low = sc.sb("low", [RANK + 1, NT * P])
        w_alpha = sc.sb("w_alpha", [RANK + 1, H * DK])
        gnorm = sc.sb("gnorm", [P, 2 * H])
        q, k = sc.sb("q", [P, T]), sc.sb("k", [P, T])
        v = sc.sb("v", [P, NT, DV])
        g_hi, g_lo = sc.sb("g_hi", [P, NT, DK], F32R), sc.sb("g_lo", [P, NT, DK], F32R)
        soft = sc.sb("soft", [P, NT, DK])
        w_low = soft[:, 0, :].rearrange("p (k r) -> p k r", k=KD)
        r = sc.sb("r", [P, 2, T])
        o = sc.sb("o", [P, 2, T])
        E = sc.sb("E", [P, 2, LV + 2, P])
        Qc = sc.sb("Qc", [P, 3, P])
        decayed = sc.sb("decayed", [P, 4])
        least = r[:].rearrange("p e t -> p (e t)")[:, 0:NT * DK].rearrange("p (t d) -> p t d", d=DK)
        sT = sc.sb("sT", [P, P])
        kT = sc.sb("kT", [P, P])
        seq_rows = sc.sb("seq_rows", [TAIL, NSEQ])
        S = sc.sb("S", [P, DV])
        Ss = sc.sb("Ss", [P, NSEQ, DV])
        odd = Ss[:].rearrange("p s e -> p (s e)").rearrange("p (n l i) -> p n l i", n=2, i=P)
        Q2 = (sc.sb("Q", [P, LV, P]), odd[:, 0, 0:LV])
        K2 = (sc.sb("K", [P, LV + 1, P]), odd[:, 1, 0:LV + 1])
        sums, pairs = sc.sb("sums", [P, LV + 2, P], F32R), sc.sb("pairs", [P, LV + 1, P])
        sums_s, pairs_s = sc.sb("sums_s", [TAIL, LV + 2, TAIL], F32R), sc.sb("pairs_s", [TAIL, LV + 1, TAIL])
        SUMS, PAIRS = (sums, sums_s), (pairs, pairs_s)
        prod = soft[:, 0:LV + 1, :]
        kTs = E[0:TAIL, 1, 0:NSEQ, :]
        sg = v[:].rearrange("p t e -> p (t e)")[:, 0:2 * T].rearrange("p (e t) -> p e t", e=2)
        flat = soft[:].rearrange("p t d -> p (t d)")[:, 0:T]
        names = ("small_in low_in low_ready low_mm q_mm k_mm q_out k_out z_mm z_min z_abs g_ready v_mm v_out r_mm r_out r_sig "
                 "e_mm e_exp qk s_mm s_red t_mm t_out o_mm o_out st_mm st_out kts st_in st_saved st_free "
                 "sq_ready sums own act_own scaled normed o_free ob_saved high low_part passed lw_high lw_low "
                 "logged rooted masked masks_set g_high").split()
        M = {n: sc.sem(n) for n in names}
        w_in = [sc.sem(f"w_in{b}") for b in range(2)]
        block = sc.block()
        bank = lambda b: PS[:, b]
        tiles = [(t, rows(t), 0 if t < NT - 1 else 1) for t in range(NT)]
        assert NT % 2

        @block.sync
        def _(sp):
            sp.sem_inc(M["st_free"], 1)
            sp.sem_inc(M["o_free"], 1)
            sp.dma_start(w_low, A["w_low"]).then_inc(M["low_in"], 16)

            def bring(i, b):
                sp.dma_start(w[:, b % 2], A["w_heads"][i, b]).then_inc(w_in[b % 2], 16)
            for b in range(2):
                bring(0, b)
            for dst, src in ((w_alpha, A["w_alpha"]), (gnorm, A["gla_norm"]),
                             (seq_rows, A["seq_rows"]), (E[:, 0], A["mask_sums"][:, 0]), (pairs, A["mask_pairs"][:, 0]),
                             (E[0:TAIL, 1, :, 0:TAIL], A["mask_sums"][0:TAIL, 1, :, 0:TAIL]),
                             (pairs_s, A["mask_pairs"][0:TAIL, 1, :, 0:TAIL])):
                sp.dma_start(dst[:], src).then_inc(M["small_in"], 16)
            for b in range(2, NW):
                sp.wait_ge(M["low_part"], b - 1)
                bring(0, b)

            def states(i):
                sp.wait_ge(M["s_mm"], NT * i + NT - 1)
                sp.dma_start(Ss[:], A["state"][i]).then_inc(M["st_in"], 16)
            def put(i):
                sp.wait_ge(M["st_out"], NST * (i + 1))
                sp.dma_start(A["out_gla_p"][i], S[:]).then_inc(M["st_saved"], 16)
                sp.dma_start(A["out_gla_s"][i], Ss[:]).then_inc(M["st_saved"], 16)
                sp.wait_ge(M["st_saved"], 32 * (i + 1))
                sp.sem_inc(M["st_free"], 1)
                sp.wait_ge(M["normed"], 2 * (i + 1))
                sp.dma_start(A["ob"][i], o[:]).then_inc(M["ob_saved"], 16)
            with sp.Fori(1, H) as i:
                for b in range(4):
                    sp.wait_ge(M["low_part"], NW * i + b - 1)
                    bring(i, b)
                states(i - 1)
                put(i - 1)
                for b in range(4, NW):
                    sp.wait_ge(M["low_part"], NW * i + b - 1)
                    bring(i, b)
                sp.wait_ge(M["ob_saved"], 16 * i)
                sp.sem_inc(M["o_free"], 1)
            states(H - 1)
            put(H - 1)
            sp.wait_ge(M["ob_saved"], 16 * H)

        @block.gpsimd
        def _(pool):
            pool.wait_ge(M["low_in"], 16)
            split(nc, pool, lw_hi[:], lw_lo[:], w_low[:], M["lw_high"], M["lw_low"], 1)
            with pool.Fori(0, H) as i:
                for b in range(NW):
                    pool.wait_ge(w_in[b % 2], 16 * (NW // 2 * i + b // 2) + 16)
                    if b < 2:
                        pool.wait_ge(M["r_mm"], 6 * i + 3 * b + 3)
                    elif b < 4:
                        pool.wait_ge(M["v_mm"], NT * i + NT)
                    else:
                        pool.wait_ge((M["q_mm"], M["k_mm"])[b - 4], 3 * i + 3)
                    pool.sem_inc(M["passed"], 1)
                    split(nc, pool, w_hi[:, SLOT[b]], w_lo[:, SLOT[b]], w[:, b % 2], M["high"], M["low_part"], NW * i + b + 1)

        @block.tensor
        def _(pe):
            pe.sem_inc(M["r_mm"], 6)
            pe.sem_inc(M["v_mm"], NT)
            pe.wait_ge(M["lw_low"], 1)
            for b, (t0, n) in enumerate(TB):
                for kk in range(KD):
                    hi, lo = h_hi[:, kk, t0:t0 + n], h_lo[:, kk, t0:t0 + n]
                    nc.tensor.matmul(PS[0:RANK, b, 0:n], lw_hi[:, kk, :], hi, start=(kk == 0), stop=False)
                    nc.tensor.matmul(PS[0:RANK, b, 0:n], lw_hi[:, kk, :], lo, start=False, stop=False)
                    last = nc.tensor.matmul(PS[0:RANK, b, 0:n], lw_lo[:, kk, :], hi, start=False, stop=(kk == KD - 1))
            last.then_inc(M["low_mm"], 1)
            pe.wait_ge(M["low_ready"], 1)
            with pe.Fori(0, H) as i:
                pe.wait_ge(M["low_part"], NW * i + 1)
                for last in project3(nc, [bank(0), bank(1), bank(2)], w_hi[:, 0], w_lo[:, 0], h_hi, h_lo, KD):
                    last.then_inc(M["q_mm"], 1)
                pe.wait_ge(M["low_part"], NW * i + 2)
                pe.wait_ge(M["rooted"], i + 1)
                for last in project3(nc, [bank(3), bank(4), bank(5)], w_hi[:, 1], w_lo[:, 1], h_hi, h_lo, KD):
                    last.then_inc(M["k_mm"], 1)
                pe.wait_ge(M["q_out"], 3 * i + 3)
                for t, n, _ in tiles:
                    last = nc.tensor.matmul(PS[:, t // 4, t % 4 * DK:(t % 4 + 1) * DK],
                                            low[:, t * P:(t + 1) * P], w_alpha[:, bass.ds(i * DK, DK)],
                                            start=True, stop=True)
                last.then_inc(M["z_mm"], 1)
                pe.wait_ge(M["low_part"], NW * i + 4)
                pe.wait_ge(M["k_out"], 3 * i + 3)
                for t, n, _ in tiles:
                    if t >= 3:
                        pe.wait_ge(M["v_out"], NT * i + t - 2)
                    out = PS[0:n, 3 + t % 3, 0:DV]
                    for kk in range(KD):
                        hi, lo = h_hi[:, kk, t * P:t * P + n], h_lo[:, kk, t * P:t * P + n]
                        nc.tensor.matmul(out, hi, w_hi[:, 2:4, kk, :], start=(kk == 0), stop=False)
                        nc.tensor.matmul(out, hi, w_lo[:, 2:4, kk, :], start=False, stop=False)
                        last = nc.tensor.matmul(out, lo, w_hi[:, 2:4, kk, :], start=False, stop=(kk == KD - 1))
                    last.then_inc(M["v_mm"], 1)
                pe.wait_ge(M["z_abs"], 2 * i + 2)
                for b in range(2):
                    pe.wait_ge(M["low_part"], NW * i + 5 + b)
                    if b:
                        pe.wait_ge(M["v_out"], NT * i + NT)
                    for last in project3(nc, [bank(3 * b), bank(3 * b + 1), bank(3 * b + 2)], w_hi[:, b], w_lo[:, b],
                                         h_hi, h_lo, KD):
                        last.then_inc(M["r_mm"], 1)
                pe.wait_ge(M["r_out"], 6 * i + 6)
                pe.wait_ge(M["g_ready"], 4 * i + 4)

                def exponents(t, n, kind):
                    if t >= 1:
                        pe.wait_ge(M["e_exp"], NT * i + t)
                    for b in range(3):
                        out = PS[:, b, 0:384].rearrange("p (l i) -> p l i", l=3)[:, :, 0:n]
                        mask = SUMS[kind][0:n, 3 * b:3 * b + 3, 0:n]
                        nc.tensor.matmul(out, g_hi[0:n, t, :], mask, start=True, stop=False)
                        last = nc.tensor.matmul(out, g_lo[0:n, t, :], mask, start=False, stop=True)
                    last.then_inc(M["e_mm"], 1)

                def results(t, n, kind):
                    if t >= 1:
                        pe.wait_ge(M["st_out"], NST * i + t)
                        pe.wait_ge(M["o_out"], NT * i + t)
                    for e in range(2) if t >= 1 else ():
                        nc.tensor.matmul(PS[:, 6, e * P:e * P + n], S[:, e * P:(e + 1) * P], Qc[:, t % 3, 0:n],
                                         start=(e == 0), stop=False, skip_group_check=True)
                    pe.wait_ge(M["s_red"], NT * i + t + 1)
                    for e in range(2):
                        last = nc.tensor.matmul(PS[:, 6, e * P:e * P + n], v[0:n, t, e * P:(e + 1) * P],
                                                sT[0:n, 0:n], start=(t == 0 and e == 0), stop=True,
                                                skip_group_check=True)
                    last.then_inc(M["o_mm"], 1)
                    pe.wait_ge(M["t_out"], NT * i + t + 1)
                    nc.tensor.matmul(PS[:, 7, 0:DV], kT[0:n, :], v[0:n, t, :],
                                     start=True, stop=True).then_inc(M["st_mm"], 1)

                exponents(*tiles[0])
                exponents(*tiles[1])
                for t, n, kind in tiles:
                    Q, K = Q2[t % 2], K2[t % 2]
                    pe.wait_ge(M["qk"], 3 * (NT * i + t) + 3)
                    if t >= 1:
                        pe.wait_ge(M["t_out"], NT * i + t)
                    nc.tensor.transpose(PS[:, 5, 0:DK], K[:, LV, :], G["ident"][:, :]).then_inc(M["t_mm"], 1)
                    if t >= 1:
                        pe.wait_ge(M["masked"], NT * i + t)
                    for l in range(LV + 1):
                        lhs = K[:, l, 0:n] if l < LV else k[:, t * P:t * P + n]
                        rhs = Q[:, l, 0:n] if l < LV else q[:, t * P:t * P + n]
                        last = nc.tensor.matmul(PS[0:n, 3 + l // 4, l % 4 * P:l % 4 * P + n], lhs, rhs,
                                                start=True, stop=True)
                    last.then_inc(M["s_mm"], 1)
                    if t >= 1:
                        results(*tiles[t - 1])
                    if t + 2 < NT:
                        exponents(*tiles[t + 2])
                t, n, kind = tiles[NT - 1]
                pe.wait_ge(M["s_red"], NT * i + t + 1)
                pe.wait_ge(M["o_out"], NT * i + t)
                pe.wait_ge(M["st_in"], 16 * i + 16)
                for e in range(2):
                    last = nc.tensor.matmul(PS[:, 6, e * P:e * P + n], v[0:n, t, e * P:(e + 1) * P],
                                            sT[0:n, 0:n], start=True, stop=False)
                    for s in range(NSEQ):
                        last = nc.tensor.matmul(PS[:, 6, e * P + s * LSEQ:e * P + (s + 1) * LSEQ],
                                                Ss[:, s, e * P:(e + 1) * P],
                                                Qc[:, t % 3, s * LSEQ:(s + 1) * LSEQ],
                                                start=False, stop=(s == NSEQ - 1))
                last.then_inc(M["o_mm"], 1)
                pe.wait_ge(M["kts"], i + 1)
                pe.wait_ge(M["masked"], NT * i + NT)
                for s in range(NSEQ):
                    pe.wait_ge(M["st_out"], NST * i + NT - 1 + max(s - 1, 0))
                    nc.tensor.matmul(PS[:, 7 if s % 2 else 4, 0:DV], kTs[:, s, :], v[0:n, t, :],
                                     start=True, stop=True).then_inc(M["st_mm"], 1)
                pe.wait_ge(M["sq_ready"], i + 1)
                pe.wait_ge(M["st_out"], NST * (i + 1))
                for b, (t0, n) in enumerate(TB):
                    for e, src in enumerate((q, k)):
                        last = nc.tensor.matmul(PS[:, 3 + b, 0:n], G["ones"][:, :], src[:, t0:t0 + n],
                                                start=(e == 0), stop=(e == 1))
                last.then_inc(M["sums"], 1)

        @block.scalar
        def _(act):
            act.sem_inc(M["rooted"], 1)
            act.wait_ge(M["small_in"], 112)
            nc.scalar.activation(sums[:], E[:, 0], ACT.Copy).then_inc(M["masks_set"], 1)
            nc.scalar.activation(sums_s[:], E[0:TAIL, 1, :, 0:TAIL], ACT.Copy).then_inc(M["masks_set"], 1)
            act.wait_ge(M["masks_set"], 2)
            with act.Fori(0, H) as i:
                for b, (t0, n) in enumerate(TB):
                    act.wait_ge(M["q_mm"], 3 * i + 1 + b)
                    nc.scalar.activation(q[:, t0:t0 + n], PS[:, b, 0:n], ACT.Copy,
                                         scale=float(DK) ** -0.5).then_inc(M["q_out"], 1)
                steps = Steps(act, M["act_own"], 4 * i)
                act.wait_ge(M["z_min"], 2 * i + 2)
                full = PS[:, 0:2, :].rearrange("p b (t d) -> p (b t) d", d=DK)
                nc.scalar.activation(soft[:, 0:NT - 1, :], full, ACT.Abs).then_inc(M["z_abs"], 1)
                nc.scalar.activation(soft[0:TAIL, NT - 1, :], PS[0:TAIL, 2, 0:DK], ACT.Abs).then_inc(M["z_abs"], 1)
                act.wait_ge(M["z_abs"], 2 * i + 2)
                for part in (soft[:, 0:NT - 1, :], soft[0:TAIL, NT - 1, :]):
                    steps(nc.scalar.activation(part, part, ACT.Exp, scale=-1.0))
                for n, part in ((P, soft[:, 0:NT - 1, :]), (TAIL, soft[0:TAIL, NT - 1, :])):
                    steps(nc.scalar.activation(part, part, ACT.Ln, bias=G["one"][0:n, 0:1]))
                for t, n, _ in tiles:
                    act.wait_ge(M["v_mm"], NT * i + t + 1 + NT)
                    nc.scalar.activation(v[0:n, t, :], PS[0:n, 3 + t % 3, 0:DV], ACT.Copy).then_inc(M["v_out"], 1)
                    if t == 3:
                        act.wait_ge(M["g_ready"], 4 * i + 2)
                        nc.scalar.activation(g_hi[:, 0:NT - 1, :], soft[:, 0:NT - 1, :], ACT.Copy).then_inc(M["g_high"], 1)
                        nc.scalar.activation(g_hi[0:TAIL, NT - 1, :], soft[0:TAIL, NT - 1, :],
                                             ACT.Copy).then_inc(M["g_high"], 1)
                for b in range(6):
                    act.wait_ge(M["r_mm"], 6 * i + b + 1 + 6)
                    t0, n = TB[b % 3]
                    nc.scalar.activation(r[:, b // 3, t0:t0 + n], PS[:, b, 0:n], ACT.Copy).then_inc(M["r_out"], 1)

                def exps(t, n, kind):
                    act.wait_ge(M["e_mm"], NT * i + t + 1)
                    if t >= 2:
                        act.wait_ge(M["qk"], 3 * (NT * i + t - 2) + 3)
                    src = PS[:, 0:3, 0:384].rearrange("p b (l i) -> p b l i", l=3)[:, :, :, 0:n]
                    dst = E[:, t % 2].rearrange("p (b l) i -> p b l i", l=3)[:, :, :, 0:n]
                    nc.scalar.activation(dst, src, ACT.Exp).then_inc(M["e_exp"], 1)
                def output(t, n, kind):
                    act.wait_ge(M["o_mm"], NT * i + t + 1)
                    if t == 0:
                        act.wait_ge(M["o_free"], i + 1)
                    nc.scalar.activation(o[:, :, t * P:t * P + n],
                                         PS[:, 6, 0:2 * P].rearrange("p (e i) -> p e i", e=2)[:, :, 0:n],
                                         ACT.Copy).then_inc(M["o_out"], 1)
                exps(*tiles[0])
                exps(*tiles[1])
                for t, n, kind in tiles:
                    if t >= 1:
                        output(*tiles[t - 1])
                        act.wait_ge(M["st_mm"], NST * i + t)
                    act.wait_ge(M["t_mm"], NT * i + t + 1)
                    nc.scalar.activation(kT[0:n, :], PS[0:n, 5, 0:DK], ACT.Copy).then_inc(M["t_out"], 1)
                    if t + 2 < NT:
                        exps(*tiles[t + 2])
                output(*tiles[NT - 1])
                act.wait_ge(M["o_out"], NT * i + NT)
                nc.scalar.activation(q[:, :], o[:, 0, :], ACT.Square)
                nc.scalar.activation(k[:, :], o[:, 1, :], ACT.Square).then_inc(M["sq_ready"], 1)
                act.wait_ge(M["sums"], i + 1)
                norm_roots(nc, act, {"logged": M["logged"], "rooted": M["rooted"]}, [bank(3), bank(4), bank(5)], flat,
                           G["eps"], DV, 3 * i)
                act.wait_ge(M["st_mm"], NST * (i + 1))
                nc.scalar.activation(sg, r[:], ACT.Sigmoid).then_inc(M["r_sig"], 1)

        @block.vector
        def _(dve):
            dve.wait_ge(M["small_in"], 112)
            nc.vector.memset(low[:, :], 1.0).then_inc(M["own"], 1)
            dve.wait_ge(M["own"], 1)
            dve.wait_ge(M["low_mm"], 1)
            for b, (t0, n) in enumerate(TB):
                last = nc.vector.tensor_copy(low[0:RANK, t0:t0 + n], PS[0:RANK, b, 0:n])
            last.then_inc(M["low_ready"], 1)
            OWN = 4
            with dve.Fori(0, H) as i:
                step = Steps(dve, M["own"], OWN * i + 1)
                for b, (t0, n) in enumerate(TB):
                    dve.wait_ge(M["k_mm"], 3 * i + 1 + b)
                    nc.vector.tensor_copy(k[:, t0:t0 + n], PS[:, 3 + b, 0:n]).then_inc(M["k_out"], 1)
                dve.wait_ge(M["z_mm"], i + 1)
                full = PS[:, 0:2, :].rearrange("p b (t d) -> p (b t) d", d=DK)
                nc.vector.tensor_scalar(least[:, 0:NT - 1, :], full, 0.0, 1.0 / TAU, ALU.min, ALU.mult).then_inc(M["z_min"], 1)
                nc.vector.tensor_scalar(least[0:TAIL, NT - 1, :], PS[0:TAIL, 2, 0:DK], 0.0, 1.0 / TAU,
                                        ALU.min, ALU.mult).then_inc(M["z_min"], 1)
                dve.wait_ge(M["z_min"], 2 * i + 2)
                dve.wait_ge(M["act_own"], 4 * i + 4)
                parts = [tuple(a[0:n, t] for a in (soft, least, g_hi, g_lo))
                         for n, t in ((P, slice(0, NT - 1)), (TAIL, slice(NT - 1, NT)))]
                for gg, low_z, _, _ in parts:
                    nc.vector.scalar_tensor_tensor(out=gg, in0=gg, scalar=-1.0 / TAU, in1=low_z, op0=ALU.mult,
                                                   op1=ALU.add).then_inc(M["g_ready"], 1)
                dve.wait_ge(M["g_high"], 2 * i + 2)
                for gg, _, hi, lo in parts:
                    nc.vector.tensor_tensor(lo, gg, hi.bitcast(F32), ALU.subtract).then_inc(M["g_ready"], 1)
                dve.wait_ge(M["g_ready"], 4 * i + 4)

                def decay(t, n, kind):
                    tok, Et, Q, K = slice(t * P, t * P + n), E[:, t % 2], Q2[t % 2], K2[t % 2]
                    dve.wait_ge(M["e_exp"], NT * i + t + 1)
                    if t >= 4:
                        dve.wait_ge(M["st_out"], NST * i + t - 3)
                    if t < NT - 1:
                        nc.vector.tensor_copy(decayed[:, t % 4:t % 4 + 1], Et[:, LV, n - 1:n])
                    nc.vector.tensor_tensor(Q[:, :, 0:n], Et[:, 0:LV, 0:n],
                                            q[:, None, tok].broadcast_to([P, LV, n]), ALU.mult).then_inc(M["qk"], 1)
                    nc.vector.tensor_tensor(K[:, 0:LV, 0:n], Et[:, 0:LV, 0:n],
                                            k[:, None, tok].broadcast_to([P, LV, n]), ALU.mult).then_inc(M["qk"], 1)
                    nc.vector.tensor_tensor(Qc[:, t % 3, 0:n], Et[:, LV, 0:n], q[:, tok], ALU.mult)
                    nc.vector.tensor_tensor(K[:, LV, 0:n], Et[:, LV + 1, 0:n], k[:, tok], ALU.mult).then_inc(M["qk"], 1)

                def state(t, n, kind):
                    dve.wait_ge(M["st_mm"], NST * i + t + 1)
                    if t == 0:
                        nc.vector.tensor_copy(S[:, :], PS[:, 7, 0:DV]).then_inc(M["st_out"], 1)
                    else:
                        dve.wait_ge(M["st_out"], NST * i + t)
                        nc.vector.scalar_tensor_tensor(out=S[:, :], in0=S[:, :], scalar=decayed[:, t % 4:t % 4 + 1],
                                                       in1=PS[:, 7, 0:DV], op0=ALU.mult,
                                                       op1=ALU.add).then_inc(M["st_out"], 1)
                decay(*tiles[0])
                dve.wait_ge(M["st_free"], i + 1)
                decay(*tiles[1])
                for t, n, kind in tiles:
                    dve.wait_ge(M["s_mm"], NT * i + t + 1)
                    if t >= 1:
                        dve.wait_ge(M["s_red"], NT * i + t)
                    nc.vector.tensor_tensor(prod[0:n, :, 0:n],
                                            PS[0:n, 3:5, :].rearrange("p b (l i) -> p (b l) i", i=P)[:, :, 0:n],
                                            PAIRS[kind][0:n, :, 0:n], ALU.mult).then_inc(M["masked"], 1)
                    dve.wait_ge(M["masked"], NT * i + t + 1)
                    if t >= 1:
                        dve.wait_ge(M["o_mm"], NT * i + t)
                    nc.vector.tensor_reduce(sT[0:n, 0:n], prod[0:n, :, 0:n].rearrange("p l i -> p i l"), AX.X,
                                            ALU.add).then_inc(M["s_red"], 1)
                    if t >= 1:
                        state(*tiles[t - 1])
                    if t + 2 < NT:
                        decay(*tiles[t + 2])
                Et = E[:, (NT - 1) % 2]
                dve.wait_ge(M["t_out"], NT * i + NT)
                nc.vector.tensor_tensor(kTs, kT[0:n, None, :].broadcast_to([n, NSEQ, DK]),
                                        seq_rows[:, :, None].broadcast_to([n, NSEQ, DK]),
                                        ALU.mult).then_inc(M["kts"], 1)
                for s in range(NSEQ):
                    dve.wait_ge(M["st_mm"], NST * i + NT + s)
                    nc.vector.scalar_tensor_tensor(out=Ss[:, s, :], in0=Ss[:, s, :],
                                                   scalar=Et[:, LV, (s + 1) * LSEQ - 1:(s + 1) * LSEQ],
                                                   in1=PS[:, 7 if s % 2 else 4, 0:DV], op0=ALU.mult,
                                                   op1=ALU.add).then_inc(M["st_out"], 1)
                dve.wait_ge(M["rooted"], i + 2)
                for e in range(2):
                    step(nc.vector.tensor_tensor(o[:, e, :], o[:, e, :], flat, ALU.mult))
                dve.wait_ge(M["r_sig"], i + 1)
                for e in range(2):
                    step(nc.vector.tensor_tensor(r[:, e, :], r[:, e, :], sg[:, e, :], ALU.mult))
                    nc.vector.scalar_tensor_tensor(out=o[:, e, :], in0=o[:, e, :], scalar=gnorm[:, bass.ds(2 * i + e, 1)],
                                                   in1=r[:, e, :], op0=ALU.mult, op1=ALU.mult).then_inc(M["normed"], 1)
                dve.wait_ge(M["normed"], 2 * i + 2)
                assert step.n == OWN


class Weights:

    def __init__(self, sc, blocks, used, sources):
        self.n, self.used, self.sources = blocks, used, sources
        self.raw = sc.sb("w", [P, blocks, KD, P])
        self.hi, self.lo = sc.sb("w_hi", [P, blocks, KD, P], F32R), sc.sb("w_lo", [P, blocks, KD, P], F32R)
        self.high, self.low, self.passed = sc.sem("w_high"), sc.sem("w_low"), sc.sem("w_passed")
        self.landed = [sc.sem(f"w_in{b}") for b in range(blocks)]

    def bring(self, sp, steps, between=None):
        def step(i, later=True):
            for b, src in enumerate(self.sources):
                if later:
                    sp.wait_ge(self.low, self.n * (i - 1) + b + 1)
                nk = src(0).shape[1]
                sp.dma_start(self.raw[:, b, 0:nk], src(i)).then_inc(self.landed[b], 16)
        step(0, later=False)
        if between is not None:
            between(sp)
        with sp.Fori(1, steps) as i:
            step(i)

    def first_highs(self, nc, act):
        for b, src in enumerate(self.sources):
            nk = src(0).shape[1]
            act.wait_ge(self.landed[b], 16)
            nc.scalar.activation(self.hi[:, b, 0:nk], self.raw[:, b, 0:nk], ACT.Copy).then_inc(self.high, 1)

    def first_lows(self, nc, dve):
        for b, src in enumerate(self.sources):
            nk = src(0).shape[1]
            dve.wait_ge(self.high, b + 1)
            nc.vector.tensor_tensor(self.lo[:, b, 0:nk], self.raw[:, b, 0:nk], self.hi[:, b, 0:nk].bitcast(F32),
                                    ALU.subtract).then_inc(self.low, 1)

    def split(self, nc, pool, steps):
        pool.wait_ge(self.low, self.n)
        with pool.Fori(1, steps) as i:
            for b, src in enumerate(self.sources):
                nk = src(0).shape[1]
                pool.wait_ge(self.landed[b], 16 * i + 16)
                sem, first, more = self.used(b)
                pool.wait_ge(sem, more * (i - 1) + first)
                pool.sem_inc(self.passed, 1)
                split(nc, pool, self.hi[:, b, 0:nk], self.lo[:, b, 0:nk], self.raw[:, b, 0:nk], self.high, self.low,
                      self.n * i + b + 1)

    def project(self, nc, pe, i, b, banks, rhs_hi, rhs_lo, nk=KD):
        pe.wait_ge(self.low, self.n * i + b + 1)
        return project3(nc, banks, self.hi[:, b], self.lo[:, b], rhs_hi, rhs_lo, nk)


def split_inputs(nc, sc, tag, hi, lo, raw, source, chunks):
    slots = raw.shape[1]
    landed = [sc.sem(f"{tag}_in{b}") for b in range(slots)]
    high, low = sc.sem(f"{tag}_high"), sc.sem(f"{tag}_low")

    def fetch(sp):
        for k in range(chunks):
            if k >= slots:
                sp.wait_ge(low, k - slots + 1)
            sp.dma_start(raw[:, k % slots, :], source(k)).then_inc(landed[k % slots], 16)

    def highs(act):
        for k in range(chunks):
            act.wait_ge(landed[k % slots], 16 * (k // slots) + 16)
            nc.scalar.activation(hi[:, k, :], raw[:, k % slots, :], ACT.Copy).then_inc(high, 1)

    def lows(dve):
        for k in range(chunks):
            dve.wait_ge(high, k + 1)
            nc.vector.tensor_tensor(lo[:, k, :], raw[:, k % slots, :], hi[:, k, :].bitcast(F32), ALU.subtract).then_inc(low, 1)
    return fetch, highs, lows, low


def conv_phase(nc, A, G):
    with Scope(nc, "conv") as sc:
        NB = 6
        PS = G["PS"]
        cg, bg, y = (sc.sb(n, [P, T]) for n in ("cg", "bg", "y"))
        a_in = sc.sb("a_in", [P, CC, T])
        up = sc.sb("up", [P, CW - 1 + SEQ])
        us = sc.sb("us", [P, NSEQ, CW - 1 + LSEQ])
        taps, cbias = sc.sb("taps", [P, CW, CC]), sc.sb("cbias", [P, CC])
        past = sc.sb("past", [P, CC, NSEQ, CW - 1])
        last_p, last_s = sc.sb("last_p", [P, CC, CW - 1]), sc.sb("last_s", [P, CC, NSEQ, CW - 1])
        small_in, c_mm, h_mm, b_mm, c_out, u_out, b_out, conv_out, own, saved = (sc.sem(n) for n in (
            "small_in c_mm h_mm b_mm c_out u_out b_out conv_out own saved").split())
        w = Weights(sc, 3, lambda b: ((c_mm, h_mm, b_mm)[b], 3, 3), [lambda i, b=b: A["w_conv"][i, b] for b in range(3)])
        block = sc.block()
        sets = lambda n: [PS[:, 3 * (n % 2) + b] for b in range(3)]
        OPS = 3 + 2 * CW

        @block.sync
        def _(sp):
            def small(sp):
                for dst, src in ((taps, A["conv_w"]), (cbias, A["conv_b"]), (past, A["conv_state"])):
                    sp.dma_start(dst[:], src).then_inc(small_in, 16)
            w.bring(sp, CC, between=small)
            sp.wait_ge(conv_out, CC + 1)
            sp.dma_start(A["out_conv_p"], last_p[:]).then_inc(saved, 16)
            sp.dma_start(A["out_conv_s"], last_s[:]).then_inc(saved, 16)
            sp.dma_start(A["a_in"], a_in[:]).then_inc(saved, 16)
            sp.wait_ge(saved, 48)

        @block.gpsimd
        def _(pool):
            w.split(nc, pool, CC)

        @block.tensor
        def _(pe):
            with pe.Fori(0, CC // 2) as i:
                for n in range(NB):
                    c, kind = n // 3, n % 3
                    if kind == 0:
                        pe.wait_ge(u_out, 6 * i + 3 * c + 3)
                    elif kind == 1:
                        pe.wait_ge(b_out, 6 * i + 3 * c + 3)
                    else:
                        pe.wait_ge(c_out, 6 * i + 3 * c + 3)
                    for last in w.project(nc, pe, 2 * i + c, kind, sets(n), G["h_hi"], G["h_lo"]):
                        last.then_inc((c_mm, h_mm, b_mm)[kind], 1)

        @block.scalar
        def _(act):
            act.sem_inc(b_out, 3)
            w.first_highs(nc, act)
            with act.Fori(0, CC // 2) as i:
                for n in (0, 2, 3, 5):
                    c = n // 3
                    mm, out, dst = (c_mm, c_out, cg) if n % 3 == 0 else (b_mm, b_out, bg)
                    if n % 3 == 0:
                        act.wait_ge(u_out, 6 * i + 3 * c + 3)
                    else:
                        act.wait_ge(conv_out, 2 * i + c + 1)
                    for b, (t0, m) in enumerate(TB):
                        act.wait_ge(mm, 6 * i + 3 * c + b + 1)
                        nc.scalar.activation(dst[:, t0:t0 + m], sets(n)[b][:, 0:m], ACT.Copy).then_inc(out, 1)

        @block.vector
        def _(dve):
            dve.sem_inc(u_out, 3)
            dve.sem_inc(conv_out, 1)
            w.first_lows(nc, dve)
            dve.wait_ge(small_in, 48)
            step = Steps(dve, own)
            step(nc.vector.memset(up[:, 0:CW - 1], 0.0))
            with dve.Fori(0, CC // 2) as i:
                step = Steps(dve, own, 2 * OPS * i + 1)
                for c in range(2):
                    ch = bass.ds(2 * i + c, 1)
                    step(nc.vector.tensor_copy(us[:, :, 0:CW - 1], past[:, ch].rearrange("p a s w -> p (a s) w")))
                    for b, (t0, m) in enumerate(TB):
                        dve.wait_ge(h_mm, 6 * i + 3 * c + b + 1)
                        dve.wait_ge(c_out, 6 * i + 3 * c + b + 1)
                        src = sets(3 * c + 1)[b]
                        n = min(m, SEQ - t0)
                        ins = nc.vector.tensor_tensor(up[:, CW - 1 + t0:CW - 1 + t0 + n], src[:, 0:n],
                                                      cg[:, t0:t0 + n], ALU.mult)
                        if n < m:
                            ins = nc.vector.tensor_tensor(us[:, :, CW - 1:], src[:, n:m].rearrange("p (s t) -> p s t", s=NSEQ),
                                                          cg[:, SEQ:T].rearrange("p (s t) -> p s t", s=NSEQ), ALU.mult)
                        ins.then_inc(u_out, 1)
                    dve.wait_ge(u_out, 6 * i + 3 * c + 6)
                    ys = y[:, SEQ:T].rearrange("p (s t) -> p s t", s=NSEQ)
                    tap = lambda n: taps[:, n, ch]
                    step(nc.vector.tensor_copy(last_p[:, ch].rearrange("p a w -> p (a w)"), up[:, SEQ:]))
                    step(nc.vector.tensor_copy(last_s[:, ch].rearrange("p a s w -> p (a s) w"), us[:, :, LSEQ:]))
                    for full, out, n in ((up, y[:, 0:SEQ], SEQ), (us, ys, LSEQ)):
                        at = lambda q: full[:, q:q + n] if full is up else full[:, :, q:q + n]
                        step(nc.vector.tensor_scalar(out, at(CW - 1), tap(CW - 1), cbias[:, ch], ALU.mult, ALU.add))
                        for q in range(CW - 1):
                            step(nc.vector.scalar_tensor_tensor(out=out, in0=at(q), scalar=tap(q), in1=out,
                                                                op0=ALU.mult, op1=ALU.add))
                    dve.wait_ge(b_out, 6 * i + 3 * c + 6)
                    nc.vector.tensor_tensor(a_in[:, ch].rearrange("p a t -> p (a t)"), y[:, :], bg[:, :],
                                            ALU.mult).then_inc(conv_out, 1)
                    dve.wait_ge(conv_out, 2 * i + c + 2)
                    assert step.n == OPS * (c + 1)


def gate_phase(nc, A, G):
    with Scope(nc, "side") as sc:
        PS = G["PS"]
        sig = sc.sb("sig", [P, 2, 2, T])
        mm, out, free = (sc.sem(n) for n in "mm out free".split())
        saved = [sc.sem(f"saved{b}") for b in range(2)]
        w = Weights(sc, 2, lambda b: (mm, 3 * b + 3, 6), [lambda i, b=b: A["w_gate_ab"][i, b] for b in range(2)])
        block = sc.block()
        sets = lambda n: [PS[:, 3 * n + b] for b in range(3)]

        @block.sync
        def _(sp):
            w.bring(sp, KD)

        @block.gpsimd
        def _(pool):
            w.split(nc, pool, KD)

        @block.tensor
        def _(pe):
            with pe.Fori(0, KD) as i:
                for n in range(2):
                    pe.wait_ge(out, 6 * i + 3 * n + 3)
                    for last in w.project(nc, pe, i, n, sets(n), G["h_hi"], G["h_lo"]):
                        last.then_inc(mm, 1)

        @block.scalar
        def _(act):
            act.sem_inc(out, 6)
            w.first_highs(nc, act)
            with act.Fori(0, KD // 2) as i:
                for par in range(2):
                    for n in range(2):
                        for b, (t0, m) in enumerate(TB):
                            act.wait_ge(mm, 12 * i + 6 * par + 3 * n + b + 1)
                            if n == 0 and b == 0:
                                act.wait_ge(free, 2 * i + par + 1)
                            nc.scalar.activation(sig[:, par, n, t0:t0 + m], sets(n)[b][:, 0:m], ACT.Sigmoid).then_inc(out, 1)
                    act.wait_ge(out, 12 * i + 6 * par + 12)
                    act.dma_start(A["sig"][2 * i + par], sig[:, par]).then_inc(saved[par], 16)

        @block.vector
        def _(dve):
            dve.sem_inc(free, 2)
            w.first_lows(nc, dve)
            with dve.Fori(0, KD // 2) as i:
                for par in range(2):
                    dve.wait_ge(saved[par], 16 * i + 16)
                    dve.sem_inc(free, 1)


def merge_phase(nc, A, G):
    with Scope(nc, "merge") as sc:
        PS, merged = G["PS"], G["merged"]
        raw = sc.sb("raw", [P, 4, T])
        a_hi, a_lo = sc.sb("a_hi", [P, CC, T], F32R), sc.sb("a_lo", [P, CC, T], F32R)
        b_hi, b_lo = G["h_hi"], G["h_lo"]
        sig = sc.sb("sig", [P, 2, T])
        parts = sc.sb("parts", [P, 2, T])
        mm, part, done = (sc.sem(n) for n in "mm part done".split())
        sig_in = sc.sem("sig_in")
        w = Weights(sc, 2, lambda b: (mm, 3 * b + 3, 6), [lambda i: A["w_proj_a"][i], lambda i: A["w_proj_b"][i]])
        fetch, highs, lows, low = split_inputs(
            nc, sc, "x", Joined(a_hi, b_hi, CC), Joined(a_lo, b_lo, CC), raw,
            lambda k: A["a_in"][:, k, :] if k < CC else A["ob"][(k - CC) // 2, :, (k - CC) % 2, :], CC + KD)
        block = sc.block()
        sets = lambda n: [PS[:, 3 * n + b] for b in range(3)]

        @block.sync
        def _(sp):
            w.bring(sp, KD, between=fetch)

        @block.gpsimd
        def _(pool):
            w.split(nc, pool, KD)

        @block.tensor
        def _(pe):
            with pe.Fori(0, KD) as i:
                for n, (x_hi, x_lo, nk) in enumerate(((a_hi, a_lo, CC), (b_hi, b_lo, KD))):
                    pe.wait_ge(low, (CC, CC + KD)[n])
                    pe.wait_ge(part, 6 * i + 3 * n + 3)
                    for last in w.project(nc, pe, i, n, sets(n), x_hi, x_lo, nk):
                        last.then_inc(mm, 1)

        @block.scalar
        def _(act):
            w.first_highs(nc, act)
            highs(act)
            with act.Fori(0, KD) as i:
                act.wait_ge(part, 6 * i + 6)
                act.dma_start(sig[:], A["sig"][i]).then_inc(sig_in, 16)

        @block.vector
        def _(dve):
            dve.sem_inc(part, 6)
            w.first_lows(nc, dve)
            lows(dve)
            with dve.Fori(0, KD) as i:
                dve.wait_ge(sig_in, 16 * i + 16)
                for n in range(2):
                    for b, (t0, m) in enumerate(TB):
                        dve.wait_ge(mm, 6 * i + 3 * n + b + 1)
                        nc.vector.tensor_tensor(parts[:, n, t0:t0 + m], sets(n)[b][:, 0:m], sig[:, n, t0:t0 + m],
                                                ALU.mult).then_inc(part, 1)
                dve.wait_ge(part, 6 * i + 12)
                nc.vector.tensor_tensor(merged[:, bass.ds(i, 1)].rearrange("p a t -> p (a t)"), parts[:, 0, :], parts[:, 1, :],
                                        ALU.add).then_inc(done, 1)
                dve.wait_ge(done, i + 1)


class Joined:

    def __init__(self, first, second, n):
        self.first, self.second, self.n = first, second, n

    def __getitem__(self, at):
        p, k, t = at
        return self.first[p, k, t] if k < self.n else self.second[p, k - self.n, t]


def out_phase(nc, A, G):
    with Scope(nc, "out") as sc:
        NB = 2
        PS, merged = G["PS"], G["merged"]
        x = merged
        m = sc.sb("m", [P, KD, T])
        m_hi, m_lo = G["h_hi"], G["h_lo"]
        sq = sc.sb("sq", [P, 2, T])
        root, tmp = sc.sb("root", [P, T]), sc.sb("tmp", [P, T])
        x_in, mm, m_out, own, saved, high, low = (sc.sem(n) for n in "x_in mm m_out own saved high low".split())
        x2_done, h2_done = sc.sem("x2_done"), sc.sem("h2_done")
        n1, n2 = norm_sems(sc, "post_"), norm_sems(sc, "pre_")
        w = Weights(sc, NB, lambda b: (mm, 3 * b + 3, 3 * NB), [lambda i, b=b: A["w_out"][2 * i + b] for b in range(NB)])
        block = sc.block()
        sets = lambda n: [PS[:, 3 * (n % 2) + b] for b in range(3)]

        @block.sync
        def _(sp):
            w.bring(sp, KD // NB)
            for k in range(KD):
                sp.wait_ge(low, k + 1)
                sp.dma_start(x[:, k, :], A["x"][k]).then_inc(x_in, 16)
            for k in range(KD):
                sp.wait_ge(x2_done, k + 1)
                sp.dma_start(A["x2"][:, k, :], x[:, k, :]).then_inc(saved, 16)
            sp.wait_ge(saved, 16 * KD)

        @block.gpsimd
        def _(pool):
            w.split(nc, pool, KD // NB)
            for k in range(KD):
                pool.wait_ge(high, KD + k + 1)
                nc.gpsimd.tensor_tensor(m_lo[:, k, :], m[:, k, :], m_hi[:, k, :].bitcast(F32), ALU.subtract)

        @block.tensor
        def _(pe):
            pe.wait_ge(low, KD)
            with pe.Fori(0, KD // NB) as i:
                for n in range(NB):
                    pe.wait_ge(m_out, 6 * i + 3 * n + 3)
                    for last in w.project(nc, pe, i, n, sets(n), m_hi, m_lo):
                        last.then_inc(mm, 1)
            pe.wait_ge(m_out, 6 + 3 * KD)
            norm_sums(nc, pe, n1, G["ones"], sq, sets(0))
            norm_sums(nc, pe, n2, G["ones"], sq, sets(1))

        @block.scalar
        def _(act):
            act.sem_inc(m_out, 6)
            for k in range(KD):
                if k == KD // 2:
                    w.first_highs(nc, act)
                nc.scalar.activation(m_hi[:, k, :], merged[:, k, :], ACT.Copy).then_inc(high, 1)
            with act.Fori(0, KD // NB) as i:
                for n in range(NB):
                    for b, (t0, q) in enumerate(TB):
                        act.wait_ge(mm, 6 * i + 3 * n + b + 1)
                        nc.scalar.activation(m[:, bass.ds(2 * i + n, 1), t0:t0 + q].rearrange("p a t -> p (a t)"),
                                             sets(n)[b][:, 0:q], ACT.Copy).then_inc(m_out, 1)
            act.wait_ge(m_out, 6 + 3 * KD)
            norm_squares(nc, act, n1, m, sq)
            act.wait_ge(n1["summed"], KD)
            norm_roots(nc, act, n1, sets(0), root, G["eps"])
            norm_squares(nc, act, n2, x, sq, x2_done)
            act.wait_ge(n2["summed"], KD)
            norm_roots(nc, act, n2, sets(1), root, G["eps"])
            for k in range(KD):
                act.wait_ge(h2_done, k + 1)
                nc.scalar.activation(m_hi[:, k, :], m[:, k, :], ACT.Copy).then_inc(high, 1)

        @block.vector
        def _(dve):
            step = Steps(dve, own)
            for k in range(KD):
                if k == KD // 2:
                    w.first_lows(nc, dve)
                dve.wait_ge(high, k + 1)
                nc.vector.tensor_tensor(m_lo[:, k, :], merged[:, k, :], m_hi[:, k, :].bitcast(F32),
                                        ALU.subtract).then_inc(low, 1)
            dve.wait_ge(x_in, 16 * KD)
            dve.wait_ge(n1["rooted"], 1)
            residual(nc, step, x, m, root, tmp, G["gate"][:, 0], x2_done)
            dve.wait_ge(n2["rooted"], 1)
            modulate(nc, step, m, x, root, tmp, G["gain"][:, 1], G["shift"][:, 1], h2_done)


def stream_weights(sp, steps, w, w_in, used, sources):
    for b, src in enumerate(sources):
        sp.dma_start(w[:, b, 0:src(0).shape[1]], src(0)).then_inc(w_in[b], 16)
    with sp.Fori(1, steps) as i:
        for b, src in enumerate(sources):
            mm, first, more = used(b)
            sp.wait_ge(mm, more * (i - 1) + first)
            sp.dma_start(w[:, b, 0:src(0).shape[1]], src(i)).then_inc(w_in[b], 16)


def keys_phase(nc, A, G):
    with Scope(nc, "keys") as sc:
        NB = 2
        PS = G["PS"]
        h_hi, h_lo = G["h_hi"], G["h_lo"]
        w = sc.sb("w", [P, NB, KD, P])
        w_hi, w_lo = sc.sb("w_hi", [P, NB, KD, P], F32R), sc.sb("w_lo", [P, NB, KD, P], F32R)
        sub = sc.sb("sub", [P, 2 * PH, NK])
        qT = sc.sb("qT", [P, NB, T])
        s1 = sc.sb("s1", [P, NB, NT, NK])
        s2 = sc.sb("s2", [P, NT, NK])
        best, place = sc.sb("best", [P, NT, TOPK]), sc.sb("place", [P, NT, TOPK], U32)
        w_in = [sc.sem(f"w_in{b}") for b in range(NB)]
        sub_in, q_mm, q_out, s_mm, s_out, own, listed, passed, high, low, q_free, passed_pool = (sc.sem(n) for n in (
            "sub_in q_mm q_out s_mm s_out own listed passed high low q_free passed_pool").split())
        block = sc.block()
        sets = lambda n: [PS[:, 3 * (n % 2) + b] for b in range(3)]
        SB = ((6, 0), (1, 3))
        pairbank = lambda n: (PS[:, 6:8, :], PS[:, 1:3, :])[n].rearrange("p b (t d) -> p (b t) d", d=NK)
        lone = lambda n: PS[0:TAIL, (0, 3)[n], 0:NK]
        OPS = 5

        @block.sync
        def _(sp):
            stream_weights(sp, PH, w, w_in, lambda b: (low, b + 1, NB), [lambda i, b=b: A["w_query"][2 * i + b] for b in range(NB)])

        @block.tensor
        def _(pe):
            pe.wait_ge(sub_in, 16)
            with pe.Fori(0, PH) as i:
                for n in range(NB):
                    pe.wait_ge(low, NB * i + n + 1)
                    pe.wait_ge(s_out, 4 * i + 4)
                    for last in project3(nc, sets(n), w_hi[:, n], w_lo[:, n], h_hi, h_lo, KD):
                        last.then_inc(q_mm, 1)
                for n in range(NB):
                    pe.wait_ge(q_out, 6 * i + (3, 6)[n])
                    for t in range(NT):
                        out = pairbank(n)[:, t, :] if t < NT - 1 else lone(n)
                        last = nc.tensor.matmul(out, qT[:, n, t * P:t * P + rows(t)],
                                                sub[:, bass.ds(2 * i + n, 1), :].rearrange("p a k -> p (a k)"),
                                                start=True, stop=True)
                    last.then_inc(s_mm, 1)

        @block.gpsimd
        def _(pool):
            pool.wait_ge(low, NB)
            with pool.Fori(1, PH) as i:
                for n in range(NB):
                    pool.wait_ge(w_in[n], 16 * i + 16)
                    pool.wait_ge(q_free, NB * i + n + 1)
                    pool.sem_inc(passed_pool, 1)
                    split(nc, pool, w_hi[:, n], w_lo[:, n], w[:, n], high, low, NB * i + n + 1)

        @block.scalar
        def _(act):
            act.dma_start(sub[:], A["subkeys"]).then_inc(sub_in, 16)
            act.sem_inc(s_out, 4)
            act.sem_inc(q_free, 2)
            for n in range(NB):
                act.wait_ge(w_in[n], 16)
                nc.scalar.activation(w_hi[:, n], w[:, n], ACT.Copy).then_inc(high, 1)
            with act.Fori(0, PH) as i:
                for n in range(NB):
                    for b, (t0, m) in enumerate(TB):
                        act.wait_ge(q_mm, 6 * i + 3 * n + b + 1)
                        nc.scalar.activation(qT[:, n, t0:t0 + m], sets(n)[b][:, 0:m], ACT.Copy).then_inc(q_out, 1)
                    act.sem_inc(q_free, 1)
                for n in range(NB):
                    act.wait_ge(s_mm, 2 * i + n + 1)
                    act.wait_ge(listed, 2 * i + n + 1)
                    nc.scalar.activation(s1[:, n, 0:NT - 1, :], pairbank(n), ACT.Copy).then_inc(s_out, 1)
                    nc.scalar.activation(s1[0:TAIL, n, NT - 1, :], lone(n), ACT.Copy).then_inc(s_out, 1)

        @block.vector
        def _(dve):
            dve.sem_inc(listed, 2)
            for n in range(NB):
                dve.wait_ge(high, n + 1)
                nc.vector.tensor_tensor(w_lo[:, n], w[:, n], w_hi[:, n].bitcast(F32), ALU.subtract).then_inc(low, 1)
            step = Steps(dve, own)
            step(nc.vector.memset(G["best"][:], 0.0))
            step(nc.vector.memset(G["place"][:], 0.0))
            with dve.Fori(0, PH) as i:
                for n in range(NB):
                    step = Steps(dve, own, OPS * (NB * i + n) + 2)
                    dve.wait_ge(s_out, 4 * i + 2 * n + 6)
                    dve.sem_inc(passed, 1)
                    for t in range(NT):
                        last = nc.vector.max(best[0:rows(t), t, 0:8], s1[0:rows(t), n, t, :])
                    step(last, passed)
                    for t in range(NT):
                        nc.vector.max_index(place[0:rows(t), t, 0:8], best[0:rows(t), t, 0:8], s1[0:rows(t), n, t, :])
                        last = nc.vector.match_replace(s2[0:rows(t), t, :], best[0:rows(t), t, 0:8],
                                                       s1[0:rows(t), n, t, :], LOWEST)
                    step(last, passed)
                    for t in range(NT):
                        last = nc.vector.max(best[0:rows(t), t, 8:16], s2[0:rows(t), t, :])
                    step(last, passed)
                    for t in range(NT):
                        last = nc.vector.max_index(place[0:rows(t), t, 8:16], best[0:rows(t), t, 8:16], s2[0:rows(t), t, :])
                    step(last)
                    side = bass.ds(2 * i + n, 1)
                    for dst, src in ((G["best"], best), (G["place"], place)):
                        last = nc.vector.tensor_copy(dst[:, 0:NT - 1, side, :].rearrange("p t a k -> p t (a k)"), src[:, 0:NT - 1, :])
                        last = nc.vector.tensor_copy(dst[0:TAIL, NT - 1, side, :].rearrange("p a k -> p (a k)"), src[0:TAIL, NT - 1, :])
                    step(last)
                    dve.sem_inc(listed, 1)


class Hidden:

    def __init__(self, sc, A, G, slots, banks, first):
        self.A, self.G, self.slots, self.banks, self.first, self.PS = A, G, slots, banks, first, G["PS"]
        self.u = sc.sb("u", [P, slots, KD, P])
        self.hi, self.lo = sc.sb("u_hi", [P, slots, KD, P], F32R), sc.sb("u_lo", [P, slots, KD, P], F32R)
        self.ge = sc.sb("ge", [P, slots, T])
        names = "u_in u_high u_low u_mm ge_out u_passed ge_free hid_saved".split()
        (_, self.high, self.low, self.mm, self.out, self.passed, self.free, _) = (sc.sem(n) for n in names)
        self.u_in = [sc.sem(f"u_in_{b}") for b in range(slots)]
        self.saved = [sc.sem(f"saved_{b}") for b in range(slots)]

    def bring(self, sp, n, slot, turn, reuse=True):
        if reuse:
            sp.wait_ge(self.low, n - self.slots + 1)
        sp.dma_start(self.u[:, slot], self.A["u"][self.first + n]).then_inc(self.u_in[slot], 16)

    def split(self, nc, pool, n, slot, turn):
        pool.wait_ge(self.u_in[slot], 16 * turn + 16)
        pool.wait_ge(self.out, 3 * n + 3)
        pool.sem_inc(self.passed, 1)
        split(nc, pool, self.hi[:, slot], self.lo[:, slot], self.u[:, slot], self.high, self.low, n + 1)

    def multiply(self, nc, pe, n, slot, b):
        t0, m = TB[b]
        if b == 0:
            pe.wait_ge(self.low, n + 1)
        pe.wait_ge(self.out, 3 * n + b + 3 * self.slots - len(self.banks) + 1)
        out, h_hi, h_lo = self.PS[:, self.banks[b], 0:m], self.G["h_hi"], self.G["h_lo"]
        for k in range(KD):
            hi, lo = h_hi[:, k, t0:t0 + m], h_lo[:, k, t0:t0 + m]
            nc.tensor.matmul(out, self.hi[:, slot, k, :], hi, start=(k == 0), stop=False)
            nc.tensor.matmul(out, self.hi[:, slot, k, :], lo, start=False, stop=False)
            last = nc.tensor.matmul(out, self.lo[:, slot, k, :], hi, start=False, stop=(k == KD - 1))
        last.then_inc(self.mm, 1)

    def gelu(self, nc, act, n, slot, b):
        t0, m = TB[b]
        if b == 0:
            act.wait_ge(self.free, n + 1)
        act.wait_ge(self.mm, 3 * n + b + 1)
        nc.scalar.activation(self.ge[:, slot, t0:t0 + m], self.PS[:, self.banks[b], 0:m],
                             ACT.Gelu_apprx_tanh).then_inc(self.out, 1)

    def credits(self, act, sp):
        if act is not None:
            act.sem_inc(self.out, 3 * self.slots)
        if sp is not None:
            sp.sem_inc(self.free, self.slots)

    def put(self, sp, n, slot):
        sp.wait_ge(self.out, 3 * n + 3 + 3 * self.slots)
        sp.dma_start(self.A["hid"][self.first + n], self.ge[:, slot]).then_inc(self.saved[slot], 16)

    def landed(self, sp, slot, turn):
        sp.wait_ge(self.saved[slot], 16 * turn + 16)
        sp.sem_inc(self.free, 1)


def pick_phase(nc, A, G):
    with Scope(nc, "pick") as sc:
        PS = G["PS"]
        sums = sc.sb("sums", [P, PH, TOPK * TOPK])
        sums2 = sc.sb("sums2", [P, PH, TOPK * TOPK])
        top, at = sc.sb("top", [P, PH, TOPK]), sc.sb("at", [P, PH, TOPK], U32)
        half = [sc.sb(f"half{s}", [P, HK], U32) for s in range(2)]
        halff = [sc.sb(f"halff{s}", [P, HK]) for s in range(2)]
        eq = [sc.sb(f"eq{s}", [P, HK, TOPK]) for s in range(2)]
        route = sc.sb("route", [P, 3, HK])
        diff, total = sc.sb("diff", [P, PH, TOPK]), sc.sb("total", [P, PH])
        own, t_mm, t_out, d_out, e_out, passed = (sc.sem(n) for n in "own t_mm t_out d_out e_out passed".split())
        NS = PICK_CHUNKS
        hid = Hidden(sc, A, G, NS, (1, 2, 3), 0)
        block = sc.block()
        OPS = 18

        def tiles(eng, body):
            with eng.Fori(0, NT - 1) as i:
                body(i, NS)
            body(NT - 1, NS - 1)

        @block.sync
        def _(sp):
            hid.credits(None, sp)
            for c in range(NS):
                hid.bring(sp, c, c, 0, reuse=False)

            def move(i, chunks):
                if chunks == NS:
                    for c in range(NS - 1):
                        hid.bring(sp, NS * (i + 1) + c, c, None)
                for c in range(chunks):
                    hid.put(sp, NS * i + c, c)
                if chunks == NS:
                    hid.bring(sp, NS * (i + 1) + NS - 1, NS - 1, None)
                for c in range(chunks):
                    hid.landed(sp, c, i)
            tiles(sp, move)

        @block.gpsimd
        def _(pool):
            def parts(i, chunks):
                for c in range(chunks):
                    hid.split(nc, pool, NS * i + c, c, i)
            tiles(pool, parts)

        @block.tensor
        def _(pe):
            def work(i, chunks):
                for c in range(chunks):
                    for b in range(len(TB)):
                        hid.multiply(nc, pe, NS * i + c, c, b)
                pe.wait_ge(own, OPS * i + OPS)
                pe.wait_ge(t_out, i + 1)
                for n in range(3):
                    last = nc.tensor.transpose(PS[:, 0, n * P:(n + 1) * P], route[:, n, :], G["ident"][:, :])
                last.then_inc(t_mm, 1)
            tiles(pe, work)

        @block.scalar
        def _(act):
            act.sem_inc(t_out, 1)
            hid.credits(act, None)

            def work(i, chunks):
                for c in range(chunks):
                    for b in range(len(TB)):
                        hid.gelu(nc, act, NS * i + c, c, b)
                    if c == 1:
                        act.wait_ge(d_out, i + 1)
                        nc.scalar.activation(diff[:], diff[:], ACT.Exp).then_inc(e_out, 1)
                act.wait_ge(t_mm, i + 1)
                nc.scalar.activation(G["routeT"][:, :, bass.ds(i * P, P)],
                                     PS[:, 0, 0:3 * P].rearrange("p (n t) -> p n t", n=3), ACT.Copy).then_inc(t_out, 1)
            tiles(act, work)

        @block.vector
        def _(dve):
            with dve.Fori(0, NT) as i:
                step = Steps(dve, own, OPS * i)
                sv = G["best"][:, bass.ds(i, 1)].rearrange("p a (h s) k -> p (a h) s k", s=2)
                si = G["place"][:, bass.ds(i, 1)].rearrange("p a (h s) k -> p (a h) s k", s=2)
                step(nc.vector.tensor_tensor(sums[:].rearrange("p h (a b) -> p h a b", a=TOPK),
                                             sv[:, :, 0, :, None].broadcast_to([P, PH, TOPK, TOPK]),
                                             sv[:, :, 1, None, :].broadcast_to([P, PH, TOPK, TOPK]), ALU.add), passed)
                for hh in range(PH):
                    last = nc.vector.max(top[:, hh, 0:8], sums[:, hh, :])
                step(last, passed)
                for hh in range(PH):
                    nc.vector.max_index(at[:, hh, 0:8], top[:, hh, 0:8], sums[:, hh, :])
                    last = nc.vector.match_replace(sums2[:, hh, :], top[:, hh, 0:8], sums[:, hh, :], LOWEST)
                step(last, passed)
                for hh in range(PH):
                    last = nc.vector.max(top[:, hh, 8:16], sums2[:, hh, :])
                step(last, passed)
                for hh in range(PH):
                    last = nc.vector.max_index(at[:, hh, 8:16], top[:, hh, 8:16], sums2[:, hh, :])
                step(last)
                nc.vector.tensor_tensor(diff[:], top[:], top[:, :, 0:1].broadcast_to([P, PH, TOPK]),
                                        ALU.subtract).then_inc(d_out, 1)
                atf = at[:].rearrange("p h k -> p (h k)")
                step(nc.vector.tensor_scalar(half[0][:, :], atf, 4, None, ALU.logical_shift_right))
                step(nc.vector.tensor_scalar(half[1][:, :], atf, TOPK - 1, None, ALU.bitwise_and))
                for n in range(2):
                    step(nc.vector.tensor_copy(halff[n][:, :], half[n][:, :]))
                for n in range(2):
                    step(nc.vector.tensor_tensor(eq[n][:], halff[n][:, :, None].broadcast_to([P, HK, TOPK]),
                                                 G["iota"][:, None, 0:TOPK].broadcast_to([P, HK, TOPK]), ALU.is_equal))
                    e4 = eq[n][:].rearrange("p (h k) a -> p h k a", h=PH)
                    step(nc.vector.tensor_tensor(e4, e4, si[:, :, n, None, :].broadcast_to([P, PH, TOPK, TOPK]), ALU.mult))
                dve.wait_ge(t_out, i + 1)
                for n in range(2):
                    step(nc.vector.tensor_reduce(route[:, n, :], eq[n][:], AX.X, ALU.add))
                dve.wait_ge(e_out, i + 1)
                step(nc.vector.tensor_reduce(total[:, :], diff[:], AX.X, ALU.add))
                step(nc.vector.reciprocal(total[:, :], total[:, :]))
                step(nc.vector.tensor_tensor(route[:, 2, :].rearrange("p (h k) -> p h k", h=PH), diff[:],
                                             total[:, :, None].broadcast_to([P, PH, TOPK]), ALU.mult))
                assert step.n == OPS


def gates_phase(nc, A, G):
    with Scope(nc, "gates") as sc:
        PS, routeT = G["PS"], G["routeT"]
        NG, TG = 4, 4
        hot_i, hot_j = sc.sb("hot_i", [P, NG, TG, NK], BF16), sc.sb("hot_j", [P, NG, TG, 3, NK], BF16)
        iota = sc.sb("iota", [P, NK], BF16)
        places = sc.sb("places", [P, 2, GB])
        gate = sc.sb("gate", [P, 3, GB])
        rest = sc.sb("rest", [P, 2, GB])
        short = sc.sb("short", [P, 2, GB], BF16)
        gm = sc.sb("gm", [P, 2, NK, GB])
        hot, mm, out, saved, gm_free, own, iota_set = (sc.sem(n) for n in (
            "hot mm out saved gm_free own iota_set").split())
        NB = 4
        hid = Hidden(sc, A, G, 2, (4, 5, 6), PICK_CHUNKS * NT - 1)
        block = sc.block()
        PER = GB // TG
        units = [(c, b) for c in range(GATE_CHUNKS) for b in range(len(TB))]
        after = [units[len(units) * g // PER:len(units) * (g + 1) // PER] for g in range(PER)]
        early = [units[g:g + 1] for g in range(PER - 1)] + [units[PER - 1:]]
        assert PICK_CHUNKS * NT - 1 + GATE_CHUNKS * NGB == NK

        def blocks(eng, body):
            with eng.Fori(0, NGB // 2) as i:
                for b in range(2):
                    body(2 * i + b, b)
            assert NGB % 2
            body(NGB - 1, 0, True)

        @block.sync
        def _(sp):
            sp.sem_inc(gm_free, 2)
            hid.credits(None, sp)
            for c in range(2):
                hid.bring(sp, c, c, None, reuse=False)

            def move(blk, b, last=False):
                def matrices():
                    sp.wait_ge(out, PER * blk + PER + NB)
                    sp.dma_start(A["gm"][blk], gm[:, b]).then_inc(saved, 16)
                for c in range(GATE_CHUNKS):
                    n = GATE_CHUNKS * blk + c
                    if not (last and c >= GATE_CHUNKS - 2):
                        hid.bring(sp, n + 2, c % 2, None)
                    if last and c == GATE_CHUNKS - 1:
                        matrices()
                    hid.put(sp, n, c % 2)
                    hid.landed(sp, c % 2, GATE_CHUNKS // 2 * blk + c // 2)
                if not last:
                    matrices()
                sp.wait_ge(saved, 16 * blk + 16)
                sp.sem_inc(gm_free, 1)
            blocks(sp, move)

        @block.gpsimd
        def _(pool):
            def parts(blk, b, last=False):
                for c in range(GATE_CHUNKS):
                    hid.split(nc, pool, GATE_CHUNKS * blk + c, c % 2, GATE_CHUNKS // 2 * blk + c // 2)
            blocks(pool, parts)

        @block.vector
        def _(dve):
            nc.vector.tensor_copy(iota[:, :], G["iota"][:, :]).then_inc(iota_set, 1)
            dve.wait_ge(iota_set, 1)
            dve.sem_inc(hot, 1)

            def build(blk, b, last_block=False):
                dve.wait_ge(hot, PER * blk + 1)
                step = Steps(dve, own, 4 * blk)
                here = bass.ds(blk * GB, GB)
                nc.vector.tensor_copy(places[:], routeT[:, 0:2, here])
                nc.vector.tensor_copy(rest[:, 0], routeT[:, 2, here])
                step(nc.vector.tensor_copy(short[:, 0], routeT[:, 2, here]))
                nc.vector.tensor_copy(gate[:, 0], short[:, 0])
                step(nc.vector.tensor_tensor(rest[:, 1], rest[:, 0], short[:, 0], ALU.subtract))
                step(nc.vector.tensor_copy(short[:, 1], rest[:, 1]))
                nc.vector.tensor_copy(gate[:, 1], short[:, 1])
                step(nc.vector.tensor_tensor(gate[:, 2], rest[:, 1], short[:, 1], ALU.subtract))
                for g in range(PER):
                    dve.wait_ge(mm, PER * blk + g + 1)
                    for t in range(TG):
                        at = g * TG + t
                        nc.vector.tensor_scalar(hot_i[:, g % NG, t, :], iota[:, :], places[:, 0, at:at + 1],
                                                None, ALU.is_equal)
                        for n in range(3):
                            last = nc.vector.tensor_scalar(hot_j[:, g % NG, t, n, :], iota[:, :],
                                                           places[:, 1, at:at + 1], gate[:, n, at:at + 1],
                                                           ALU.is_equal, ALU.mult)
                    last.then_inc(hot, 1)
            blocks(dve, build)

        @block.tensor
        def _(pe):
            pe.sem_inc(mm, NG)
            def multiply(blk, b, last_block=False):
                for g in range(PER):
                    pe.wait_ge(hot, PER * blk + g + 2)
                    pe.wait_ge(out, PER * blk + g + 1)
                    for t in range(TG):
                        for n in range(3):
                            last = nc.tensor.matmul(PS[:, g % NB, t * NK:(t + 1) * NK], hot_i[:, g % NG, t, :],
                                                    hot_j[:, g % NG, t, n, :], start=(n == 0), stop=(n == 2))
                    last.then_inc(mm, 1)
                    for c, q in (early if last_block else after)[g]:
                        hid.multiply(nc, pe, GATE_CHUNKS * blk + c, c % 2, q)
            blocks(pe, multiply)

        @block.scalar
        def _(act):
            act.sem_inc(out, NB)
            hid.credits(act, None)

            def empty(blk, b, last_block=False):
                act.wait_ge(gm_free, blk + 1)
                for g in range(PER):
                    act.wait_ge(mm, PER * blk + g + 1 + NG)
                    nc.scalar.activation(gm[:, b, :, g * TG:(g + 1) * TG].rearrange("p j t -> p t j"),
                                         PS[:, g % NB, :].rearrange("p (t j) -> p t j", t=TG), ACT.Copy).then_inc(out, 1)
                    for c, q in (early if last_block else after)[g]:
                        hid.gelu(nc, act, GATE_CHUNKS * blk + c, c % 2, q)
            blocks(act, empty)


def experts_phase(nc, A, G):
    with Scope(nc, "exp") as sc:
        PS, acc = G["PS"], G["acc"]
        v, v_hi, v_lo = sc.sb("v", [P, CP, D]), sc.sb("v_hi", [P, CP, D], F32R), sc.sb("v_lo", [P, CP, D], F32R)
        hid, gm = sc.sb("hid", [P, CP, T]), sc.sb("gm", [P, CP, NGB, GB])
        pr = sc.sb("pr", [P, 3, 384])
        w_hi, w_lo = sc.sb("w_hi", [P, 2, CP, T], F32R), sc.sb("w_lo", [P, 2, CP, T], F32R)
        v_in, v_high, v_low, pr_out, w_high, w_low, v_mm, acc_out = (sc.sem(n) for n in (
            "v_in v_high v_low pr_out w_high w_low v_mm acc_out").split())
        c_in = [sc.sem(f"c_in{c}") for c in range(CP)]
        block = sc.block()
        NW, NV, NBANK = CP * len(TB), KD * len(TB), 8
        w_tiles = [(c, t0, n) for c in range(CP) for t0, n in TB]
        v_tiles = [(d, t0, n) for d in range(KD) for t0, n in TB]
        slices = [slice(d * P, (d + 1) * P) for d in range(KD)]

        def steps(eng, body):
            with eng.Fori(0, NSTEP // 2 - 1) as i:
                for par in range(2):
                    body(2 * i + par, par, False)
            body(NSTEP - 2, 0, False)
            body(NSTEP - 1, 1, True)

        @block.sync
        def _(sp):
            def chunk(i, c):
                sp.dma_start(hid[:, c], A["hid"][CP * i + c]).then_inc(c_in[c], 16)
                sp.dma_start(gm[:, c], A["gm"][:, :, bass.ds(CP * i + c, 1), :].rearrange("b p a t -> p b (a t)")
                             ).then_inc(c_in[c], 16)
            sp.dma_start(v[:], A["v"][0]).then_inc(v_in, 16)
            for c in range(CP):
                chunk(0, c)

            def ahead(i):
                for c in range(CP):
                    sp.wait_ge(pr_out, NW * (i - 1) + len(TB) * (c + 1) + 3)
                    chunk(i, c)
                sp.wait_ge(v_low, KD * (i - 1) + KD)
                sp.dma_start(v[:], A["v"][i]).then_inc(v_in, 16)
            with sp.Fori(1, NSTEP) as i:
                ahead(i)

        @block.tensor
        def _(pe):
            def step(i, par, last_step):
                pe.wait_ge(w_low, NW * i + NW + 3)
                for m, (d, t0, n) in enumerate(v_tiles):
                    if m % len(TB) == 0:
                        pe.wait_ge(v_low, KD * i + d + 1)
                    pe.wait_ge(acc_out, NV * i + m + 1)
                    out = PS[:, m % NBANK, 0:n]
                    for c in range(CP):
                        hi, lo = w_hi[:, par, c, t0:t0 + n], w_lo[:, par, c, t0:t0 + n]
                        nc.tensor.matmul(out, v_hi[:, c, slices[d]], hi, start=(c == 0), stop=False)
                        nc.tensor.matmul(out, v_hi[:, c, slices[d]], lo, start=False, stop=False)
                        last = nc.tensor.matmul(out, v_lo[:, c, slices[d]], hi, start=False, stop=(c == CP - 1))
                    last.then_inc(v_mm, 1)
            steps(pe, step)

        @block.scalar
        def _(act):
            def high_w(i, m, par):
                c, t0, n = w_tiles[m]
                act.wait_ge(pr_out, NW * i + m + 1 + 3)
                nc.scalar.activation(w_hi[:, par, c, t0:t0 + n], pr[:, m % 3, 0:n], ACT.Copy).then_inc(w_high, 1)

            def high_v(d):
                nc.scalar.activation(v_hi[:, :, slices[d]], v[:, :, slices[d]], ACT.Copy).then_inc(v_high, 1)
            act.wait_ge(v_in, 16)
            for d in range(KD):
                high_v(d)
            for m in range(NW):
                high_w(0, m, 0)

            def step(i, par, last_step):
                if last_step:
                    return
                for d in range(KD):
                    for m in range(NW * d // KD, NW * (d + 1) // KD):
                        high_w(i + 1, m, 1 - par)
                    act.wait_ge(v_in, 16 * i + 32)
                    act.wait_ge(v_mm, NV * i + len(TB) * (d + 1))
                    high_v(d)
            steps(act, step)

        @block.gpsimd
        def _(pool):
            def low_v(d):
                nc.gpsimd.tensor_tensor(v_lo[:, :, slices[d]], v[:, :, slices[d]], v_hi[:, :, slices[d]].bitcast(F32),
                                        ALU.subtract).then_inc(v_low, 1)
            nc.gpsimd.memset(acc[:], 0.0).then_inc(acc_out, NBANK)
            for d in range(KD):
                pool.wait_ge(v_high, d + 1)
                low_v(d)
            with pool.Fori(1, NSTEP) as i:
                for d in range(KD):
                    pool.wait_ge(v_high, KD * i + d + 1)
                    low_v(d)

        @block.vector
        def _(dve):
            dve.sem_inc(pr_out, 3)
            dve.sem_inc(w_low, 3)

            def product(i, m):
                c, t0, n = w_tiles[m]
                if m % len(TB) == 0:
                    dve.wait_ge(c_in[c], 32 * i + 32)
                dve.wait_ge(w_low, NW * i + m + 1)
                nc.vector.tensor_tensor(pr[:, m % 3, 0:n], hid[:, c, t0:t0 + n],
                                        gm[:, c].rearrange("p b t -> p (b t)")[:, t0:t0 + n], ALU.mult).then_inc(pr_out, 1)

            def low_w(i, m, par):
                c, t0, n = w_tiles[m]
                dve.wait_ge(w_high, NW * i + m + 1)
                nc.vector.tensor_tensor(w_lo[:, par, c, t0:t0 + n], pr[:, m % 3, 0:n],
                                        w_hi[:, par, c, t0:t0 + n].bitcast(F32), ALU.subtract).then_inc(w_low, 1)
            for m in range(NW):
                product(0, m)
                if m:
                    low_w(0, m - 1, 0)
            low_w(0, NW - 1, 0)

            def step(i, par, last_step):
                dve.wait_ge(acc_out, NV * i + NBANK)
                for m, (d, t0, n) in enumerate(v_tiles):
                    if m % 2 == 0 and not last_step:
                        product(i + 1, m // 2)
                        if m:
                            low_w(i + 1, m // 2 - 1, 1 - par)
                    dve.wait_ge(v_mm, NV * i + m + 1)
                    nc.vector.tensor_tensor(acc[:, d, t0:t0 + n], acc[:, d, t0:t0 + n], PS[:, m % NBANK, 0:n],
                                            ALU.add).then_inc(acc_out, 1)
                if not last_step:
                    low_w(i + 1, NW - 1, 1 - par)
            steps(dve, step)


def final_phase(nc, A, G):
    with Scope(nc, "fin") as sc:
        PS, acc = G["PS"], G["acc"]
        x = sc.sb("x", [P, KD, T])
        sq = sc.sb("sq", [P, 2, T])
        root, tmp = sc.sb("root", [P, T]), sc.sb("tmp", [P, T])
        x_in, own, done, saved = (sc.sem(n) for n in "x_in own done saved".split())
        ns = norm_sems(sc)
        block = sc.block()
        banks = [PS[:, b] for b in range(3)]

        @block.sync
        def _(sp):
            sp.dma_start(x[:], A["x2"]).then_inc(x_in, 16)
            for k in range(KD):
                sp.wait_ge(done, k + 1)
                sp.dma_start(A["out_y"][:, k, :], x[:, k, :]).then_inc(saved, 16)
            sp.wait_ge(saved, 16 * KD)

        @block.scalar
        def _(act):
            norm_squares(nc, act, ns, acc, sq)
            act.wait_ge(ns["summed"], KD)
            norm_roots(nc, act, ns, banks, root, G["eps"])

        @block.tensor
        def _(pe):
            norm_sums(nc, pe, ns, G["ones"], sq, banks)

        @block.vector
        def _(dve):
            step = Steps(dve, own)
            dve.wait_ge(x_in, 16)
            dve.wait_ge(ns["rooted"], 1)
            residual(nc, step, x, acc, root, tmp, G["gate"][:, 1], done)


def hybrid_decoder(nc, A):
    with Scope(nc, "all") as top:
        G = {"PS": top.ps("PS", [P, 8, 512])}
        for name, shape in (("ones", [P, P]), ("ident", [P, P]), ("iota", [P, NK]), ("eps", [P, 1]), ("one", [P, 1]),
                            ("gain", [P, 2, KD, NC]), ("shift", [P, 2, KD, NC]), ("gate", [P, 2, KD, NC])):
            G[name] = top.sb(name, shape)
        with Scope(nc, "stream") as route:
            G["h_hi"], G["h_lo"] = route.sb("h_hi", [P, KD, T], F32R), route.sb("h_lo", [P, KD, T], F32R)
            condition_phase(nc, A, G)
            heads_phase(nc, A, G)
            conv_phase(nc, A, G)
            gate_phase(nc, A, G)
            with Scope(nc, "join") as join:
                G["merged"] = join.sb("merged", [P, KD, T])
                merge_phase(nc, A, G)
                out_phase(nc, A, G)
            G["routeT"] = route.sb("routeT", [P, 3, NT * P])
            with Scope(nc, "lists") as lists:
                G["best"] = lists.sb("best", [P, NT, 2 * PH, TOPK])
                G["place"] = lists.sb("place", [P, NT, 2 * PH, TOPK])
                keys_phase(nc, A, G)
                pick_phase(nc, A, G)
            gates_phase(nc, A, G)
        G["acc"] = top.sb("acc", [P, KD, T])
        experts_phase(nc, A, G)
        final_phase(nc, A, G)


def chunked(a):
    a = np.asarray(a)
    a = a.reshape(a.shape[:-1] + (-1, P))
    return np.ascontiguousarray(np.moveaxis(a, -1, 0))


def blocks_of(w):
    k, n = w.shape
    return np.ascontiguousarray(w.reshape(k // P, P, n // P, P).transpose(2, 1, 0, 3))


def arrange(i):
    i = {k: np.asarray(v) for k, v in i.items()}
    sizes = (D // 2, D // 2, D // 2, H * DK, H * DK, H * DV, H * DV, D, D, RANK)
    cuts = np.cumsum((0,) + sizes)
    part = [i["w_in"][0][:, a:b] for a, b in zip(cuts[:-1], cuts[1:])]
    bg, cg, hin, q, k, v, r, ga, gb = (blocks_of(p) for p in part[:9])
    x = np.concatenate([i["x_prompt"].reshape(SEQ, D), i["x_sample"].reshape(NSEQ * LSEQ, D)]).T
    sums, pairs = chunk_masks()
    seq_rows = (np.arange(TAIL)[:, None] // LSEQ == np.arange(NSEQ)[None, :]).astype(np.float32)
    u = i["peer_u"][0].reshape(NK, NK, KD, P)
    a = {
        "x": x.reshape(KD, P, T),
        "cond": chunked(np.concatenate([i["c_prompt"], i["c_sample"]])).transpose(0, 2, 1),
        "ada_bias": chunked(i["b_ada"][0]),
        "gains": chunked(np.concatenate([i["norm_mix_pre"], i["norm_mix_post"], i["norm_ffn_pre"], i["norm_ffn_post"]])),
        "w_ada": i["w_ada"][0].reshape(KD, P, 12, 512).transpose(2, 1, 0, 3),
        "w_low": part[9].reshape(KD, P, RANK).transpose(1, 0, 2),
        "w_alpha": np.concatenate([i["w_alpha"][0], i["b_alpha"]]),
        "gla_norm": chunked(i["gla_norm_w"][0]),
        "seq_rows": seq_rows, "mask_sums": sums, "mask_pairs": pairs,
        "w_heads": np.stack([q, k, v[0::2], v[1::2], r[0::2], r[1::2]], 1),
        "state": i["state_gla"][0].transpose(1, 2, 0, 3),
        "conv_w": chunked(i["conv_w"][0]), "conv_b": chunked(i["conv_b"][0]),
        "conv_state": chunked(i["state_conv"][0]).transpose(0, 3, 1, 2),
        "w_conv": np.stack([cg, hin, bg], 1),
        "w_gate_ab": np.stack([ga, gb], 1),
        "w_proj_a": blocks_of(i["w_proj_a"][0]), "w_proj_b": blocks_of(i["w_proj_b"][0]),
        "w_out": blocks_of(i["w_out"][0]), "w_query": blocks_of(i["peer_wq"][0]),
        "subkeys": i["peer_subkeys"][0].reshape(2 * PH, NK, P).transpose(2, 0, 1),
        "u": u.transpose(1, 3, 2, 0),
        "v": i["peer_v"][0].reshape(NK, NSTEP, CP, D).transpose(1, 0, 2, 3),
    }
    return {n: np.ascontiguousarray(v) for n, v in a.items()}


_OUTS = {"out_y": (P, KD, T), "out_conv_p": (P, CC, CW - 1), "out_conv_s": (P, CC, NSEQ, CW - 1),
         "out_gla_p": (H, DK, DV), "out_gla_s": (H, DK, NSEQ, DV)}
_SCRATCH = {"ob": (H, P, 2, T), "a_in": (P, CC, T), "sig": (KD, P, 2, T), "x2": (P, KD, T), "gm": (NGB, P, NK, GB), "hid": (NK, P, T)}


def kernel(**inputs):
    import concourse.bacc as bacc
    from concourse.bass_utils import run_bass_kernel_spmd

    nc = bacc.Bacc("TRN2", target_bir_lowering=False, num_devices=1)
    arrays, A = {}, {}
    for name, a in arrange(inputs).items():
        arrays[f"in_{name}"] = a
        A[name] = nc.dram_tensor(f"in_{name}", a.shape, F32, kind="ExternalInput").ap()
    for name, shape in _OUTS.items():
        A[name] = nc.dram_tensor(name, shape, F32, kind="ExternalOutput").ap()
    for name, shape in _SCRATCH.items():
        A[name] = nc.dram_tensor(f"scratch_{name}", shape, F32, kind="Internal").ap()
    hybrid_decoder(nc, A)
    got = run_bass_kernel_spmd(nc, [arrays], core_ids=[0]).results[0]
    y = got["out_y"].transpose(2, 1, 0).reshape(T, D)
    conv_p = got["out_conv_p"].transpose(2, 1, 0).reshape(1, 1, CW - 1, D // 2)
    conv_s = got["out_conv_s"].transpose(2, 3, 1, 0).reshape(1, NSEQ, CW - 1, D // 2)
    gla_p = got["out_gla_p"].reshape(1, 1, H, DK, DV)
    gla_s = got["out_gla_s"].transpose(2, 0, 1, 3).reshape(1, NSEQ, H, DK, DV)
    return (y[:SEQ].reshape(1, SEQ, D), y[SEQ:].reshape(NSEQ, LSEQ, D), conv_p, gla_p, conv_s, gla_s)
```
